# Optimizing a Trainium2 kernel written in Bass

```python
import math
import jax, jax.numpy as jnp
from jax import lax
import numpy as np

D_MODEL = 1024
BATCH = 1
SEQ = 256
DEPTH = 2

N_MEM = 256
CONV_WIDTH = D_MODEL // 2
CONV_K = 31
HGRN_WIDTH = D_MODEL // 2
HGRN_HEAD_DIM = 128
HGRN_HEADS = HGRN_WIDTH // HGRN_HEAD_DIM
CHUNK = 64
XA_HEADS = 4
XA_HEAD_DIM = D_MODEL // XA_HEADS
D_FF = 128 * math.ceil(8 * D_MODEL / 3 / 128)
IN_SIZES = (CONV_WIDTH, CONV_WIDTH, HGRN_WIDTH, HGRN_WIDTH, HGRN_WIDTH, HGRN_WIDTH, D_MODEL, D_MODEL)
IN_COLS = sum(IN_SIZES)
IN_SPLITS = tuple(int(s) for s in np.cumsum(IN_SIZES)[:-1])
DEEPNORM_ALPHA = (2 * DEPTH) ** 0.25
DEEPNORM_BETA = (8 * DEPTH) ** -0.25
LN_EPS = 1e-5
RMS_EPS = 1e-6
KEY_MAX = 1.0 - 1e-6

kernel_name = 'hybrid_conformer_hgrn2_gated_deepnorm'

def layer_norm(x, g, b):
    xf = x.astype(jnp.float32)
    mu = jnp.mean(xf, axis=-1, keepdims=True)
    xc = xf - mu
    var = jnp.mean(xc * xc, axis=-1, keepdims=True)
    y = xc * lax.rsqrt(var + LN_EPS) * g.astype(jnp.float32) + b.astype(jnp.float32)
    return y.astype(x.dtype)

def swiglu(h, w_gu, w_down):
    gate, up = jnp.split(h @ w_gu, 2, axis=-1)
    return (jax.nn.silu(gate) * up) @ w_down

def conformer_conv(a, b_gate, conv_w, conv_b, ln_g, ln_b, w_proj):
    h = a * jax.nn.sigmoid(b_gate)
    h = lax.conv_general_dilated(
        h, conv_w[:, None, :], window_strides=(1,), padding=[(CONV_K - 1, 0)],
        dimension_numbers=('NWC', 'WIO', 'NWC'), feature_group_count=CONV_WIDTH) + conv_b
    h = jax.nn.silu(layer_norm(h, ln_g, ln_b))
    return h @ w_proj

def hgrn2_branch(q, f_logit, i_val, o_gate, lb, norm_g, w_proj):
    bsz, seq = q.shape[0], q.shape[1]
    n_chunks = seq // CHUNK
    z = f_logit.astype(jnp.float32)
    k = (1.0 - lb) * jax.nn.sigmoid(-z)
    log_f = jnp.log1p(-jnp.minimum(k, KEY_MAX))
    qf = jax.nn.silu(q.astype(jnp.float32)) * HGRN_HEAD_DIM ** -0.5
    vf = i_val.astype(jnp.float32)

    def to_chunks(t):
        t = t.reshape(bsz, n_chunks, CHUNK, HGRN_HEADS, HGRN_HEAD_DIM)
        return t.transpose(1, 0, 3, 2, 4)

    causal = jnp.tril(jnp.ones((CHUNK, CHUNK), dtype=bool))[:, :, None]

    def step(state, inp):
        qc, kc, vc, lfc = inp
        b = jnp.cumsum(lfc, axis=2)
        diff = b[:, :, :, None, :] - b[:, :, None, :, :]
        decay = jnp.where(causal, jnp.exp(jnp.where(causal, diff, 0.0)), 0.0)
        scores = jnp.einsum('bhtk,bhtsk,bhsk->bhts', qc, decay, kc)
        o = (jnp.einsum('bhts,bhsv->bhtv', scores, vc)
             + jnp.einsum('bhtk,bhkv->bhtv', qc * jnp.exp(b), state))
        b_last = b[:, :, -1, :]
        new_state = (jnp.exp(b_last)[..., None] * state
                     + jnp.einsum('bhsk,bhsv->bhkv', kc * jnp.exp(b_last[:, :, None, :] - b), vc))
        return new_state, o

    state0 = jnp.zeros((bsz, HGRN_HEADS, HGRN_HEAD_DIM, HGRN_HEAD_DIM), jnp.float32)
    _, o = lax.scan(step, state0, (to_chunks(qf), to_chunks(k), to_chunks(vf), to_chunks(log_f)))
    o = o.transpose(1, 0, 3, 2, 4).reshape(bsz, seq, HGRN_HEADS, HGRN_HEAD_DIM)
    o = o * lax.rsqrt(jnp.mean(o * o, axis=-1, keepdims=True) + RMS_EPS)
    o = o.reshape(bsz, seq, HGRN_WIDTH) * norm_g.astype(jnp.float32) * jax.nn.silu(o_gate.astype(jnp.float32))
    return o.astype(q.dtype) @ w_proj

def cross_attention(h, mem, wq, wkv, wo):
    bsz, seq = h.shape[0], h.shape[1]
    n_mem = mem.shape[1]
    q = (h @ wq).reshape(bsz, seq, XA_HEADS, XA_HEAD_DIM)
    k, v = jnp.split(mem @ wkv, 2, axis=-1)
    k = k.reshape(bsz, n_mem, XA_HEADS, XA_HEAD_DIM)
    v = v.reshape(bsz, n_mem, XA_HEADS, XA_HEAD_DIM)
    s = jnp.einsum('bshd,bmhd->bhsm', q, k).astype(jnp.float32) * XA_HEAD_DIM ** -0.5
    p = jax.nn.softmax(s, axis=-1).astype(h.dtype)
    o = jnp.einsum('bhsm,bmhd->bshd', p, v).reshape(bsz, seq, D_MODEL)
    return o @ wo

def setup_inputs(seed: int = 0) -> dict:
    key = jax.random.key(seed)
    ks = jax.random.split(key, 24)
    f32 = jnp.float32

    def w(k, shape, fan_in, scale=1.0):
        return jax.random.normal(k, shape, f32) * (fan_in ** -0.5) * scale

    wk = w(ks[16], (DEPTH, D_MODEL, D_MODEL), D_MODEL)
    wv = w(ks[17], (DEPTH, D_MODEL, D_MODEL), D_MODEL, DEEPNORM_BETA)
    return {
        'x': jax.random.normal(ks[0], (BATCH, SEQ, D_MODEL), f32),
        'mem': jax.random.normal(ks[1], (BATCH, N_MEM, D_MODEL), f32),
        'ln_g': 1.0 + 0.02 * jax.random.normal(ks[2], (DEPTH, 4, D_MODEL), f32),
        'ln_b': 0.02 * jax.random.normal(ks[3], (DEPTH, 4, D_MODEL), f32),
        'ffn1_w_gu': w(ks[4], (DEPTH, D_MODEL, 2 * D_FF), D_MODEL, DEEPNORM_BETA),
        'ffn1_w_down': w(ks[5], (DEPTH, D_FF, D_MODEL), D_FF, DEEPNORM_BETA),
        'w_in': w(ks[6], (DEPTH, D_MODEL, IN_COLS), D_MODEL),
        'conv_w': w(ks[7], (DEPTH, CONV_K, CONV_WIDTH), CONV_K),
        'conv_b': 0.01 * jax.random.normal(ks[8], (DEPTH, CONV_WIDTH), f32),
        'conv_ln_g': 1.0 + 0.02 * jax.random.normal(ks[9], (DEPTH, CONV_WIDTH), f32),
        'conv_ln_b': 0.02 * jax.random.normal(ks[10], (DEPTH, CONV_WIDTH), f32),
        'w_conv_proj': w(ks[11], (DEPTH, CONV_WIDTH, D_MODEL), CONV_WIDTH, DEEPNORM_BETA),
        'hgrn_lb': 1.0 + 0.1 * jax.random.normal(ks[12], (DEPTH, HGRN_WIDTH), f32),
        'hgrn_norm_g': 1.0 + 0.02 * jax.random.normal(ks[13], (DEPTH, HGRN_WIDTH), f32),
        'w_hgrn_proj': w(ks[14], (DEPTH, HGRN_WIDTH, D_MODEL), HGRN_WIDTH, DEEPNORM_BETA),
        'w_mix_out': w(ks[15], (DEPTH, D_MODEL, D_MODEL), D_MODEL, DEEPNORM_BETA),
        'xa_wq': w(ks[18], (DEPTH, D_MODEL, D_MODEL), D_MODEL),
        'xa_wkv': jnp.concatenate([wk, wv], axis=-1),
        'xa_wo': w(ks[19], (DEPTH, D_MODEL, D_MODEL), D_MODEL, DEEPNORM_BETA),
        'ffn2_w_gu': w(ks[20], (DEPTH, D_MODEL, 2 * D_FF), D_MODEL, DEEPNORM_BETA),
        'ffn2_w_down': w(ks[21], (DEPTH, D_FF, D_MODEL), D_FF, DEEPNORM_BETA),
    }

def reference(x, mem, ln_g, ln_b, ffn1_w_gu, ffn1_w_down, w_in, conv_w, conv_b, conv_ln_g,
              conv_ln_b, w_conv_proj, hgrn_lb, hgrn_norm_g, w_hgrn_proj, w_mix_out,
              xa_wq, xa_wkv, xa_wo, ffn2_w_gu, ffn2_w_down):
    lb_soft = jax.nn.softmax(hgrn_lb.astype(jnp.float32), axis=0)
    lb_all = jnp.cumsum(lb_soft, axis=0) - lb_soft[0]
    for l in range(DEPTH):
        x = layer_norm(DEEPNORM_ALPHA * x + 0.5 * swiglu(x, ffn1_w_gu[l], ffn1_w_down[l]),
                       ln_g[l, 0], ln_b[l, 0])
        a, b_gate, q, f_logit, i_val, o_gate, gate_a, gate_b = jnp.split(x @ w_in[l], IN_SPLITS, axis=-1)
        y_conv = conformer_conv(a, b_gate, conv_w[l], conv_b[l], conv_ln_g[l], conv_ln_b[l], w_conv_proj[l])
        y_hgrn = hgrn2_branch(q, f_logit, i_val, o_gate, lb_all[l], hgrn_norm_g[l], w_hgrn_proj[l])
        mix = (jax.nn.sigmoid(gate_a) * y_conv + jax.nn.sigmoid(gate_b) * y_hgrn) @ w_mix_out[l]
        x = layer_norm(DEEPNORM_ALPHA * x + mix, ln_g[l, 1], ln_b[l, 1])
        x = layer_norm(DEEPNORM_ALPHA * x + cross_attention(x, mem, xa_wq[l], xa_wkv[l], xa_wo[l]),
                       ln_g[l, 2], ln_b[l, 2])
        x = layer_norm(DEEPNORM_ALPHA * x + 0.5 * swiglu(x, ffn2_w_gu[l], ffn2_w_down[l]),
                       ln_g[l, 3], ln_b[l, 3])
    return x


_drawn_inputs = setup_inputs


def setup_inputs(seed=0):
    import zlib

    import numpy as np

    out = dict(_drawn_inputs(seed))
    spreads = {}
    factors = {'conv_b': 8.0,
     'conv_ln_g': 32.698,
     'conv_ln_b': 33.334,
     'hgrn_lb': 8.0,
     'hgrn_norm_g': 39.387}
    for name, (base, spread) in spreads.items():
        noise = np.random.default_rng([zlib.crc32(name.encode()), seed]).standard_normal(out[name].shape)
        drawn = base * np.exp(spread * noise) if base else spread * noise
        out[name] = __import__('jax').numpy.asarray(drawn.astype(out[name].dtype))
    for name, factor in factors.items():
        out[name] = (out[name] * factor).astype(out[name].dtype)
    return out
```

```python
from contextlib import ExitStack
import math

import numpy as np

import concourse.bass as bass
from concourse import mybir
from concourse.alu_op_type import AluOpType as ALU

ACT = mybir.ActivationFunctionType
F32 = mybir.dt.float32
FR = mybir.dt.float32r
BF16 = mybir.dt.bfloat16
AX_X = mybir.AxisListType.X

P = 128
HALF = 512
RING = 3
CHUNK = 64
CONV_K = 31
LN_EPS = 1e-5
RMS_EPS = 1e-6
KEY_MAX = 1.0 - 1e-6
LEVELS = (32, 16, 8, 4, 2, 1)
NL = len(LEVELS)
DECAYS = NL + 1
MASKS = NL + 1


def layout_constants():
    t = np.arange(P)
    same_chunk = (t[:, None] // CHUNK) == (t[None, :] // CHUNK)
    sums = np.zeros((P, DECAYS, P), np.float32)
    masks = np.zeros((P, MASKS, P), np.float32)
    for i, m in enumerate(LEVELS):
        mid = t // (2 * m) * (2 * m) + m
        late = t >= mid
        src = t[:, None]
        sums[:, i, :] = np.where(late[None, :], (src >= mid[None, :]) & (src <= t[None, :]),
                                 (src > t[None, :]) & (src < mid[None, :]))
        same = (t[:, None] // (2 * m)) == (t[None, :] // (2 * m))
        masks[:, i, :] = same & ~late[:, None] & late[None, :]
    sums[:, NL, :] = same_chunk & (t[:, None] <= t[None, :])
    masks[:, NL, :] = np.eye(P)
    tail = (same_chunk & (t[:, None] > t[None, :])).astype(np.float32)
    chunk_sum = ((t[:, None] // CHUNK) == np.arange(P // CHUNK)[None, :]).astype(np.float32)
    return np.concatenate([sums.reshape(P, -1), tail, chunk_sum, masks.reshape(P, -1),
                           np.eye(P, dtype=np.float32)], axis=1)


class Uses:

    def __init__(self, names):
        self.names = names
        self.n = len(names)

    def __call__(self, name):
        return self.names.index(name)


def build(nc, x, mem, ln_g, ln_b, ffn1_w_gu, ffn1_w_down, w_in, conv_w, conv_b, conv_ln_g, conv_ln_b,
          w_conv_proj, hgrn_lb, hgrn_norm_g, w_hgrn_proj, w_mix_out, xa_wq, xa_wkv, xa_wo,
          ffn2_w_gu, ffn2_w_down, consts, out):
    _, SEQ, D = x.shape
    N_MEM = mem.shape[1]
    L = ln_g.shape[0]
    D_FF = ffn1_w_down.shape[1]
    W = conv_w.shape[2]
    ALPHA = float((2 * L) ** 0.25)
    S = SEQ // P
    KT = D // P
    HEADS = W // P
    XH = 4
    XD = D // XH
    XSCALE = XD ** -0.5
    QSCALE = P ** -0.5
    CF = 256
    NC = D_FF // CF
    NCH = SEQ // CHUNK
    assert S == 2 and KT == 8 and NC * CF == D_FF and N_MEM == SEQ and XD == 2 * P and W == HALF and L == 2

    MID = 44
    FFN_USES = [NC, NC, NC]
    MID_BASE = list(FFN_USES)
    SKIP = 20
    mid_slots = [(u + (u >= SKIP)) % RING for u in range(MID)]
    FFN2_BASE = [MID_BASE[j] + mid_slots.count(j) for j in range(RING)]
    USES = [FFN2_BASE[j] + FFN_USES[j] for j in range(RING)]
    F_BASE = ([0] * RING, FFN2_BASE)

    def mid_unit(u):
        j = mid_slots[u]
        return j, MID_BASE[j] + mid_slots[:u].count(j)

    ffn = [f"gu{f}_{c}" for f in (0, 1) for c in range(NC)]
    W_IN, K_, YC, YH, MO, Q_, V_, WO = 0, 10, 12, 14, 16, 18, 20, 22
    R0 = Uses(ffn[:NC] + ["ln0"] + [f"chunk{c}" for c in range(0, 24, 2)] + ffn[NC:] + ["ln3"])
    R1 = Uses(ffn[:NC] + ["ln0"] + [f"chunk{c}" for c in range(1, 24, 2)] + ffn[NC:] + ["ln3"])

    def chunk_units(ch):
        first = 2 * ch if ch < YC else 2 * YC + ch - YC if ch < MO else 2 * ch - 4
        return (first,) if YC <= ch < MO else (first, first + 1)

    heads = [f"{k}{h}" for h in range(HEADS) for k in "es"]
    R2 = Uses(["acc0", "taps", "conv_h", "q_T", "state"] + heads
              + ["c_seq", "c_T", "mix", "K0", "ln1", "Q0", "score", "P_T", "pv", "ln2", "acc1"])
    R3 = Uses(["acc0", "k_T", "kd", "state"] + heads
              + ["z_T", "mix", "K1", "ln1", "Q1", "score", "P_T", "pv", "ln2", "acc1"])
    R = [R0, R1, R2, R3]
    D0 = Uses(["ln0", "ln3"])
    D1 = Uses(ffn[:NC] + ["ln0"] + ffn[NC:] + ["ln3"])
    D2, D3 = (Uses([k for n in r.names if not n.startswith("acc")
                    for k in ([n, "o" + n[1:]] if n[0] == "s" and n[1:].isdigit() else [n])]) for r in (R2, R3))
    DONE = [D0, D1, D2, D3]

    with ExitStack() as ctx:
        def sb(name, shape, dt=F32):
            return ctx.enter_context(nc.sbuf_tensor(name, shape, dt))

        def sem(name):
            return ctx.enter_context(nc.semaphore(name))

        UNIT = 4 * HALF
        raw = [sb(f"raw{j}", [P, UNIT]) for j in range(RING)]
        w_hi = [sb(f"w_hi{j}", [P, UNIT], FR) for j in range(RING)]
        w_lo = [sb(f"w_lo{j}", [P, UNIT], FR) for j in range(RING)]
        xT_hi = sb("xT_hi", [P, KT, SEQ], FR)
        xT_lo = sb("xT_lo", [P, KT, SEQ], FR)
        memT_hi = sb("memT_hi", [P, KT, SEQ], FR)
        memT_lo = sb("memT_lo", [P, KT, SEQ], FR)
        hT_hi = sb("hT_hi", [P, 2, SEQ], FR)
        hT_lo = sb("hT_lo", [P, 2, SEQ], FR)
        x_res = sb("x_res", [P, S, D])
        y = sb("y", [P, S, D])
        sums = sb("sums", [P, (DECAYS + 1) * P + 2], FR)
        logf_hi = sb("logf_hi", [P, S, W], FR)
        logf_lo = sb("logf_lo", [P, S, W], FR)
        ident = sb("ident", [P, P])
        masks = sb("masks", [P, MASKS * P], BF16)
        rows = sb("rows", [P, 4, HALF])
        rows_ln = rows[:, :, :].rearrange("p (a b) n -> p a (b n)", a=2)
        taps = sb("taps", [P, HEADS, 32])
        stats = sb("stats", [P, S, 12])
        mv = sb("mv", [P, S, 2])
        var = sb("var", [P, S])
        rstd = sb("rstd", [P, S])
        mhalf = sb("mhalf", [P, 8])
        eb = sb("eb", [P, HEADS, NCH])
        sq = sb("sq", [P, S, HEADS])
        squares = sb("squares", [P, S, P])
        rrms = sb("rrms", [P, S, HEADS])
        mx = sb("mx", [P, 2, 4])
        den = sb("den", [P, 2, 4])
        rden = sb("rden", [P, 2, 4])

        ARENA = 15104
        arena = sb("arena", [P, ARENA])
        top = [0]

        def cut(n):
            top[0] += n
            assert top[0] <= ARENA
            return arena[:, top[0] - n:top[0]]

        def by(ap, a):
            return ap.rearrange("p (a n) -> p a n", a=a)

        sigA = by(cut(S * D), S)
        sigB = by(cut(S * D), S)
        E = by(cut(DECAYS * SEQ), DECAYS)
        kT = by(cut(HEADS * SEQ), HEADS)
        qT = by(cut(HEADS * SEQ), HEADS)
        v_seq = by(cut(S * W), S)
        kd = by(cut(S * W), S)
        logf = kd
        og = by(cut(S * W), S)
        PAD = CONV_K - 1
        hc = by(cut(HEADS * (SEQ + PAD)), HEADS)
        acc = by(cut(HEADS * SEQ), HEADS)
        conv_rows = arena[:, top[0]:top[0] + W]
        state = cut((NCH - 1) * W).rearrange("p (c h v) -> p c h v", c=NCH - 1, h=HEADS)
        ST = by(cut(S * P), S)
        k_seq = y[:, 0, :].rearrange("p (s n) -> p s n", s=S)
        q_seq = y[:, 1, :].rearrange("p (s n) -> p s n", s=S)
        sig_b, h_seq, sig_c = og, by(acc.rearrange("p h t -> p (h t)"), S), by(acc.rearrange("p h t -> p (h t)"), S)
        prod, c_seq, o_seq = y[:, 0, 0:MASKS * P], k_seq, q_seq
        top[0] = 0
        KTx = by(cut(KT * N_MEM), KT)
        QTx = by(cut(KT * SEQ), KT)
        kseq_x = [by(cut(S * HALF), S) for _ in range(2)]
        Vx = by(cut(S * D), S)
        qseq_x = [by(cut(S * HALF), S) for _ in range(2)]
        Px = by(cut(XH * S * N_MEM), XH * S)
        PTx = cut(XH * 2 * SEQ).rearrange("p (h m t) -> p h m t", h=XH, m=2)
        top[0] = 0
        sg = by(cut(S * CF), S)
        hx = by(cut(S * CF), S)

        ps = ctx.enter_context(nc.psum_tensor("ps", [P, 8, HALF], F32))

        def bank(r, i=0):
            return ps[:, 2 * r + i, :]

        def pair(r):
            return ps[:, 2 * r:2 * r + 2, :].rearrange("p b n -> p (b n)")

        scratch = nc.dram_tensor("key_scale", [L, W], F32, kind="Internal").ap()

        raw_landed = [sem(f"raw_landed{j}") for j in range(RING)]
        hi_ready = [sem(f"hi_ready{j}") for j in range(RING)]
        lo_ready = [sem(f"lo_ready{j}") for j in range(RING)]
        unit_done = [sem(f"unit_done{j}") for j in range(RING)]
        psum_read = [sem(f"psum_read{r}") for r in range(4)]
        done = [sem(f"psum_done{r}") for r in range(4)]
        acc0_done = sem("acc0_done")
        rows0_done = sem("rows0_done")
        in_landed = sem("in_landed")
        slot_free = sem("slot_free")
        const_landed = sem("const_landed")
        pro_T = sem("pro_T")
        pro_hi = sem("pro_hi")
        pro_lo = sem("pro_lo")
        rest_landed = sem("rest_landed")
        lb_landed = sem("lb_landed")
        sums_ready = sem("sums_ready")
        masks_ready = sem("masks_ready")
        conv_landed = sem("conv_landed")
        mem_landed = sem("mem_landed")
        mhalf_ready = sem("mhalf_ready")
        lb_centered = sem("lb_centered")
        lb_exp = sem("lb_exp")
        key_ready = sem("key_ready")
        scratch_stored = sem("scratch_stored")
        rows_landed = sem("rows_landed")
        rows_used = sem("rows_used")
        sig_ready = sem("sig_ready")
        hThi_ready = sem("hThi_ready")
        var_ready = sem("var_ready")
        rstd_ready = sem("rstd_ready")
        x_ready = sem("x_ready")
        xThi_ready = sem("xThi_ready")
        names = ["kscaled", "logf_hi", "logf_lo", "sigq", "kd", "sigo", "eb", "X", "ST", "sq", "ms", "rrms", "z", "zThi", "cvar",
                 "crstd", "c_norm", "sigc", "c_out", "cThi", "conv", "mix", "mixThi", "mx", "Pn", "oThi"]
        ev = {n: sem(n + "_ready") for n in names}
        out_stored = sem("out_stored")

        PER = dict.fromkeys(names, 1)
        PER.update(X=HEADS, ST=2 * HEADS, mixThi=2, mx=2, Pn=2, oThi=2)

        def wait_event(eng, l, name, k=1):
            eng.wait_ge(ev[name], l * PER[name] + k)

        def wait_unit_done(eng, l, slot, use):
            eng.wait_ge(unit_done[slot], l * USES[slot] + use + 2)

        def wait_chunk(eng, l, ch):
            wait_unit_done(eng, l, *mid_unit(chunk_units(ch)[-1]))

        def wait_rows(eng, l, ch, s):
            if s == 0:
                eng.wait_ge(rows0_done, l * 2 + (1 if ch < WO else 2))
            else:
                wait_chunk(eng, l, ch)

        def wait_done(eng, l, r, name):
            eng.wait_ge(done[r], l * DONE[r].n + DONE[r](name) + 1)

        def wait_done_step(eng, l, r, f, c):
            eng.wait_ge(done[r], l * DONE[r].n + DONE[r](f"gu{f}_0") + c + 1)

        def wait_room(eng, l, r, name):
            eng.wait_ge(psum_read[r], l * R[r].n + R[r](name) + 1)

        def wait_read(eng, l, r, name):
            eng.wait_ge(psum_read[r], l * R[r].n + R[r](name) + 2)

        def wait_room_step(eng, l, r, f, c):
            eng.wait_ge(psum_read[r], c + (l * R[r].n + R[r](f"gu{f}_0") + 1))

        def wait_read_step(eng, l, r, f, c):
            eng.wait_ge(psum_read[r], c + (l * R[r].n + R[r](f"gu{f}_0") + 2))

        block = ctx.enter_context(nc.Block())

        @block.sync
        def _(sp):
            sp.dma_start(x_res[:, :, :], x[0].rearrange("(s p) d -> p s d", p=P)).then_inc(in_landed, 16)

            def load(l, slot, use, *parts):
                sp.wait_ge(lo_ready[slot], l * USES[slot] + use + 1)
                sp.sem_inc(slot_free, 1)
                for dst, src in parts:
                    sp.dma_start(dst, src).then_inc(raw_landed[slot], 16)

            def load_gu(l, f, w, c, part, slot, use):
                src = w.rearrange("l (t p) (g n) -> l g p t n", p=P, g=2)
                dst = raw[slot][:, :].rearrange("p (t g n) -> p g t n", t=4, g=2)
                load(l, slot, use, *[(dst[:, g], src[l, g, :, 4 * part:4 * part + 4, bass.ds(c * CF, CF)])
                                     for g in range(2)])

            def load_down(l, f, w, c, slot, use):
                src = w.rearrange("l (t p) n -> l p t n", p=P)
                load(l, slot, use, *[(raw[slot][:, i * D:(i + 1) * D], src[l, :, bass.ds(c * 2 + i, 1), :])
                                     for i in range(2)])

            def load_ffn(l, f, w_gu, w_down):
                b = F_BASE[f]
                load_gu(l, f, w_gu, 0, 0, 0, b[0])
                load_gu(l, f, w_gu, 0, 1, 1, b[1])
                with sp.Fori(1, NC) as c:
                    load_gu(l, f, w_gu, c, 0, 2, c + (b[2] - 1))
                    load_gu(l, f, w_gu, c, 1, 0, c + b[0])
                    load_down(l, f, w_down, c - 1, 1, c + b[1])
                load_down(l, f, w_down, NC - 1, 2, b[2] + NC - 1)

            def load_cols(l, u, w, rows0, cols0):
                src = w.rearrange("l (t p) n -> l p t n", p=P)
                t0 = rows0 // P
                slot, use = mid_unit(u)
                dst = raw[slot][:, :].rearrange("p (t n) -> p t n", t=4)
                load(l, slot, use, *[(dst[:, t:t + 2], src[l, :, t0 + t:t0 + t + 2, cols0:cols0 + HALF])
                                     for t in (0, 2)])

            with sp.Fori(0, L) as l:
                load_ffn(l, 0, ffn1_w_gu, ffn1_w_down)
                u = 0
                order = [1, 0, 3, 2, 4, 5, 6, 7, 8, 9]
                for col in order:
                    for part in range(2):
                        load_cols(l, u, w_in, part * HALF, col * HALF)
                        u += 1
                for w, first in ((xa_wkv, 0), (w_conv_proj, 0), (w_hgrn_proj, 0), (w_mix_out, 0), (xa_wq, 0),
                                 (xa_wkv, D), (xa_wo, 0)):
                    for n in range(2):
                        for part in range(w.shape[1] // HALF):
                            load_cols(l, u, w, part * HALF, first + n * HALF)
                            u += 1
                assert u == MID
                load_ffn(l, 1, ffn2_w_gu, ffn2_w_down)
            sp.wait_ge(x_ready, 8 * L)
            sp.dma_start(out[0].rearrange("(s p) d -> p s d", p=P), x_res[:, :, :]).then_inc(out_stored, 16)
            sp.wait_ge(out_stored, 16)

        @block.gpsimd
        def _(pool):
            cn = (DECAYS + 1) * P + 2
            consts_in = arena[:, S * D:S * D + cn + MASKS * P]
            pool.dma_start(consts_in, consts[:, 0:cn + MASKS * P]).then_inc(rest_landed, 16)
            pool.memset(mhalf[:, :], -0.5).then_inc(mhalf_ready, 1)
            pool.wait_ge(key_ready, 1)
            pool.dma_start(scratch.rearrange("l n -> (l n)")[None, :],
                           kT[0:1, :, :].rearrange("p a b -> p (a b)")).then_inc(scratch_stored, 16)
            pool.wait_ge(scratch_stored, 16)
            pool.wait_ge(mhalf_ready, 1)
            pool.wait_ge(rest_landed, 16)
            pool.tensor_copy(masks[:, :], consts_in[:, cn:]).then_inc(masks_ready, 1)
            pool.tensor_copy(sums[:, :], consts_in[:, 0:cn]).then_inc(sums_ready, 1)

            def load_ln(l, n):
                pool.wait_ge(rows_used, l * 5 + n + 1)
                k = n if n == 0 else n - 1
                pool.dma_start(rows_ln[:, 0, :], ln_g[l, k:k + 1, :].broadcast_to([P, D])).then_inc(rows_landed, 16)
                pool.dma_start(rows_ln[:, 1, :], ln_b[l, k:k + 1, :].broadcast_to([P, D])).then_inc(rows_landed, 16)

            def power(l, k, per, src_sem, out_sem, dst, src):
                pool.wait_ge(src_sem, l * per + k)
                pool.tensor_tensor(dst, src, mhalf[:, 0:src.shape[1]], ALU.pow).then_inc(out_sem, 1)

            def ln_powers(l, n):
                for s in range(S):
                    power(l, 2 * n + s + 1, 8, var_ready, rstd_ready, rstd[:, s:s + 1], var[:, s:s + 1])

            with pool.Fori(0, L) as l:
                load_ln(l, 0)
                ln_powers(l, 0)
                pool.wait_ge(rows_used, l * 5 + 2)
                for i, a in enumerate((conv_ln_g, conv_ln_b, hgrn_norm_g, scratch)):
                    pool.dma_start(rows[:, i, :], a[bass.ds(l, 1), :].broadcast_to([P, W])).then_inc(rows_landed, 16)
                pool.dma_start(conv_rows[0:CONV_K, :], conv_w[l]).then_inc(conv_landed, 16)
                pool.dma_start(conv_rows[CONV_K:32, :], conv_b[bass.ds(l, 1), :]).then_inc(conv_landed, 16)
                pool.wait_ge(ev["ms"], l + 1)
                pool.tensor_tensor(rrms[:, :, :], sq[:, :, :], mhalf[:, 0:8].rearrange("p (a b) -> p a b", a=2),
                                   ALU.pow).then_inc(ev["rrms"], 1)
                pool.wait_ge(ev["cvar"], l + 1)
                pool.tensor_tensor(rstd[:, :], var[:, :], mhalf[:, 0:2], ALU.pow).then_inc(ev["crstd"], 1)
                for n in (1, 2, 3):
                    load_ln(l, n + 1)
                    ln_powers(l, n)

        @block.scalar
        def _(act):
            sc = nc.scalar

            def hi(l, slot, use):
                act.wait_ge(raw_landed[slot], (l * USES[slot] + use + 1) * 32)
                act.wait_ge(unit_done[slot], l * USES[slot] + use + 1)
                sc.copy(w_hi[slot][:, :], raw[slot][:, :]).then_inc(hi_ready[slot], 1)

            def mid_hi(l, *us):
                for u in us:
                    hi(l, *mid_unit(u))

            def split_hi(dst, r, width=2 * HALF):
                return sc.copy(dst, pair(r)[:, 0:width].rearrange("p (a n) -> p a n", a=dst.shape[1]))

            def ln_T(l, n, regs):
                for s in range(S):
                    wait_done(act, l, regs[s], f"ln{n}")
                    split_hi(xT_hi[:, :, s * P:(s + 1) * P], regs[s]).then_inc(xThi_ready, 1)

            act.dma_start(ident[:, :], consts[:, consts.shape[1] - P:]).then_inc(const_landed, 16)
            act.dma_start(E[0:1, 0:4, :].rearrange("p a b -> p (a b)"),
                          hgrn_lb.rearrange("l n -> (l n)")[None, :]).then_inc(lb_landed, 16)
            act.dma_start(y[:, :, :], mem[0].rearrange("(s p) d -> p s d", p=P)).then_inc(mem_landed, 16)
            act.wait_ge(lb_centered, 1)
            sc.activation(E[0:1, 0:4, :], E[0:1, 0:4, :], ACT.Exp).then_inc(lb_exp, 1)
            for i, dst in enumerate((xT_hi, memT_hi)):
                for s in range(S):
                    act.wait_ge(pro_T, 2 * i + s + 1)
                    split_hi(dst[:, :, s * P:(s + 1) * P], 2 * i + s).then_inc(pro_hi, 1)
            def ffn_act(l, f):
                b = F_BASE[f]

                def gate(c):
                    wait_unit_done(act, l, *((1, b[1]) if isinstance(c, int) and c == 0 else (0, c + b[0])))
                    for s in range(S):
                        sc.activation(sg[:, s, :], bank(0, s)[:, 0:CF], ACT.Sigmoid).then_inc(sig_ready, 1)

                def hT(c, dst=hT_hi, last=False):
                    wait_done_step(act, l, 1, f, c)
                    if not last and not (isinstance(c, int) and c == 0):
                        wait_unit_done(act, l, 1, c + b[1])
                    sc.copy(dst[:, 0:2, :], bank(1)[:, :].rearrange("p (a n) -> p a n", a=2)).then_inc(hThi_ready, 1)

                if f == 0:
                    hi(l, 0, b[0])
                    hi(l, 1, b[1])
                hi(l, 2, b[2])
                gate(0)
                hi(l, 0, b[0] + 1)

                def step(c, last):
                    hi(l, 1, c + b[1])
                    hT(c - 1)
                    hi(l, 2, c + b[2])
                    wait_read_step(act, l, 0, f, c - 1)
                    gate(c)
                    if not (last and f):
                        hi(l, 0, c + (b[0] + 1))

                step(1, False)
                with act.Fori(2, NC - 1) as c:
                    step(c, False)
                step(NC - 1, True)
                hT(NC - 1, xT_hi, True)

            with act.Fori(0, L) as l:
                ffn_act(l, 0)
                mid_hi(l, 1)
                ln_T(l, 0, (0, 1))
                mid_hi(l, 2, 3)
                wait_chunk(act, l, 0)
                for s in range(S):
                    i = sc.activation(sig_b[:, s, :], bank(0, s), ACT.Sigmoid)
                i.then_inc(psum_read[0], 1)
                mid_hi(l, 4, 5, 6)
                wait_done(act, l, 2, "taps")
                sc.copy(taps[:, :, :], bank(2)[:, 0:HEADS * 32].rearrange("p (h t) -> p h t", h=HEADS))\
                    .then_inc(psum_read[2], 1)
                wait_done(act, l, 2, "conv_h")
                sc.copy(hc[:, :, PAD:], pair(2).rearrange("p (a n) -> p a n", a=HEADS)).then_inc(psum_read[2], 1)
                mid_hi(l, 7)
                wait_chunk(act, l, 2)
                for s in range(S):
                    i = sc.activation(k_seq[:, s, :], bank(0, s), ACT.Sigmoid, scale=-1.0)
                i.then_inc(psum_read[0], 1)
                mid_hi(l, 8, 9)
                wait_chunk(act, l, 3)
                for s in range(S):
                    i = sc.activation(q_seq[:, s, :], bank(1, s), ACT.Sigmoid)
                i.then_inc(ev["sigq"], 1)
                wait_event(act, l, "kscaled")
                sc.activation(logf[:, :, :], logf[:, :, :], ACT.Ln, scale=-1.0, bias=1.0)
                act.drain()
                sc.copy(logf_hi[:, :, :], logf[:, :, :]).then_inc(ev["logf_hi"], 1)
                mid_hi(l, 10)
                wait_done(act, l, 3, "k_T")
                sc.copy(kT[:, :, :], pair(3).rearrange("p (a n) -> p a n", a=HEADS)).then_inc(psum_read[3], 1)
                mid_hi(l, 11)
                wait_chunk(act, l, 4)
                for s in range(S):
                    i = sc.copy(v_seq[:, s, :], bank(0, s))
                i.then_inc(psum_read[0], 1)
                wait_done(act, l, 2, "q_T")
                sc.copy(qT[:, :, :], pair(2).rearrange("p (a n) -> p a n", a=HEADS)).then_inc(psum_read[2], 1)
                wait_done(act, l, 3, "kd")
                sc.activation(kd[:, :, :], pair(3).rearrange("p (a n) -> p a n", a=S), ACT.Exp).then_inc(psum_read[3], 1)
                mid_hi(l, 12, 13)
                wait_done(act, l, 3, "state")
                sc.activation(eb[:, :, :], bank(3, 1)[:, 0:HEADS * NCH].rearrange("p (h c) -> p h c", h=HEADS),
                              ACT.Exp).then_inc(ev["eb"], 1)

                def decays(h):
                    if h:
                        wait_done(act, l, 3, f"s{h - 1}")
                    for s in range(S):
                        wait_done(act, l, 2 + s, f"e{h}")
                        sc.activation(E[:, :, s * P:(s + 1) * P],
                                      pair(2 + s)[:, 0:DECAYS * P].rearrange("p (a n) -> p a n", a=DECAYS),
                                      ACT.Exp).then_inc(psum_read[2 + s], 1)

                def gate_chunk(ch, dst):
                    wait_chunk(act, l, ch)
                    for s in range(S):
                        i = sc.activation(dst[:, s, :], bank(ch % 2, s), ACT.Sigmoid)
                    return i

                def copy_chunk(ch, dst):
                    wait_chunk(act, l, ch)
                    for s in range(S):
                        i = sc.copy(dst[:, s, :], bank(ch % 2, s))
                    i.then_inc(psum_read[ch % 2], 1)

                def out_rows(h):
                    for s in range(S):
                        wait_done(act, l, 2 + s, f"o{h}")
                        o = pair(2 + s)[:, MASKS * P:]
                        sc.activation(squares[:, s, :], o, ACT.Square, accum_out=sq[:, s, h:h + 1])
                        sc.copy(o_seq[:, s, h * P:(h + 1) * P], o).then_inc(psum_read[2 + s], 1)
                    return act.drain()

                decays(0)
                gate_chunk(5, og).then_inc(ev["sigo"], 1)
                mid_hi(l, 14, 15)
                gate_chunk(6, sigA[:, :, 0:HALF]).then_inc(psum_read[0], 1)
                out_rows(0)
                decays(1)
                mid_hi(l, 16)
                gate_chunk(7, sigA[:, :, HALF:D]).then_inc(psum_read[1], 1)
                mid_hi(l, 17)
                out_rows(1)
                decays(2)
                mid_hi(l, 18)
                gate_chunk(8, sigB[:, :, 0:HALF]).then_inc(psum_read[0], 1)
                mid_hi(l, 19)
                out_rows(2)
                decays(3)
                mid_hi(l, 20)
                gate_chunk(9, sigB[:, :, HALF:D]).then_inc(psum_read[1], 1)
                mid_hi(l, 21)
                out_rows(3).then_inc(ev["sq"], 1)
                mid_hi(l, 22)
                copy_chunk(K_, kseq_x[0])
                mid_hi(l, 23, 24)
                wait_event(act, l, "c_norm")
                sc.activation(sig_c[:, :, :], c_seq[:, :, :], ACT.Sigmoid).then_inc(ev["sigc"], 1)
                copy_chunk(K_ + 1, kseq_x[1])
                wait_done(act, l, 3, "z_T")
                split_hi(xT_hi[:, 4:8, :], 3).then_inc(ev["zThi"], 1)
                wait_done(act, l, 2, "c_T")
                split_hi(xT_hi[:, 0:4, :], 2).then_inc(ev["cThi"], 1)
                mid_hi(l, 25, 26, 27, 28, 29, 30)
                wait_chunk(act, l, YH + 1)
                for s in range(S):
                    wait_done(act, l, 2 + s, "mix")
                    split_hi(xT_hi[:, :, s * P:(s + 1) * P], 2 + s).then_inc(ev["mixThi"], 1)

                def copy_T(r, use, dst):
                    wait_done(act, l, r, use)
                    sc.copy(dst, pair(r).rearrange("p (a n) -> p a n", a=4)).then_inc(psum_read[r], 1)

                copy_T(2, "K0", KTx[:, 0:4, :])
                copy_T(3, "K1", KTx[:, 4:8, :])
                mid_hi(l, 31, 32, 33)
                ln_T(l, 1, (2, 3))
                mid_hi(l, 34, 35)
                copy_chunk(Q_, qseq_x[0])
                mid_hi(l, 36, 37)
                copy_chunk(Q_ + 1, qseq_x[1])
                copy_T(2, "Q0", QTx[:, 0:4, :])
                copy_T(3, "Q1", QTx[:, 4:8, :])
                mid_hi(l, 38)

                def softmax(g):
                    wait_event(act, l, "mx", g + 1)
                    for i in range(4):
                        k = sc.activation(Px[:, 4 * g + i, :], pair(2 + g)[:, i * N_MEM:(i + 1) * N_MEM], ACT.Exp,
                                          bias=mx[:, g, i:i + 1], scale=XSCALE, accum_out=den[:, g, i:i + 1])
                    k.then_inc(psum_read[2 + g], 1)

                softmax(0)
                softmax(1)
                mid_hi(l, 39)
                copy_chunk(V_, Vx[:, :, 0:HALF])
                mid_hi(l, 40, 41)
                copy_chunk(V_ + 1, Vx[:, :, HALF:D])
                for g in range(2):
                    wait_done(act, l, 2 + g, "P_T")
                    sc.copy(PTx[:, 2 * g:2 * g + 2, :, :].rearrange("p h m t -> p (h m t)"), pair(2 + g)).then_inc(psum_read[2 + g], 1)
                for g in range(2):
                    wait_done(act, l, 2 + g, "pv")
                    split_hi(xT_hi[:, 4 * g:4 * g + 4, :], 2 + g).then_inc(ev["oThi"], 1)
                mid_hi(l, 42, 43)
                hi(l, 0, FFN2_BASE[0])
                hi(l, 1, FFN2_BASE[1])
                ln_T(l, 2, (2, 3))
                ffn_act(l, 1)
                ln_T(l, 3, (0, 1))

        @block.vector
        def _(dve):
            v = nc.vector

            def lo(l, slot, use):
                dve.wait_ge(hi_ready[slot], l * USES[slot] + use + 1)
                v.tensor_tensor(w_lo[slot][:, :], raw[slot][:, :], w_hi[slot][:, :], ALU.subtract).then_inc(lo_ready[slot], 1)

            def mid_lo(l, *us):
                for u in us:
                    lo(l, *mid_unit(u))

            def split_lo(dst, hi, r):
                n = dst.shape[1]
                return v.tensor_tensor(dst, pair(r).rearrange("p (a n) -> p a n", a=n), hi, ALU.subtract)

            for s_ in lo_ready + unit_done + psum_read:
                dve.sem_inc(s_, 1)
            dve.wait_ge(lb_landed, 16)
            lbv = E[0:1, 0:4, :].rearrange("p a b -> p (a b)")
            m0 = E[0:1, 4:6, :].rearrange("p a b -> p (a b)")
            key = kT[0:1, :, :].rearrange("p a b -> p (a b)")
            v.tensor_tensor(m0, lbv[:, 0:W], lbv[:, W:2 * W], ALU.max)
            dve.drain()
            for l in range(L):
                i = v.tensor_tensor(lbv[:, l * W:(l + 1) * W], lbv[:, l * W:(l + 1) * W], m0, ALU.subtract)
            dve.drain()
            v.memset(key[:, 0:W], 1.0).then_inc(lb_centered, 1)
            dve.wait_ge(lb_exp, 1)
            v.tensor_tensor(m0, lbv[:, 0:W], lbv[:, W:2 * W], ALU.add)
            dve.drain()
            v.reciprocal(m0, m0)
            dve.drain()
            v.tensor_tensor(key[:, W:2 * W], lbv[:, W:2 * W], m0, ALU.mult)
            dve.drain()
            v.tensor_scalar(key[:, W:2 * W], key[:, W:2 * W], -1.0, 1.0, ALU.mult, ALU.add).then_inc(key_ready, 1)
            for i, (hi_, lo_) in enumerate(((xT_hi, xT_lo), (memT_hi, memT_lo))):
                for s in range(S):
                    dve.wait_ge(pro_hi, 2 * i + s + 1)
                    c = slice(s * P, (s + 1) * P)
                    split_lo(lo_[:, :, c], hi_[:, :, c], 2 * i + s).then_inc(pro_lo, 1)
            dve.sem_inc(rows_used, 1)

            def layer_norm(l, n, src, wait_src, free_regs, regs, between):

                def moments(s):
                    wait_src(s)
                    for i in range(2):
                        c = slice(i * HALF, (i + 1) * HALF)
                        k = v.scalar_tensor_tensor(y[:, s, c], x_res[:, s, c], ALPHA, src(s, i), ALU.mult, ALU.add)
                        if free_regs is not None:
                            if i == 1:
                                k.then_inc(psum_read[free_regs[s]], 1)
                        elif s == 1:
                            k.then_inc(psum_read[i], 1)
                    dve.drain()
                    for i in range(2):
                        v.bn_stats(stats[:, s, 6 * i:6 * i + 6], y[:, s, i * HALF:(i + 1) * HALF])
                    dve.drain()
                    v.bn_aggr(mv[:, s, :], stats[:, s, :])
                    dve.drain()
                    v.tensor_scalar(var[:, s:s + 1], mv[:, s, 1:2], LN_EPS, None, ALU.add).then_inc(var_ready, 1)

                def scale(s):
                    if s == 0:
                        dve.wait_ge(rows_landed, l * 16 * 12 + 16 * (2, 8, 10, 12)[n])
                    v.scalar_tensor_tensor(y[:, s, :], y[:, s, :], mv[:, s, 0:1], rows_ln[:, 0, :],
                                           ALU.subtract, ALU.mult)
                    dve.drain()
                    dve.wait_ge(rstd_ready, l * 8 + 2 * n + s + 1)
                    v.scalar_tensor_tensor(x_res[:, s, :], y[:, s, :], rstd[:, s:s + 1], rows_ln[:, 1, :],
                                           ALU.mult, ALU.add).then_inc(x_ready, 1)

                def split(s):
                    dve.wait_ge(xThi_ready, l * 8 + 2 * n + s + 1)
                    c = slice(s * P, (s + 1) * P)
                    split_lo(xT_lo[:, :, c], xT_hi[:, :, c], regs[s]).then_inc(psum_read[regs[s]], 1)

                moments(0)
                scale(0)
                moments(1)
                split(0)
                between()
                scale(1)
                dve.drain().then_inc(rows_used, 1)
                split(1)

            def ffn_dve(l, f):
                b = F_BASE[f]

                def gate(c):
                    if not (isinstance(c, int) and c == 0):
                        wait_done_step(dve, l, 1, f, c - 1)
                    for s in range(S):
                        dve.wait_ge(sig_ready, (l * 2 + f) * 2 * NC + c * 2 + (s + 1))
                        v.scalar_tensor_tensor(hx[:, s, :], bank(0, s)[:, 0:CF], 0.5, sg[:, s, :], ALU.mult, ALU.mult)
                    dve.drain()
                    for s in range(S):
                        i = v.tensor_tensor(hx[:, s, :], bank(0, s)[:, CF:2 * CF], hx[:, s, :], ALU.mult)
                    i.then_inc(psum_read[0], 1)

                def hT(c, lo_=hT_lo, hi_=hT_hi):
                    dve.wait_ge(hThi_ready, (l * 2 + f) * NC + c + 1)
                    v.tensor_tensor(lo_[:, 0:2, :], bank(1)[:, :].rearrange("p (a n) -> p a n", a=2), hi_[:, 0:2, :],
                                    ALU.subtract).then_inc(psum_read[1], 1)

                if f == 0:
                    lo(l, 0, b[0])
                    lo(l, 1, b[1])
                lo(l, 2, b[2])
                gate(0)
                lo(l, 0, b[0] + 1)

                def step(c, last):
                    lo(l, 1, c + b[1])
                    hT(c - 1)
                    lo(l, 2, c + b[2])
                    gate(c)
                    if not (last and f):
                        lo(l, 0, c + (b[0] + 1))

                with dve.Fori(1, NC - 1) as c:
                    step(c, False)
                step(NC - 1, True)
                hT(NC - 1, xT_lo, xT_hi)

                def wait_acc(s):
                    if s == 0:
                        dve.wait_ge(acc0_done, l * 2 + f + 1)
                    else:
                        wait_unit_done(dve, l, 2, b[2] + NC - 1)

                return wait_acc

            with dve.Fori(0, L) as l:
                wait_acc = ffn_dve(l, 0)
                layer_norm(l, 0, lambda s, i: bank(2 + s, i), wait_acc, (2, 3), (0, 1), lambda: mid_lo(l, 1))
                mid_lo(l, 2, 3, 4, 5)
                v.memset(hc[:, :, 0:PAD], 0.0)
                wait_chunk(dve, l, 1)
                wait_read(dve, l, 0, "chunk0")
                for s in range(S):
                    i = v.tensor_tensor(h_seq[:, s, :], bank(1, s), sig_b[:, s, :], ALU.mult)
                i.then_inc(psum_read[1], 1)
                mid_lo(l, 6, 7)
                wait_read(dve, l, 0, "chunk2")
                dve.wait_ge(rows_landed, l * 16 * 12 + 16 * 6)
                for s in range(S):
                    v.tensor_tensor(k_seq[:, s, :], k_seq[:, s, :], rows[:, 3, :], ALU.mult)
                dve.drain()
                v.tensor_scalar(logf[:, :, :], k_seq[:, :, :], KEY_MAX, None, ALU.min).then_inc(ev["kscaled"], 1)

                def conv(first, last):
                    for j in range(first, last):
                        if j:
                            dve.drain()
                        for g in range(HEADS):
                            src = hc[:, g, j:j + SEQ]
                            if j == 0:
                                i = v.tensor_scalar(acc[:, g, :], src, taps[:, g, 0:1], taps[:, g, CONV_K:CONV_K + 1],
                                                    ALU.mult, ALU.add)
                            else:
                                i = v.scalar_tensor_tensor(acc[:, g, :], src, taps[:, g, j:j + 1], acc[:, g, :],
                                                           ALU.mult, ALU.add)
                    return i

                wait_read(dve, l, 2, "conv_h")
                conv(0, 3)
                mid_lo(l, 8)
                wait_event(dve, l, "logf_hi")
                v.tensor_tensor(logf_lo[:, :, :], logf[:, :, :], logf_hi[:, :, :], ALU.subtract).then_inc(ev["logf_lo"], 1)
                conv(3, 5)
                mid_lo(l, 9)
                wait_event(dve, l, "sigq")
                for s in range(S):
                    i = v.scalar_tensor_tensor(q_seq[:, s, :], bank(1, s), QSCALE, q_seq[:, s, :], ALU.mult, ALU.mult)
                i.then_inc(psum_read[1], 1)
                conv(5, 8)
                mid_lo(l, 10)
                conv(8, 11)
                mid_lo(l, 11)
                wait_read(dve, l, 3, "kd")
                v.tensor_tensor(kd[:, :, :], kd[:, :, :], k_seq[:, :, :], ALU.mult).then_inc(ev["kd"], 1)
                conv(11, 14)
                mid_lo(l, 12)
                conv(14, 17)
                mid_lo(l, 13)
                wait_done(dve, l, 2, "state")
                wait_event(dve, l, "eb")
                v.tensor_copy(state[:, 0, :, :], bank(2, 0).rearrange("p (h v) -> p h v", h=HEADS))
                dve.drain()
                for c in range(1, NCH - 1):
                    u_c = bank(2, 1) if c == 1 else bank(3, 0)
                    for h in range(HEADS):
                        i = v.scalar_tensor_tensor(state[:, c, h, :], state[:, c - 1, h, :], eb[:, h, c:c + 1],
                                                   u_c[:, h * P:(h + 1) * P], ALU.mult, ALU.add)
                        if h == HEADS - 1:
                            i.then_inc(psum_read[2] if c == 1 else psum_read[3], 1)
                    dve.drain()

                def scale_keys(h):
                    wait_read(dve, l, 2, f"e{h}")
                    wait_read(dve, l, 3, f"e{h}")
                    for i, m in enumerate(LEVELS):
                        half = lambda ap, k: ap.rearrange("p (b k m) -> p b k m", k=2, m=m)[:, :, k, :]
                        for k, src in ((0, kT), (1, qT)):
                            v.tensor_tensor(half(E[:, i, :], k), half(E[:, i, :], k), half(src[:, h, :], k), ALU.mult)
                    v.tensor_tensor(E[:, NL, :], E[:, NL, :], qT[:, h, :], ALU.mult).then_inc(ev["X"], 1)

                def scores(h):
                    for s in range(S):
                        wait_done(dve, l, 2 + s, f"s{h}")
                        v.tensor_tensor(prod, pair(2 + s)[:, 0:MASKS * P], masks[:, :], ALU.mult)
                        dve.drain()
                        v.tensor_reduce(ST[:, s, :], prod.rearrange("p (i t) -> p t i", i=MASKS), AX_X, ALU.add)\
                            .then_inc(ev["ST"], 1)
                        dve.drain()

                scale_keys(0)
                wait_event(dve, l, "sigo")
                for s in range(S):
                    i = v.tensor_tensor(og[:, s, :], bank(1, s), og[:, s, :], ALU.mult)
                i.then_inc(psum_read[1], 1)
                dve.drain()
                for s in range(S):
                    v.tensor_tensor(og[:, s, :], og[:, s, :], rows[:, 2, :], ALU.mult)
                dve.wait_ge(masks_ready, 1)
                mid_lo(l, 14)
                scores(0)
                conv(17, 19)
                mid_lo(l, 15)
                scale_keys(1)
                conv(19, 21)
                mid_lo(l, 16)
                scores(1)
                conv(21, 23)
                mid_lo(l, 17)
                scale_keys(2)
                conv(23, 25)
                mid_lo(l, 18)
                scores(2)
                conv(25, 27)
                mid_lo(l, 19)
                scale_keys(3)
                mid_lo(l, 20)
                scores(3)
                conv(27, 29)
                mid_lo(l, 21)
                conv(29, CONV_K).then_inc(ev["conv"], 1)
                mid_lo(l, 22)
                wait_event(dve, l, "sq")
                v.tensor_scalar(sq[:, :, :], sq[:, :, :], 1.0 / P, RMS_EPS, ALU.mult, ALU.add).then_inc(ev["ms"], 1)
                wait_done(dve, l, 2, "c_seq")
                for s in range(S):
                    v.bn_stats(stats[:, s, 0:6], bank(2, s))
                dve.drain()
                for s in range(S):
                    v.bn_aggr(mv[:, s, :], stats[:, s, 0:6])
                dve.drain()
                v.tensor_scalar(var[:, :], mv[:, :, 1], LN_EPS, None, ALU.add).then_inc(ev["cvar"], 1)
                for s in range(S):
                    i = v.scalar_tensor_tensor(c_seq[:, s, :], bank(2, s), mv[:, s, 0:1], rows[:, 0, :],
                                               ALU.subtract, ALU.mult)
                i.then_inc(psum_read[2], 1)
                dve.drain()
                wait_event(dve, l, "crstd")
                for s in range(S):
                    i = v.scalar_tensor_tensor(c_seq[:, s, :], c_seq[:, s, :], rstd[:, s:s + 1], rows[:, 1, :],
                                               ALU.mult, ALU.add)
                i.then_inc(ev["c_norm"], 1)
                wait_event(dve, l, "rrms")
                for h in range(HEADS):
                    for s in range(S):
                        c = slice(h * P, (h + 1) * P)
                        i = v.scalar_tensor_tensor(o_seq[:, s, c], o_seq[:, s, c], rrms[:, s, h:h + 1], og[:, s, c],
                                                   ALU.mult, ALU.mult)
                i.then_inc(ev["z"], 1)
                wait_event(dve, l, "sigc")
                v.tensor_tensor(c_seq[:, :, :], c_seq[:, :, :], sig_c[:, :, :], ALU.mult).then_inc(ev["c_out"], 1)
                dve.drain().then_inc(rows_used, 1)
                mid_lo(l, 23, 24)
                wait_event(dve, l, "zThi")
                split_lo(xT_lo[:, 4:8, :], xT_hi[:, 4:8, :], 3).then_inc(psum_read[3], 1)
                wait_event(dve, l, "cThi")
                split_lo(xT_lo[:, 0:4, :], xT_hi[:, 0:4, :], 2).then_inc(psum_read[2], 1)
                mid_lo(l, 25, 26)
                for ch, dst in ((YC, sigA), (YC + 1, sigA), (YH, sigB), (YH + 1, sigB)):
                    wait_chunk(dve, l, ch)
                    c = slice((ch % 2) * HALF, (ch % 2 + 1) * HALF)
                    for s in range(S):
                        i = v.tensor_tensor(dst[:, s, c], bank(ch % 2, s), dst[:, s, c], ALU.mult)
                    i.then_inc(psum_read[ch % 2], 1)
                    if ch == YC:
                        mid_lo(l, 27)
                    if ch == YC + 1:
                        mid_lo(l, 28)
                dve.drain()
                for s in range(S):
                    i = v.tensor_tensor(sigA[:, s, :], sigA[:, s, :], sigB[:, s, :], ALU.add)
                i.then_inc(ev["mix"], 1)
                mid_lo(l, 29)
                for s in range(S):
                    wait_event(dve, l, "mixThi", s + 1)
                    c = slice(s * P, (s + 1) * P)
                    split_lo(xT_lo[:, :, c], xT_hi[:, :, c], 2 + s).then_inc(psum_read[2 + s], 1)
                mid_lo(l, 30, 31, 32)
                layer_norm(l, 1, lambda s, i: bank(i, s), lambda s: wait_rows(dve, l, MO + 1, s), None, (2, 3),
                           lambda: mid_lo(l, 33))
                mid_lo(l, 34, 35, 36, 37, 38)

                def row_max(g):
                    wait_done(dve, l, 2 + g, "score")
                    v.tensor_reduce(mx[:, g, :], pair(2 + g).rearrange("p (i m) -> p i m", i=4), AX_X, ALU.max)
                    dve.drain()
                    v.tensor_scalar(mx[:, g, :], mx[:, g, :], -XSCALE, None, ALU.mult).then_inc(ev["mx"], 1)

                row_max(0)
                row_max(1)
                for g in range(2):
                    wait_read(dve, l, 2 + g, "score")
                    v.reciprocal(rden[:, g, :], den[:, g, :])
                    dve.drain()
                    for i in range(4):
                        k = v.tensor_scalar(Px[:, 4 * g + i, :], Px[:, 4 * g + i, :], rden[:, g, i:i + 1], None, ALU.mult)
                    k.then_inc(ev["Pn"], 1)
                mid_lo(l, 39, 40, 41)
                for g in range(2):
                    wait_event(dve, l, "oThi", g + 1)
                    split_lo(xT_lo[:, 4 * g:4 * g + 4, :], xT_hi[:, 4 * g:4 * g + 4, :], 2 + g).then_inc(psum_read[2 + g], 1)
                mid_lo(l, 42, 43)
                lo(l, 0, FFN2_BASE[0])
                layer_norm(l, 2, lambda s, i: bank(i, s), lambda s: wait_rows(dve, l, WO + 1, s), None, (2, 3),
                           lambda: lo(l, 1, FFN2_BASE[1]))
                wait_acc = ffn_dve(l, 1)
                layer_norm(l, 3, lambda s, i: bank(2 + s, i), wait_acc, (2, 3), (0, 1), lambda: None)

        @block.tensor
        def _(pe):
            t_ = nc.tensor

            def turn(dst, src):
                return t_.transpose(dst, src, ident[0:src.shape[0], 0:src.shape[0]])

            def three(dst, hi_, lo_, w, slot, start, stop):
                t_.matmul(dst, hi_, w_hi[slot][:, w], start=start, stop=False)
                t_.matmul(dst, hi_, w_lo[slot][:, w], start=False, stop=False)
                return t_.matmul(dst, lo_, w_hi[slot][:, w], start=False, stop=stop)

            def wait_weights(l, slot, use):
                pe.wait_ge(lo_ready[slot], l * USES[slot] + use + 2)

            def unit(l, slot, use, hi_, lo_, t0, r, first, last):
                wait_weights(l, slot, use)
                for i in range(4):
                    for s in range(S):
                        c = slice(s * P, (s + 1) * P)
                        k = three(bank(r, s), hi_[:, t0 + i, c], lo_[:, t0 + i, c], slice(i * HALF, (i + 1) * HALF),
                                  slot, first and i == 0, last and i == 3)
                k.then_inc(unit_done[slot], 1)

            def units_by_rows(l, units, hi_, lo_, r, ready, between, finished=None):
                for s in range(S):
                    ready(s)
                    c = slice(s * P, (s + 1) * P)
                    for part, (slot, use) in enumerate(units):
                        if s == 0:
                            wait_weights(l, slot, use)
                        for i in range(4):
                            k = three(bank(r, s), hi_[:, 4 * part + i, c], lo_[:, 4 * part + i, c],
                                      slice(i * HALF, (i + 1) * HALF), slot, part + i == 0, part + i == 4)
                        if s == 1:
                            k.then_inc(unit_done[slot], 1)
                        elif part == 0:
                            between()
                        elif finished is not None:
                            k.then_inc(finished, 1)

            def tiles_T(dst, src, n):
                for s in range(S):
                    for i in range(n):
                        k = turn(dst[:, i * SEQ + s * P:i * SEQ + (s + 1) * P], src(s, i))
                return k

            def ln_T(l, n, regs, which=(0, 1)):
                for s in which:
                    wait_room(pe, l, regs[s], f"ln{n}")
                    pe.wait_ge(x_ready, l * 8 + 2 * n + s + 1)
                    for i in range(KT):
                        k = turn(pair(regs[s])[:, i * P:(i + 1) * P], x_res[:, s, i * P:(i + 1) * P])
                    k.then_inc(done[regs[s]], 1)

            pe.wait_ge(const_landed, 16)
            pe.wait_ge(in_landed, 16)
            for i, src in enumerate((x_res, y)):
                if i:
                    pe.wait_ge(mem_landed, 16)
                for s in range(S):
                    for j in range(KT):
                        k = turn(pair(2 * i + s)[:, j * P:(j + 1) * P], src[:, s, j * P:(j + 1) * P])
                    k.then_inc(pro_T, 1)
            pe.wait_ge(pro_lo, 4)

            def ffn_pe(l, f):
                b = F_BASE[f]

                def gate_up(c, part, slot, use):
                    if part == 0:
                        wait_room_step(pe, l, 0, f, c)
                    unit(l, slot, use, xT_hi, xT_lo, 4 * part, 0, part == 0, part == 1)

                def h_T(c):
                    wait_read_step(pe, l, 0, f, c)
                    wait_room_step(pe, l, 1, f, c)
                    tiles_T(bank(1), lambda s, i: hx[:, s, i * P:(i + 1) * P], 2).then_inc(done[1], 1)

                def down_rows(s, slot, hi_, lo_, first, last, tiles=(0, 1)):
                    t = slice(s * P, (s + 1) * P)
                    for i in tiles:
                        for half in range(2):
                            w = slice(i * D + half * HALF, i * D + (half + 1) * HALF)
                            k = three(bank(2 + s, half), hi_[:, i, t], lo_[:, i, t], w, slot,
                                      first and i == 0, last and i == 1)
                    return k

                def down(c, slot, use, first):
                    wait_weights(l, slot, use)
                    wait_read_step(pe, l, 1, f, c)
                    for s in range(S):
                        k = down_rows(s, slot, hT_hi, hT_lo, first, False)
                    k.then_inc(unit_done[slot], 1)

                def ready(s):
                    if f:
                        wait_read(pe, l, 2 + s, "ln2")
                        if s == 0:
                            wait_room_step(pe, l, 0, 1, 0)
                    else:
                        wait_room_step(pe, l, 0, 0, 0) if s == 0 else wait_room_step(pe, l, 1, 0, 0)

                units_by_rows(l, [(0, b[0]), (1, b[1])], xT_hi, xT_lo, 0, ready,
                              (lambda: ln_T(l, 2, (2, 3), (1,))) if f else (lambda: None))

                def step(c, first):
                    gate_up(c, 0, 2, c + (b[2] - 1))
                    h_T(c - 1)
                    gate_up(c, 1, 0, c + b[0])
                    if first:
                        wait_room(pe, l, 2, f"acc{f}")
                        wait_room(pe, l, 3, f"acc{f}")
                    if not (isinstance(c, int) and c == NC - 1):
                        down(c - 1, 1, c + b[1], first)

                step(1, True)
                with pe.Fori(2, NC - 1) as c:
                    step(c, False)
                step(NC - 1, False)
                wait_weights(l, 1, b[1] + NC - 1)
                wait_read_step(pe, l, 1, f, NC - 2)
                down_rows(0, 1, hT_hi, hT_lo, False, False)
                h_T(NC - 1)
                down_rows(1, 1, hT_hi, hT_lo, False, False, (0,))
                wait_weights(l, 2, b[2] + NC - 1)
                wait_read_step(pe, l, 1, f, NC - 1)
                down_rows(0, 2, xT_hi, xT_lo, False, True).then_inc(acc0_done, 1)
                down_rows(1, 1, hT_hi, hT_lo, False, False, (1,)).then_inc(unit_done[1], 1)
                down_rows(1, 2, xT_hi, xT_lo, False, True).then_inc(unit_done[2], 1)

            with pe.Fori(0, L) as l:
                ffn_pe(l, 0)
                ln_T(l, 0, (0, 1), (0,))

                def chunk_part(ch, part, hi_=xT_hi, lo_=xT_lo):
                    if part == 0:
                        wait_room(pe, l, ch % 2, f"chunk{ch}")
                    unit(l, *mid_unit(chunk_units(ch)[part]), hi_, lo_, 4 * part, ch % 2, part == 0, part == 1)

                def chunk(ch, hi_=xT_hi, lo_=xT_lo):
                    chunk_part(ch, 0, hi_, lo_)
                    chunk_part(ch, 1, hi_, lo_)

                def small_T(r, name, src, n=4):
                    wait_room(pe, l, r, name)
                    tiles_T(pair(r), src, n).then_inc(done[r], 1)

                def chunk_by_rows(ch, ready, between, finished=None):
                    units_by_rows(l, [mid_unit(u) for u in chunk_units(ch)], xT_hi, xT_lo, ch % 2, ready, between,
                                  finished)

                chunk_by_rows(0, lambda s: wait_read(pe, l, s, "ln0"), lambda: ln_T(l, 0, (0, 1), (1,)))
                wait_room(pe, l, 2, "taps")
                pe.wait_ge(conv_landed, l * 32 + 32)
                chunk_part(1, 0)
                for g in range(HEADS):
                    k = turn(bank(2)[:, g * 32:(g + 1) * 32], conv_rows[0:32, g * P:(g + 1) * P])
                k.then_inc(done[2], 1)
                chunk_part(1, 1)
                chunk_part(2, 0)
                wait_read(pe, l, 1, "chunk1")
                small_T(2, "conv_h", lambda s, g: h_seq[:, s, g * P:(g + 1) * P])
                chunk_part(2, 1)
                chunk_part(3, 0)
                wait_event(pe, l, "kscaled")
                small_T(3, "k_T", lambda s, g: k_seq[:, s, g * P:(g + 1) * P])
                chunk_part(3, 1)
                chunk_part(4, 0)
                wait_read(pe, l, 1, "chunk3")
                small_T(2, "q_T", lambda s, g: q_seq[:, s, g * P:(g + 1) * P])
                wait_room(pe, l, 3, "kd")
                wait_event(pe, l, "logf_lo")
                pe.wait_ge(sums_ready, 1)
                for s in range(S):
                    tail = sums[:, DECAYS * P:(DECAYS + 1) * P]
                    t_.matmul(bank(3, s), tail, logf_hi[:, s, :], start=True, stop=False)
                    k = t_.matmul(bank(3, s), tail, logf_lo[:, s, :], start=False, stop=True)
                k.then_inc(done[3], 1)
                chunk_part(4, 1)
                chunk(5)
                for r in (2, 3):
                    wait_room(pe, l, r, "state")
                wait_event(pe, l, "kd")
                wait_read(pe, l, 0, "chunk4")
                for c in range(NCH - 1):
                    rows_c = slice(c % 2 * CHUNK, (c % 2 + 1) * CHUNK)
                    for h in range(HEADS):
                        cols = slice(h * P, (h + 1) * P)
                        k = t_.matmul(bank(2 + c // 2, c % 2)[:, cols], kd[rows_c, c // 2, cols],
                                      v_seq[rows_c, c // 2, cols], start=True, stop=True)
                    if c == 1:
                        k.then_inc(done[2], 1)
                for h in range(HEADS):
                    for s in range(S):
                        for f_ in (logf_hi, logf_lo):
                            k = t_.matmul(bank(3, 1)[:, h * NCH + 2 * s:h * NCH + 2 * s + 2],
                                          f_[:, s, h * P:(h + 1) * P], sums[:, (DECAYS + 1) * P:],
                                          start=f_ is logf_hi, stop=f_ is logf_lo)
                k.then_inc(done[3], 1)
                chunk_part(6, 0)

                def decays(h):
                    for s in range(S):
                        wait_room(pe, l, 2 + s, f"e{h}")
                        for part in (logf_hi, logf_lo):
                            f_, first = part[:, s, h * P:(h + 1) * P], part is logf_hi
                            t_.matmul(bank(2 + s, 0), f_, sums[:, 0:HALF], start=first, stop=not first)
                            k = t_.matmul(bank(2 + s, 1)[:, 0:DECAYS * P - HALF], f_, sums[:, HALF:DECAYS * P],
                                          start=first, stop=not first)
                        k.then_inc(done[2 + s], 1)

                def scores(h):
                    wait_event(pe, l, "X", h + 1)
                    for s in range(S):
                        wait_room(pe, l, 2 + s, f"s{h}")
                        t = slice(s * P, (s + 1) * P)
                        for i in range(NL):
                            t_.matmul(pair(2 + s)[:, i * P:(i + 1) * P], E[:, i, t], E[:, i, t], start=True, stop=True)
                        t_.matmul(pair(2 + s)[:, NL * P:MASKS * P], kT[:, h, t], qT[:, h, t], start=True,
                                  stop=True).then_inc(done[2 + s], 1)

                def outputs(h):
                    cols = slice(h * P, (h + 1) * P)
                    for s in range(S):
                        wait_event(pe, l, "ST", 2 * h + s + 1)
                        if h == 0 and s == 0:
                            wait_read(pe, l, 3, "state")
                        o = pair(2 + s)[:, MASKS * P:]
                        for c in (2 * s, 2 * s + 1):
                            at = slice(c % 2 * CHUNK, (c % 2 + 1) * CHUNK)
                            k = t_.matmul(o[at, :], ST[:, s, at], v_seq[:, s, cols], start=True, stop=c == 0)
                            if c:
                                k = t_.matmul(o[at, :], E[:, NL, c * CHUNK:(c + 1) * CHUNK], state[:, c - 1, h, :],
                                              start=False, stop=True)
                        k.then_inc(done[2 + s], 1)

                decays(0)
                chunk_part(6, 1)
                scores(0)
                chunk_part(7, 0)
                outputs(0)
                decays(1)
                chunk_part(7, 1)
                scores(1)
                chunk_part(8, 0)
                outputs(1)
                decays(2)
                chunk_part(8, 1)
                scores(2)
                chunk_part(9, 0)
                outputs(2)
                decays(3)
                chunk_part(9, 1)
                scores(3)
                chunk_part(K_, 0, memT_hi, memT_lo)
                outputs(3)
                chunk_part(K_, 1, memT_hi, memT_lo)
                wait_event(pe, l, "conv")
                wait_room(pe, l, 2, "c_seq")
                for s in range(S):
                    for g in range(HEADS):
                        k = turn(bank(2, s)[:, g * P:(g + 1) * P], acc[:, g, s * P:(s + 1) * P])
                k.then_inc(done[2], 1)
                chunk(K_ + 1, memT_hi, memT_lo)
                wait_event(pe, l, "z")
                small_T(3, "z_T", lambda s, g: o_seq[:, s, g * P:(g + 1) * P])
                wait_event(pe, l, "c_out")
                small_T(2, "c_T", lambda s, g: c_seq[:, s, g * P:(g + 1) * P])
                for ch in range(YC, MO):
                    if ch == YC:
                        wait_read(pe, l, 2, "c_T")
                    if ch == YH:
                        wait_read(pe, l, 3, "z_T")
                    wait_room(pe, l, ch % 2, f"chunk{ch}")
                    unit(l, *mid_unit(chunk_units(ch)[0]), xT_hi, xT_lo, 0 if ch < YH else 4, ch % 2, True, True)
                wait_event(pe, l, "mix")
                for s in range(S):
                    wait_room(pe, l, 2 + s, "mix")
                    for i in range(KT):
                        k = turn(pair(2 + s)[:, i * P:(i + 1) * P], sigA[:, s, i * P:(i + 1) * P])
                    k.then_inc(done[2 + s], 1)
                wait_read(pe, l, 2, "mix")
                wait_read(pe, l, 3, "mix")
                chunk(MO)
                wait_read(pe, l, 0, f"chunk{K_}")
                small_T(2, "K0", lambda s, g: kseq_x[0][:, s, g * P:(g + 1) * P])
                wait_read(pe, l, 1, f"chunk{K_ + 1}")
                small_T(3, "K1", lambda s, g: kseq_x[1][:, s, g * P:(g + 1) * P])

                def room(ch):
                    return lambda s: wait_room(pe, l, ch % 2, f"chunk{ch}") if s == 0 else None

                chunk_by_rows(MO + 1, room(MO + 1), lambda: None, rows0_done)
                ln_T(l, 1, (2, 3), (0,))

                def q_ready(s):
                    wait_read(pe, l, 2 + s, "ln1")
                    room(Q_)(s)

                chunk_by_rows(Q_, q_ready, lambda: ln_T(l, 1, (2, 3), (1,)))
                chunk_part(Q_ + 1, 0)
                wait_read(pe, l, 0, f"chunk{Q_}")
                small_T(2, "Q0", lambda s, g: qseq_x[0][:, s, g * P:(g + 1) * P])
                chunk_part(Q_ + 1, 1)
                wait_read(pe, l, 1, f"chunk{Q_ + 1}")
                small_T(3, "Q1", lambda s, g: qseq_x[1][:, s, g * P:(g + 1) * P])

                def score(g):
                    wait_room(pe, l, 2 + g, "score")
                    for h in (2 * g, 2 * g + 1):
                        for s in range(S):
                            o = bank(2 + g, h % 2)[:, s * N_MEM:(s + 1) * N_MEM]
                            for d in range(2):
                                k = t_.matmul(o, QTx[:, 2 * h + d, s * P:(s + 1) * P], KTx[:, 2 * h + d, :],
                                              start=d == 0, stop=d == 1)
                    k.then_inc(done[2 + g], 1)

                score(0)
                score(1)
                chunk(V_, memT_hi, memT_lo)
                chunk(V_ + 1, memT_hi, memT_lo)
                for g in range(2):
                    wait_room(pe, l, 2 + g, "P_T")
                    wait_event(pe, l, "Pn", g + 1)
                    for h in (2 * g, 2 * g + 1):
                        k = tiles_T(bank(2 + g, h % 2), lambda s, m: Px[:, 2 * h + s, m * P:(m + 1) * P], 2)
                    k.then_inc(done[2 + g], 1)
                wait_read(pe, l, 0, f"chunk{V_}")
                wait_read(pe, l, 1, f"chunk{V_ + 1}")
                for g in range(2):
                    wait_room(pe, l, 2 + g, "pv")
                    for h in (2 * g, 2 * g + 1):
                        for d in range(2):
                            for m in range(2):
                                k = t_.matmul(bank(2 + g, h % 2)[:, d * SEQ:(d + 1) * SEQ],
                                              Vx[:, m, h * XD + d * P:h * XD + (d + 1) * P], PTx[:, h, m, :],
                                              start=m == 0, stop=m == 1)
                    k.then_inc(done[2 + g], 1)
                wait_read(pe, l, 2, "pv")
                wait_read(pe, l, 3, "pv")
                chunk(WO)
                chunk_by_rows(WO + 1, room(WO + 1), lambda: None, rows0_done)
                ln_T(l, 2, (2, 3), (0,))
                ffn_pe(l, 1)
                ln_T(l, 3, (0, 1))


INPUTS = ("x mem ln_g ln_b ffn1_w_gu ffn1_w_down w_in conv_w conv_b conv_ln_g conv_ln_b w_conv_proj hgrn_lb "
          "hgrn_norm_g w_hgrn_proj w_mix_out xa_wq xa_wkv xa_wo ffn2_w_gu ffn2_w_down").split()


def kernel(**inputs):
    import concourse.bacc as bacc
    from concourse.bass_utils import run_bass_kernel_spmd

    nc = bacc.Bacc("TRN2", target_bir_lowering=False, num_devices=1)
    arrays, args = {}, []
    for name in INPUTS + ["consts"]:
        a = np.ascontiguousarray(layout_constants() if name == "consts" else inputs[name])
        arrays["in_" + name] = a
        args.append(nc.dram_tensor("in_" + name, a.shape, mybir.dt.from_np(a.dtype), kind="ExternalInput").ap())
    shape = tuple(inputs["x"].shape)
    out = nc.dram_tensor("out_0", shape, F32, kind="ExternalOutput").ap()
    build(nc, *args, out)
    r = run_bass_kernel_spmd(nc, [arrays], core_ids=[0])
    return r.results[0]["out_0"]
```

```python
from contextlib import ExitStack
import math

import numpy as np

import concourse.bass as bass
from concourse import mybir
from concourse.alu_op_type import AluOpType as ALU

ACT = mybir.ActivationFunctionType
F32 = mybir.dt.float32
FR = mybir.dt.float32r
BF16 = mybir.dt.bfloat16
AX_X = mybir.AxisListType.X

P = 128
HALF = 512
RING = 3
CHUNK = 64
CONV_K = 31
LN_EPS = 1e-5
RMS_EPS = 1e-6
KEY_MAX = 1.0 - 1e-6
LEVELS = (32, 16, 8, 4, 2, 1)
NL = len(LEVELS)
DECAYS = NL + 1
MASKS = NL + 1


def layout_constants():
    t = np.arange(P)
    same_chunk = (t[:, None] // CHUNK) == (t[None, :] // CHUNK)
    sums = np.zeros((P, DECAYS, P), np.float32)
    masks = np.zeros((P, MASKS, P), np.float32)
    for i, m in enumerate(LEVELS):
        mid = t // (2 * m) * (2 * m) + m
        late = t >= mid
        src = t[:, None]
        sums[:, i, :] = np.where(late[None, :], (src >= mid[None, :]) & (src <= t[None, :]),
                                 (src > t[None, :]) & (src < mid[None, :]))
        same = (t[:, None] // (2 * m)) == (t[None, :] // (2 * m))
        masks[:, i, :] = same & ~late[:, None] & late[None, :]
    sums[:, NL, :] = same_chunk & (t[:, None] <= t[None, :])
    masks[:, NL, :] = np.eye(P)
    masks = np.concatenate([masks[c:c + CHUNK, :, c:c + CHUNK] for c in range(0, P, CHUNK)])
    tail = (same_chunk & (t[:, None] > t[None, :])).astype(np.float32)
    chunk_sum = ((t[:, None] // CHUNK) == np.arange(P // CHUNK)[None, :]).astype(np.float32)
    return np.concatenate([sums.reshape(P, -1), tail, chunk_sum, masks.reshape(P, -1),
                           np.eye(P, dtype=np.float32)], axis=1)


class Uses:

    def __init__(self, names):
        self.names = names
        self.n = len(names)

    def __call__(self, name):
        return self.names.index(name)


def build(nc, x, mem, ln_g, ln_b, ffn1_w_gu, ffn1_w_down, w_in, conv_w, conv_b, conv_ln_g, conv_ln_b,
          w_conv_proj, hgrn_lb, hgrn_norm_g, w_hgrn_proj, w_mix_out, xa_wq, xa_wkv, xa_wo,
          ffn2_w_gu, ffn2_w_down, consts, out):
    _, SEQ, D = x.shape
    N_MEM = mem.shape[1]
    L = ln_g.shape[0]
    D_FF = ffn1_w_down.shape[1]
    W = conv_w.shape[2]
    ALPHA = float((2 * L) ** 0.25)
    S = SEQ // P
    KT = D // P
    HEADS = W // P
    XH = 4
    XD = D // XH
    XSCALE = XD ** -0.5
    QSCALE = P ** -0.5
    CF = 256
    NC = D_FF // CF
    NCH = SEQ // CHUNK
    assert S == 2 and KT == 8 and NC * CF == D_FF and N_MEM == SEQ and XD == 2 * P and W == HALF and L == 2

    MID = 44
    FFN_USES = [NC, NC, NC]
    MID_BASE = list(FFN_USES)
    SKIP = 20
    mid_slots = [(u + (u >= SKIP)) % RING for u in range(MID)]
    FFN2_BASE = [MID_BASE[j] + mid_slots.count(j) for j in range(RING)]
    USES = [FFN2_BASE[j] + FFN_USES[j] for j in range(RING)]
    F_BASE = ([0] * RING, FFN2_BASE)

    def mid_unit(u):
        j = mid_slots[u]
        return j, MID_BASE[j] + mid_slots[:u].count(j)

    ffn = [f"gu{f}_{c}" for f in (0, 1) for c in range(NC)]
    K_, YH, YC, V0, MO, Q_, V1, WO = 10, 12, 14, 16, 17, 19, 21, 22
    R0 = Uses(["x"] + ffn[:NC] + ["ln0"] + [f"chunk{c}" for c in range(0, 24, 2)] + ffn[NC:])
    R1 = Uses(["x"] + ffn[:NC] + ["ln0"] + [f"chunk{c}" for c in range(1, 24, 2)] + ffn[NC:])

    def chunk_units(ch):
        first = 2 * ch if ch < YH else 2 * YH + ch - YH if ch < V0 else 2 * ch - 4
        return (first,) if YH <= ch < V0 else (first, first + 1)

    heads = [f"{k}{h}" for h in range(HEADS) for k in "es"]
    R2 = Uses(["acc0", "taps", "conv_h", "q_T", "state"] + heads
              + ["c_seq", "c_T", "mix", "K0", "ln1", "Q0", "score", "P_T", "pv", "ln2", "acc1"])
    R3 = Uses(["acc0", "k_T", "kd", "state"] + heads
              + ["z_T", "mix", "K1", "ln1", "Q1", "score", "P_T", "pv", "ln2", "acc1"])
    R = [R0, R1, R2, R3]
    D0 = Uses(["x", "ln0"])
    D1 = Uses(["x"] + ffn[:NC] + ["ln0"] + ffn[NC:])
    D2, D3 = (Uses([k for n in r.names if not n.startswith("acc")
                    for k in ([n, "o" + n[1:]] if n[0] == "s" and n[1:].isdigit() else [n])]) for r in (R2, R3))
    DONE = [D0, D1, D2, D3]

    with ExitStack() as ctx:
        def sb(name, shape, dt=F32):
            return ctx.enter_context(nc.sbuf_tensor(name, shape, dt))

        def sem(name):
            return ctx.enter_context(nc.semaphore(name))

        UNIT = 4 * HALF
        raw = [sb(f"raw{j}", [P, UNIT]) for j in range(RING)]
        w_hi = [sb(f"w_hi{j}", [P, UNIT], FR) for j in range(RING)]
        w_lo = [sb(f"w_lo{j}", [P, UNIT], FR) for j in range(RING)]
        xT_hi = sb("xT_hi", [P, KT, SEQ], FR)
        xT_lo = sb("xT_lo", [P, KT, SEQ], FR)
        memT_hi = sb("memT_hi", [P, KT, SEQ], FR)
        memT_lo = sb("memT_lo", [P, KT, SEQ], FR)
        hT_hi = sb("hT_hi", [P, 2, SEQ], FR)
        hT_lo = sb("hT_lo", [P, 2, SEQ], FR)
        x_res = sb("x_res", [P, S, D])
        y = sb("y", [P, S, D])
        sums = sb("sums", [P, (DECAYS + 1) * P + 2], FR)
        logf_hi = sb("logf_hi", [P, S, W], FR)
        logf_lo = sb("logf_lo", [P, S, W], FR)
        ident = sb("ident", [P, P])
        masks = sb("masks", [P, MASKS * CHUNK], BF16)
        rows = sb("rows", [P, 4, HALF])
        rows_ln = rows[:, :, :].rearrange("p (a b) n -> p a (b n)", a=2)
        taps = sb("taps", [P, HEADS, 32])
        stats = sb("stats", [P, S, 12])
        mv = sb("mv", [P, S, 2])
        var = sb("var", [P, S])
        rstd = sb("rstd", [P, S])
        mhalf = sb("mhalf", [P, 8])
        eb = sb("eb", [P, HEADS, NCH])
        sq = sb("sq", [P, S, HEADS])
        squares = sb("squares", [P, S, P])
        rrms = sb("rrms", [P, S, HEADS])
        mx = sb("mx", [P, 2, 4])
        den = sb("den", [P, 2, 4])
        rden = sb("rden", [P, 2, 4])

        ARENA = 15104
        arena = sb("arena", [P, ARENA])
        top = [0]

        def cut(n):
            top[0] += n
            assert top[0] <= ARENA
            return arena[:, top[0] - n:top[0]]

        def by(ap, a):
            return ap.rearrange("p (a n) -> p a n", a=a)

        sigA = by(cut(S * D), S)
        sigB = by(cut(S * D), S)
        E = by(cut(DECAYS * SEQ), DECAYS)
        kT = by(cut(HEADS * SEQ), HEADS)
        qT = by(cut(HEADS * SEQ), HEADS)
        v_seq = by(cut(S * W), S)
        kd = by(cut(S * W), S)
        logf = kd
        og = by(cut(S * W), S)
        PAD = CONV_K - 1
        hc = by(cut(HEADS * (SEQ + PAD)), HEADS)
        acc = by(cut(HEADS * SEQ), HEADS)
        conv_rows = arena[:, top[0]:top[0] + W]
        state = cut((NCH - 1) * W).rearrange("p (c h v) -> p c h v", c=NCH - 1, h=HEADS)
        ST = by(cut(S * CHUNK), S)
        k_seq = y[:, 0, :].rearrange("p (s n) -> p s n", s=S)
        q_seq = y[:, 1, :].rearrange("p (s n) -> p s n", s=S)
        sig_b, h_seq, sig_c = og, by(acc.rearrange("p h t -> p (h t)"), S), by(acc.rearrange("p h t -> p (h t)"), S)
        prod, c_seq, o_seq = y[:, 0, 0:MASKS * CHUNK], k_seq, q_seq
        top[0] = 0
        KTx = by(cut(KT * N_MEM), KT)
        QTx = by(cut(KT * SEQ), KT)
        kseq_x = [by(cut(S * HALF), S) for _ in range(2)]
        Vx = by(cut(S * D), S)
        qseq_x = [by(cut(S * HALF), S) for _ in range(2)]
        Px = by(cut(XH * S * N_MEM), XH * S)
        PTx = cut(XH * 2 * SEQ).rearrange("p (h m t) -> p h m t", h=XH, m=2)
        top[0] = 0
        sg = by(cut(S * CF), S)
        hx = by(cut(S * CF), S)

        lb_in = by(E[:, 0, 0:L * W // P], L)
        lb_sum = E[:, 1, 0:W // P]
        key = by(kT[:, 0, 0:L * W // P], L)

        ps = ctx.enter_context(nc.psum_tensor("ps", [P, 8, HALF], F32))

        def bank(r, i=0):
            return ps[:, 2 * r + i, :]

        def pair(r):
            return ps[:, 2 * r:2 * r + 2, :].rearrange("p b n -> p (b n)")

        scratch = nc.dram_tensor("key_scale", [L, W], F32, kind="Internal").ap()

        raw_landed = [sem(f"raw_landed{j}") for j in range(RING)]
        hi_ready = [sem(f"hi_ready{j}") for j in range(RING)]
        lo_ready = [sem(f"lo_ready{j}") for j in range(RING)]
        unit_done = [sem(f"unit_done{j}") for j in range(RING)]
        psum_read = [sem(f"psum_read{r}") for r in range(4)]
        done = [sem(f"psum_done{r}") for r in range(4)]
        acc0_done = sem("acc0_done")
        rows0_done = sem("rows0_done")
        x_landed = sem("x_landed")
        slot_free = sem("slot_free")
        pe_steps = sem("pe_steps")
        const_landed = sem("const_landed")
        memT_done = sem("memT_done")
        memThi_ready = sem("memThi_ready")
        rest_landed = sem("rest_landed")
        lb_landed = sem("lb_landed")
        sums_ready = sem("sums_ready")
        masks_ready = sem("masks_ready")
        conv_landed = sem("conv_landed")
        mem_landed = sem("mem_landed")
        mhalf_ready = sem("mhalf_ready")
        lb_centered = sem("lb_centered")
        lb_exp = sem("lb_exp")
        key_ready = sem("key_ready")
        scratch_stored = sem("scratch_stored")
        rows_landed = sem("rows_landed")
        rows_used = sem("rows_used")
        sig_ready = sem("sig_ready")
        hThi_ready = sem("hThi_ready")
        var_ready = sem("var_ready")
        rstd_ready = sem("rstd_ready")
        x_ready = sem("x_ready")
        xThi_ready = sem("xThi_ready")
        names = ["kscaled", "logf_hi", "logf_lo", "sigq", "kd", "sigo", "eb", "X", "ST", "sq", "ms", "rrms", "z", "zThi", "cvar",
                 "crstd", "c_norm", "sigc", "c_out", "cThi", "conv", "mix", "mixThi", "mx", "Pn", "oThi"]
        ev = {n: sem(n + "_ready") for n in names}
        out_stored = sem("out_stored")

        X0 = S
        PER = dict.fromkeys(names, 1)
        PER.update(X=HEADS, ST=2 * HEADS, mix=S, mixThi=S, mx=2, Pn=2, oThi=2)

        def wait_event(eng, l, name, k=1):
            eng.wait_ge(ev[name], l * PER[name] + k)

        def wait_unit_done(eng, l, slot, use):
            eng.wait_ge(unit_done[slot], l * USES[slot] + use + 2)

        def wait_chunk(eng, l, ch):
            wait_unit_done(eng, l, *mid_unit(chunk_units(ch)[-1]))

        def wait_rows(eng, l, ch, s):
            if s == 0:
                eng.wait_ge(rows0_done, l * 2 + (1 if ch < WO else 2))
            else:
                wait_chunk(eng, l, ch)

        def wait_done(eng, l, r, name):
            eng.wait_ge(done[r], l * DONE[r].n + DONE[r](name) + 1)

        def wait_done_step(eng, l, r, f, c):
            eng.wait_ge(done[r], l * DONE[r].n + DONE[r](f"gu{f}_0") + c + 1)

        def wait_room(eng, l, r, name):
            eng.wait_ge(psum_read[r], l * R[r].n + R[r](name) + 1)

        def wait_read(eng, l, r, name):
            eng.wait_ge(psum_read[r], l * R[r].n + R[r](name) + 2)

        def wait_room_step(eng, l, r, f, c):
            eng.wait_ge(psum_read[r], c + (l * R[r].n + R[r](f"gu{f}_0") + 1))

        def wait_read_step(eng, l, r, f, c):
            eng.wait_ge(psum_read[r], c + (l * R[r].n + R[r](f"gu{f}_0") + 2))

        block = ctx.enter_context(nc.Block())

        @block.sync
        def _(sp):
            sp.dma_start(ident[:, :], consts[:, consts.shape[1] - P:]).then_inc(const_landed, 16)
            sp.dma_start(y[:, :, :], mem[0].rearrange("(s p) d -> p s d", p=P)).then_inc(mem_landed, 16)
            for s in range(S):
                sp.dma_start(x_res[:, s, :], x[0, s * P:(s + 1) * P, :]).then_inc(x_landed, 16)

            def load(l, slot, use, *parts):
                sp.wait_ge(lo_ready[slot], l * USES[slot] + use + 1)
                sp.sem_inc(slot_free, 1)
                for dst, src in parts:
                    sp.dma_start(dst, src).then_inc(raw_landed[slot], 16)

            def load_gu(l, f, w, c, part, slot, use):
                src = w.rearrange("l (t p) (g n) -> l g p t n", p=P, g=2)
                dst = raw[slot][:, :].rearrange("p (t g n) -> p g t n", t=4, g=2)
                load(l, slot, use, *[(dst[:, g], src[l, g, :, 4 * part:4 * part + 4, bass.ds(c * CF, CF)])
                                     for g in range(2)])

            def load_down(l, f, w, c, slot, use):
                src = w.rearrange("l (t p) n -> l p t n", p=P)
                load(l, slot, use, *[(raw[slot][:, i * D:(i + 1) * D], src[l, :, bass.ds(c * 2 + i, 1), :])
                                     for i in range(2)])

            def load_ffn(l, f, w_gu, w_down):
                b = F_BASE[f]
                load_gu(l, f, w_gu, 0, 0, 0, b[0])
                load_gu(l, f, w_gu, 0, 1, 1, b[1])
                with sp.Fori(1, NC) as c:
                    load_gu(l, f, w_gu, c, 0, 2, c + (b[2] - 1))
                    load_gu(l, f, w_gu, c, 1, 0, c + b[0])
                    load_down(l, f, w_down, c - 1, 1, c + b[1])
                load_down(l, f, w_down, NC - 1, 2, b[2] + NC - 1)

            def load_cols(l, u, w, rows0, cols0):
                src = w.rearrange("l (t p) n -> l p t n", p=P)
                t0 = rows0 // P
                slot, use = mid_unit(u)
                dst = raw[slot][:, :].rearrange("p (t n) -> p t n", t=4)
                load(l, slot, use, *[(dst[:, t:t + 2], src[l, :, t0 + t:t0 + t + 2, cols0:cols0 + HALF])
                                     for t in (0, 2)])

            with sp.Fori(0, L) as l:
                load_ffn(l, 0, ffn1_w_gu, ffn1_w_down)
                u = 0
                order = [1, 0, 3, 2, 4, 5, 6, 7, 8, 9]
                for col in order:
                    for part in range(2):
                        load_cols(l, u, w_in, part * HALF, col * HALF)
                        u += 1
                for w, first, n in ((xa_wkv, 0, 2), (w_hgrn_proj, 0, 2), (w_conv_proj, 0, 2), (xa_wkv, D, 1),
                                    (w_mix_out, 0, 2), (xa_wq, 0, 2), (xa_wkv, D + HALF, 1), (xa_wo, 0, 2)):
                    for i in range(n):
                        for part in range(w.shape[1] // HALF):
                            load_cols(l, u, w, part * HALF, first + i * HALF)
                            u += 1
                assert u == MID
                load_ffn(l, 1, ffn2_w_gu, ffn2_w_down)
            for s in range(S):
                sp.wait_ge(x_ready, X0 + 8 * (L - 1) + 6 + s + 1)
                sp.dma_start(out[0, s * P:(s + 1) * P, :], x_res[:, s, :]).then_inc(out_stored, 16)
            sp.wait_ge(out_stored, 16 * S)

        @block.gpsimd
        def _(pool):
            cn = (DECAYS + 1) * P + 2
            consts_in = arena[:, S * D:S * D + cn + MASKS * CHUNK]
            pool.dma_start(consts_in, consts[:, 0:cn + MASKS * CHUNK]).then_inc(rest_landed, 16)
            pool.memset(mhalf[:, :], -0.5).then_inc(mhalf_ready, 1)
            pool.wait_ge(key_ready, 1)
            pool.dma_start(scratch.rearrange("l (p n) -> p l n", p=P), key).then_inc(scratch_stored, 16)
            pool.wait_ge(scratch_stored, 16)
            pool.wait_ge(mhalf_ready, 1)
            pool.wait_ge(rest_landed, 16)
            pool.tensor_copy(masks[:, :], consts_in[:, cn:]).then_inc(masks_ready, 1)
            pool.tensor_copy(sums[:, :], consts_in[:, 0:cn]).then_inc(sums_ready, 1)

            def load_ln(l, n):
                pool.wait_ge(rows_used, l * 5 + n + 1)
                k = n if n == 0 else n - 1
                pool.dma_start(rows_ln[:, 0, :], ln_g[l, k:k + 1, :].broadcast_to([P, D])).then_inc(rows_landed, 16)
                pool.dma_start(rows_ln[:, 1, :], ln_b[l, k:k + 1, :].broadcast_to([P, D])).then_inc(rows_landed, 16)

            def power(l, k, per, src_sem, out_sem, dst, src):
                pool.wait_ge(src_sem, l * per + k)
                pool.tensor_tensor(dst, src, mhalf[:, 0:src.shape[1]], ALU.pow).then_inc(out_sem, 1)

            def ln_powers(l, n):
                for s in range(S):
                    power(l, 2 * n + s + 1, 8, var_ready, rstd_ready, rstd[:, s:s + 1], var[:, s:s + 1])

            with pool.Fori(0, L) as l:
                load_ln(l, 0)
                ln_powers(l, 0)
                pool.wait_ge(rows_used, l * 5 + 2)
                for i, a in enumerate((conv_ln_g, conv_ln_b, hgrn_norm_g, scratch)):
                    pool.dma_start(rows[:, i, :], a[bass.ds(l, 1), :].broadcast_to([P, W])).then_inc(rows_landed, 16)
                pool.dma_start(conv_rows[0:CONV_K, :], conv_w[l]).then_inc(conv_landed, 16)
                pool.dma_start(conv_rows[CONV_K:32, :], conv_b[bass.ds(l, 1), :]).then_inc(conv_landed, 16)
                pool.wait_ge(ev["ms"], l + 1)
                pool.tensor_tensor(rrms[:, :, :], sq[:, :, :], mhalf[:, 0:8].rearrange("p (a b) -> p a b", a=2),
                                   ALU.pow).then_inc(ev["rrms"], 1)
                pool.wait_ge(ev["cvar"], l + 1)
                pool.tensor_tensor(rstd[:, :], var[:, :], mhalf[:, 0:2], ALU.pow).then_inc(ev["crstd"], 1)
                for n in (1, 2, 3):
                    load_ln(l, n + 1)
                    ln_powers(l, n)

        @block.scalar
        def _(act):
            sc = nc.scalar

            def hi(l, slot, use):
                act.wait_ge(raw_landed[slot], (l * USES[slot] + use + 1) * 32)
                act.wait_ge(unit_done[slot], l * USES[slot] + use + 1)
                sc.copy(w_hi[slot][:, :], raw[slot][:, :]).then_inc(hi_ready[slot], 1)

            def mid_hi(l, *us):
                for u in us:
                    hi(l, *mid_unit(u))

            def split_hi(dst, r, width=2 * HALF):
                return sc.copy(dst, pair(r)[:, 0:width].rearrange("p (a n) -> p a n", a=dst.shape[1]))

            def ln_T(l, n, regs):
                for s in range(S):
                    wait_done(act, l, regs[s], f"ln{n}")
                    split_hi(xT_hi[:, :, s * P:(s + 1) * P], regs[s]).then_inc(xThi_ready, 1)

            act.dma_start(lb_in, hgrn_lb.rearrange("l (p n) -> p l n", p=P)).then_inc(lb_landed, 16)
            act.wait_ge(lb_centered, 1)
            sc.activation(lb_in, lb_in, ACT.Exp).then_inc(lb_exp, 1)
            for s in range(S):
                act.wait_ge(memT_done, s + 1)
                split_hi(memT_hi[:, :, s * P:(s + 1) * P], 2 + s).then_inc(memThi_ready, 1)

            def ffn_act(l, f):
                b = F_BASE[f]

                def gate(c):
                    wait_unit_done(act, l, *((1, b[1]) if isinstance(c, int) and c == 0 else (0, c + b[0])))
                    for s in range(S):
                        sc.activation(sg[:, s, :], bank(0, s)[:, 0:CF], ACT.Sigmoid).then_inc(sig_ready, 1)

                def hT(c, dst=hT_hi, last=False):
                    wait_done_step(act, l, 1, f, c)
                    if not last and not (isinstance(c, int) and c == 0):
                        wait_unit_done(act, l, 1, c + b[1])
                    sc.copy(dst[:, 0:2, :], bank(1)[:, :].rearrange("p (a n) -> p a n", a=2)).then_inc(hThi_ready, 1)

                if f == 0:
                    hi(l, 0, b[0])
                    wait_done(act, l, 0, "x")
                    split_hi(xT_hi[:, :, 0:P], 0).then_inc(xThi_ready, 1)
                    hi(l, 1, b[1])
                    wait_done(act, l, 1, "x")
                    split_hi(xT_hi[:, :, P:2 * P], 1).then_inc(xThi_ready, 1)
                hi(l, 2, b[2])
                gate(0)
                hi(l, 0, b[0] + 1)

                def step(c, last):
                    hi(l, 1, c + b[1])
                    hT(c - 1)
                    hi(l, 2, c + b[2])
                    wait_read_step(act, l, 0, f, c - 1)
                    gate(c)
                    if not (last and f):
                        hi(l, 0, c + (b[0] + 1))

                step(1, False)
                with act.Fori(2, NC - 1) as c:
                    step(c, False)
                step(NC - 1, True)
                hT(NC - 1, xT_hi, True)

            with act.Fori(0, L) as l:
                ffn_act(l, 0)
                mid_hi(l, 1)
                ln_T(l, 0, (0, 1))
                mid_hi(l, 2, 3)
                wait_chunk(act, l, 0)
                for s in range(S):
                    i = sc.activation(sig_b[:, s, :], bank(0, s), ACT.Sigmoid)
                i.then_inc(psum_read[0], 1)
                mid_hi(l, 4, 5, 6)
                wait_done(act, l, 2, "taps")
                sc.copy(taps[:, :, :], bank(2)[:, 0:HEADS * 32].rearrange("p (h t) -> p h t", h=HEADS))\
                    .then_inc(psum_read[2], 1)
                wait_done(act, l, 2, "conv_h")
                sc.copy(hc[:, :, PAD:], pair(2).rearrange("p (a n) -> p a n", a=HEADS)).then_inc(psum_read[2], 1)
                mid_hi(l, 7)
                wait_chunk(act, l, 2)
                for s in range(S):
                    i = sc.activation(k_seq[:, s, :], bank(0, s), ACT.Sigmoid, scale=-1.0)
                i.then_inc(psum_read[0], 1)
                mid_hi(l, 8, 9)
                wait_chunk(act, l, 3)
                for s in range(S):
                    i = sc.activation(q_seq[:, s, :], bank(1, s), ACT.Sigmoid)
                i.then_inc(ev["sigq"], 1)
                wait_event(act, l, "kscaled")
                sc.activation(logf[:, :, :], logf[:, :, :], ACT.Ln, scale=-1.0, bias=1.0)
                act.drain()
                sc.copy(logf_hi[:, :, :], logf[:, :, :]).then_inc(ev["logf_hi"], 1)
                mid_hi(l, 10)
                wait_done(act, l, 3, "k_T")
                sc.copy(kT[:, :, :], pair(3).rearrange("p (a n) -> p a n", a=HEADS)).then_inc(psum_read[3], 1)
                mid_hi(l, 11)
                wait_chunk(act, l, 4)
                for s in range(S):
                    i = sc.copy(v_seq[:, s, :], bank(0, s))
                i.then_inc(psum_read[0], 1)
                wait_done(act, l, 2, "q_T")
                sc.copy(qT[:, :, :], pair(2).rearrange("p (a n) -> p a n", a=HEADS)).then_inc(psum_read[2], 1)
                wait_done(act, l, 3, "kd")
                sc.activation(kd[:, :, :], pair(3).rearrange("p (a n) -> p a n", a=S), ACT.Exp).then_inc(psum_read[3], 1)
                mid_hi(l, 12, 13)
                wait_done(act, l, 3, "state")
                sc.activation(eb[:, :, :], bank(3, 1)[:, 0:HEADS * NCH].rearrange("p (h c) -> p h c", h=HEADS),
                              ACT.Exp).then_inc(ev["eb"], 1)

                def decays(h):
                    if h:
                        wait_done(act, l, 3, f"s{h - 1}")
                    for s in range(S):
                        wait_done(act, l, 2 + s, f"e{h}")
                        sc.activation(E[:, :, s * P:(s + 1) * P],
                                      pair(2 + s)[:, 0:DECAYS * P].rearrange("p (a n) -> p a n", a=DECAYS),
                                      ACT.Exp).then_inc(psum_read[2 + s], 1)

                def gate_chunk(ch, dst):
                    wait_chunk(act, l, ch)
                    for s in range(S):
                        i = sc.activation(dst[:, s, :], bank(ch % 2, s), ACT.Sigmoid)
                    return i

                def copy_chunk(ch, dst):
                    wait_chunk(act, l, ch)
                    for s in range(S):
                        i = sc.copy(dst[:, s, :], bank(ch % 2, s))
                    i.then_inc(psum_read[ch % 2], 1)

                def out_rows(h):
                    for s in range(S):
                        wait_done(act, l, 2 + s, f"o{h}")
                        o = bank(2 + s, 1)[:, 0:P]
                        sc.activation(squares[:, s, :], o, ACT.Square, accum_out=sq[:, s, h:h + 1])
                        sc.copy(o_seq[:, s, h * P:(h + 1) * P], o).then_inc(psum_read[2 + s], 1)
                    return act.drain()

                decays(0)
                gate_chunk(5, og).then_inc(ev["sigo"], 1)
                mid_hi(l, 14, 15)
                gate_chunk(6, sigA[:, :, 0:HALF]).then_inc(psum_read[0], 1)
                out_rows(0)
                decays(1)
                mid_hi(l, 16)
                gate_chunk(7, sigA[:, :, HALF:D]).then_inc(psum_read[1], 1)
                mid_hi(l, 17)
                out_rows(1)
                decays(2)
                mid_hi(l, 18)
                gate_chunk(8, sigB[:, :, 0:HALF]).then_inc(psum_read[0], 1)
                mid_hi(l, 19)
                out_rows(2)
                decays(3)
                mid_hi(l, 20)
                gate_chunk(9, sigB[:, :, HALF:D]).then_inc(psum_read[1], 1)
                mid_hi(l, 21)
                out_rows(3).then_inc(ev["sq"], 1)
                mid_hi(l, 22)
                copy_chunk(K_, kseq_x[0])
                mid_hi(l, 23, 24)
                wait_done(act, l, 3, "z_T")
                split_hi(xT_hi[:, 4:8, :], 3).then_inc(ev["zThi"], 1)
                mid_hi(l, 25)
                copy_chunk(K_ + 1, kseq_x[1])
                wait_event(act, l, "c_norm")
                sc.activation(sig_c[:, :, :], c_seq[:, :, :], ACT.Sigmoid).then_inc(ev["sigc"], 1)
                mid_hi(l, 26, 27)
                wait_done(act, l, 2, "c_T")
                split_hi(xT_hi[:, 0:4, :], 2).then_inc(ev["cThi"], 1)
                mid_hi(l, 28)
                mid_hi(l, 29, 30)
                wait_chunk(act, l, YC + 1)
                for s in range(S):
                    wait_done(act, l, 2 + s, "mix")
                    split_hi(xT_hi[:, :, s * P:(s + 1) * P], 2 + s).then_inc(ev["mixThi"], 1)
                mid_hi(l, 31)
                copy_chunk(V0, Vx[:, :, 0:HALF])
                mid_hi(l, 32, 33)

                def copy_T(r, use, dst):
                    wait_done(act, l, r, use)
                    sc.copy(dst, pair(r).rearrange("p (a n) -> p a n", a=4)).then_inc(psum_read[r], 1)

                copy_T(2, "K0", KTx[:, 0:4, :])
                copy_T(3, "K1", KTx[:, 4:8, :])
                mid_hi(l, 34, 35)
                ln_T(l, 1, (2, 3))
                mid_hi(l, 36)
                copy_chunk(Q_, qseq_x[0])
                mid_hi(l, 37, 38)
                copy_T(2, "Q0", QTx[:, 0:4, :])
                mid_hi(l, 39)
                copy_chunk(Q_ + 1, qseq_x[1])
                mid_hi(l, 40)
                copy_T(3, "Q1", QTx[:, 4:8, :])

                def softmax(g):
                    wait_event(act, l, "mx", g + 1)
                    for i in range(4):
                        k = sc.activation(Px[:, 4 * g + i, :], pair(2 + g)[:, i * N_MEM:(i + 1) * N_MEM], ACT.Exp,
                                          bias=mx[:, g, i:i + 1], scale=XSCALE, accum_out=den[:, g, i:i + 1])
                    k.then_inc(psum_read[2 + g], 1)

                def copy_P_T(g):
                    wait_done(act, l, 2 + g, "P_T")
                    sc.copy(PTx[:, 2 * g:2 * g + 2, :, :].rearrange("p h m t -> p (h m t)"), pair(2 + g))\
                        .then_inc(psum_read[2 + g], 1)

                softmax(0)
                mid_hi(l, 41)
                copy_P_T(0)
                softmax(1)
                copy_chunk(V1, Vx[:, :, HALF:D])
                copy_P_T(1)
                mid_hi(l, 42)
                for g in range(2):
                    wait_done(act, l, 2 + g, "pv")
                    split_hi(xT_hi[:, 4 * g:4 * g + 4, :], 2 + g).then_inc(ev["oThi"], 1)
                mid_hi(l, 43)
                hi(l, 0, FFN2_BASE[0])
                hi(l, 1, FFN2_BASE[1])
                ln_T(l, 2, (2, 3))
                ffn_act(l, 1)

        @block.vector
        def _(dve):
            v = nc.vector

            def lo(l, slot, use):
                dve.wait_ge(hi_ready[slot], l * USES[slot] + use + 1)
                v.tensor_tensor(w_lo[slot][:, :], raw[slot][:, :], w_hi[slot][:, :], ALU.subtract).then_inc(lo_ready[slot], 1)

            def mid_lo(l, *us):
                for u in us:
                    lo(l, *mid_unit(u))

            def split_lo(dst, hi, r):
                n = dst.shape[1]
                return v.tensor_tensor(dst, pair(r).rearrange("p (a n) -> p a n", a=n), hi, ALU.subtract)

            for s_ in lo_ready + unit_done + psum_read[0:2] + [rows_used]:
                dve.sem_inc(s_, 1)
            dve.wait_ge(lb_landed, 16)
            v.tensor_tensor(lb_sum, lb_in[:, 0, :], lb_in[:, 1, :], ALU.max)
            dve.drain()
            for l in range(L):
                v.tensor_tensor(lb_in[:, l, :], lb_in[:, l, :], lb_sum, ALU.subtract)
            dve.drain()
            v.memset(key[:, 0, :], 1.0).then_inc(lb_centered, 1)
            dve.wait_ge(lb_exp, 1)
            v.tensor_tensor(lb_sum, lb_in[:, 0, :], lb_in[:, 1, :], ALU.add)
            dve.drain()
            v.reciprocal(lb_sum, lb_sum)
            dve.drain()
            v.tensor_tensor(key[:, 1, :], lb_in[:, 1, :], lb_sum, ALU.mult)
            dve.drain()
            v.tensor_scalar(key[:, 1, :], key[:, 1, :], -1.0, 1.0, ALU.mult, ALU.add).then_inc(key_ready, 1)
            dve.wait_ge(x_landed, 16 * S)
            dve.sem_inc(x_ready, S)
            for s in range(S):
                dve.wait_ge(memThi_ready, s + 1)
                c = slice(s * P, (s + 1) * P)
                split_lo(memT_lo[:, :, c], memT_hi[:, :, c], 2 + s).then_inc(psum_read[2 + s], 1)

            def layer_norm(l, n, src, wait_src, free_regs, regs, between, chunk0=None):

                def moments(s):
                    wait_src(s)
                    for i in range(2):
                        c = slice(i * HALF, (i + 1) * HALF)
                        k = v.scalar_tensor_tensor(y[:, s, c], x_res[:, s, c], ALPHA, src(s, i), ALU.mult, ALU.add)
                        if free_regs is not None:
                            if i == 1:
                                k.then_inc(psum_read[free_regs[s]], 1)
                        elif s == 1:
                            k.then_inc(psum_read[(chunk0 + i) % 2], 1)
                    dve.drain()
                    for i in range(2):
                        v.bn_stats(stats[:, s, 6 * i:6 * i + 6], y[:, s, i * HALF:(i + 1) * HALF])
                        if s == 1 and i == 0 and regs is not None:
                            split(0)
                    dve.drain()
                    v.bn_aggr(mv[:, s, :], stats[:, s, :])
                    dve.drain()
                    v.tensor_scalar(var[:, s:s + 1], mv[:, s, 1:2], LN_EPS, None, ALU.add).then_inc(var_ready, 1)

                def scale(s):
                    if s == 0:
                        dve.wait_ge(rows_landed, l * 16 * 12 + 16 * (2, 8, 10, 12)[n])
                    v.scalar_tensor_tensor(y[:, s, :], y[:, s, :], mv[:, s, 0:1], rows_ln[:, 0, :],
                                           ALU.subtract, ALU.mult)
                    dve.drain()
                    dve.wait_ge(rstd_ready, l * 8 + 2 * n + s + 1)
                    v.scalar_tensor_tensor(x_res[:, s, :], y[:, s, :], rstd[:, s:s + 1], rows_ln[:, 1, :],
                                           ALU.mult, ALU.add).then_inc(x_ready, 1)

                def split(s):
                    dve.wait_ge(xThi_ready, l * 8 + 2 * n + s + 3)
                    c = slice(s * P, (s + 1) * P)
                    split_lo(xT_lo[:, :, c], xT_hi[:, :, c], regs[s]).then_inc(psum_read[regs[s]], 1)

                moments(0)
                scale(0)
                moments(1)
                if regs is not None:
                    between()
                scale(1)
                dve.drain().then_inc(rows_used, 1)
                if regs is not None:
                    split(1)

            def ffn_dve(l, f):
                b = F_BASE[f]

                def gate(c):
                    if not (isinstance(c, int) and c == 0):
                        wait_done_step(dve, l, 1, f, c - 1)
                    for s in range(S):
                        dve.wait_ge(sig_ready, (l * 2 + f) * 2 * NC + c * 2 + (s + 1))
                        v.scalar_tensor_tensor(hx[:, s, :], bank(0, s)[:, 0:CF], 0.5, sg[:, s, :], ALU.mult, ALU.mult)
                    dve.drain()
                    for s in range(S):
                        i = v.tensor_tensor(hx[:, s, :], bank(0, s)[:, CF:2 * CF], hx[:, s, :], ALU.mult)
                    i.then_inc(psum_read[0], 1)

                def hT(c, lo_=hT_lo, hi_=hT_hi):
                    dve.wait_ge(hThi_ready, (l * 2 + f) * NC + c + 1)
                    v.tensor_tensor(lo_[:, 0:2, :], bank(1)[:, :].rearrange("p (a n) -> p a n", a=2), hi_[:, 0:2, :],
                                    ALU.subtract).then_inc(psum_read[1], 1)

                if f == 0:
                    lo(l, 0, b[0])
                    dve.wait_ge(xThi_ready, l * 8 + 1)
                    split_lo(xT_lo[:, :, 0:P], xT_hi[:, :, 0:P], 0).then_inc(psum_read[0], 1)
                    lo(l, 1, b[1])
                    dve.wait_ge(xThi_ready, l * 8 + 2)
                    split_lo(xT_lo[:, :, P:2 * P], xT_hi[:, :, P:2 * P], 1).then_inc(psum_read[1], 1)
                lo(l, 2, b[2])
                gate(0)
                lo(l, 0, b[0] + 1)

                def step(c, last):
                    lo(l, 1, c + b[1])
                    hT(c - 1)
                    lo(l, 2, c + b[2])
                    gate(c)
                    if not (last and f):
                        lo(l, 0, c + (b[0] + 1))

                with dve.Fori(1, NC - 1) as c:
                    step(c, False)
                step(NC - 1, True)
                hT(NC - 1, xT_lo, xT_hi)

                def wait_acc(s):
                    if s == 0:
                        dve.wait_ge(acc0_done, l * 2 + f + 1)
                    else:
                        wait_unit_done(dve, l, 2, b[2] + NC - 1)

                return wait_acc

            with dve.Fori(0, L) as l:
                wait_acc = ffn_dve(l, 0)
                layer_norm(l, 0, lambda s, i: bank(2 + s, i), wait_acc, (2, 3), (0, 1), lambda: mid_lo(l, 1))
                mid_lo(l, 2, 3, 4, 5)
                v.memset(hc[:, :, 0:PAD], 0.0)
                def conv(first, last):
                    for j in range(first, last):
                        if j:
                            dve.drain()
                        for g in range(HEADS):
                            src = hc[:, g, j:j + SEQ]
                            if j == 0:
                                i = v.tensor_scalar(acc[:, g, :], src, taps[:, g, 0:1], taps[:, g, CONV_K:CONV_K + 1],
                                                    ALU.mult, ALU.add)
                            else:
                                i = v.scalar_tensor_tensor(acc[:, g, :], src, taps[:, g, j:j + 1], acc[:, g, :],
                                                           ALU.mult, ALU.add)
                    return i

                wait_chunk(dve, l, 1)
                wait_read(dve, l, 0, "chunk0")
                for s in range(S):
                    i = v.tensor_tensor(h_seq[:, s, :], bank(1, s), sig_b[:, s, :], ALU.mult)
                i.then_inc(psum_read[1], 1)
                mid_lo(l, 6)
                wait_read(dve, l, 2, "conv_h")
                conv(0, 1)
                mid_lo(l, 7)
                wait_read(dve, l, 0, "chunk2")
                dve.wait_ge(rows_landed, l * 16 * 12 + 16 * 6)
                for s in range(S):
                    v.tensor_tensor(k_seq[:, s, :], k_seq[:, s, :], rows[:, 3, :], ALU.mult)
                dve.drain()
                v.tensor_scalar(logf[:, :, :], k_seq[:, :, :], KEY_MAX, None, ALU.min).then_inc(ev["kscaled"], 1)

                conv(1, 3)
                mid_lo(l, 8)
                conv(3, 4)
                wait_event(dve, l, "sigq")
                for s in range(S):
                    i = v.scalar_tensor_tensor(q_seq[:, s, :], bank(1, s), QSCALE, q_seq[:, s, :], ALU.mult, ALU.mult)
                i.then_inc(psum_read[1], 1)
                mid_lo(l, 9)
                wait_event(dve, l, "logf_hi")
                v.tensor_tensor(logf_lo[:, :, :], logf[:, :, :], logf_hi[:, :, :], ALU.subtract).then_inc(ev["logf_lo"], 1)
                conv(4, 7)
                mid_lo(l, 10)
                conv(7, 10)
                mid_lo(l, 11)
                wait_read(dve, l, 3, "kd")
                v.tensor_tensor(kd[:, :, :], kd[:, :, :], k_seq[:, :, :], ALU.mult).then_inc(ev["kd"], 1)
                conv(10, 13)
                mid_lo(l, 12)
                conv(13, 14)
                wait_done(dve, l, 2, "state")
                wait_event(dve, l, "eb")
                v.tensor_copy(state[:, 0, :, :], bank(2, 0).rearrange("p (h v) -> p h v", h=HEADS))
                dve.drain()
                for c in range(1, NCH - 1):
                    u_c = bank(2, 1) if c == 1 else bank(3, 0)
                    for h in range(HEADS):
                        i = v.scalar_tensor_tensor(state[:, c, h, :], state[:, c - 1, h, :], eb[:, h, c:c + 1],
                                                   u_c[:, h * P:(h + 1) * P], ALU.mult, ALU.add)
                        if h == HEADS - 1:
                            i.then_inc(psum_read[2] if c == 1 else psum_read[3], 1)
                    dve.drain()

                mid_lo(l, 13)

                def scale_keys(h):
                    wait_read(dve, l, 2, f"e{h}")
                    wait_read(dve, l, 3, f"e{h}")
                    for i, m in enumerate(LEVELS):
                        half = lambda ap, k: ap.rearrange("p (b k m) -> p b k m", k=2, m=m)[:, :, k, :]
                        for k, src in ((0, kT), (1, qT)):
                            v.tensor_tensor(half(E[:, i, :], k), half(E[:, i, :], k), half(src[:, h, :], k), ALU.mult)
                    v.tensor_tensor(E[:, NL, :], E[:, NL, :], qT[:, h, :], ALU.mult).then_inc(ev["X"], 1)

                def scores(h):
                    for s in range(S):
                        wait_done(dve, l, 2 + s, f"s{h}")
                        v.tensor_tensor(prod, bank(2 + s)[:, 0:MASKS * CHUNK], masks[:, :], ALU.mult)
                        dve.drain()
                        v.tensor_reduce(ST[:, s, :], prod.rearrange("p (i t) -> p t i", i=MASKS), AX_X, ALU.add)\
                            .then_inc(ev["ST"], 1)
                        dve.drain()

                scale_keys(0)
                wait_event(dve, l, "sigo")
                for s in range(S):
                    i = v.tensor_tensor(og[:, s, :], bank(1, s), og[:, s, :], ALU.mult)
                i.then_inc(psum_read[1], 1)
                dve.drain()
                for s in range(S):
                    v.tensor_tensor(og[:, s, :], og[:, s, :], rows[:, 2, :], ALU.mult)
                dve.wait_ge(masks_ready, 1)
                mid_lo(l, 14)
                scores(0)
                mid_lo(l, 15)
                conv(14, 17)
                scale_keys(1)
                mid_lo(l, 16)
                conv(17, 18)
                scores(1)
                mid_lo(l, 17)
                conv(18, 20)
                scale_keys(2)
                mid_lo(l, 18)
                conv(20, 21)
                scores(2)
                mid_lo(l, 19)
                conv(21, 23)
                scale_keys(3)
                mid_lo(l, 20)
                conv(23, 24)
                scores(3)
                mid_lo(l, 21)
                conv(24, 25)
                wait_event(dve, l, "sq")
                v.tensor_scalar(sq[:, :, :], sq[:, :, :], 1.0 / P, RMS_EPS, ALU.mult, ALU.add).then_inc(ev["ms"], 1)
                mid_lo(l, 22)
                conv(25, 26)
                wait_event(dve, l, "rrms")
                for h in range(HEADS):
                    for s in range(S):
                        c = slice(h * P, (h + 1) * P)
                        i = v.scalar_tensor_tensor(o_seq[:, s, c], o_seq[:, s, c], rrms[:, s, h:h + 1], og[:, s, c],
                                                   ALU.mult, ALU.mult)
                i.then_inc(ev["z"], 1)
                mid_lo(l, 23)
                conv(26, CONV_K).then_inc(ev["conv"], 1)
                wait_event(dve, l, "zThi")
                split_lo(xT_lo[:, 4:8, :], xT_hi[:, 4:8, :], 3).then_inc(psum_read[3], 1)
                mid_lo(l, 24)
                wait_done(dve, l, 2, "c_seq")
                for s in range(S):
                    v.bn_stats(stats[:, s, 0:6], bank(2, s))
                dve.drain()
                for s in range(S):
                    v.bn_aggr(mv[:, s, :], stats[:, s, 0:6])
                dve.drain()
                v.tensor_scalar(var[:, :], mv[:, :, 1], LN_EPS, None, ALU.add).then_inc(ev["cvar"], 1)
                for s in range(S):
                    i = v.scalar_tensor_tensor(c_seq[:, s, :], bank(2, s), mv[:, s, 0:1], rows[:, 0, :],
                                               ALU.subtract, ALU.mult)
                i.then_inc(psum_read[2], 1)
                dve.drain()
                wait_event(dve, l, "crstd")
                for s in range(S):
                    i = v.scalar_tensor_tensor(c_seq[:, s, :], c_seq[:, s, :], rstd[:, s:s + 1], rows[:, 1, :],
                                               ALU.mult, ALU.add)
                i.then_inc(ev["c_norm"], 1)
                mid_lo(l, 25)
                wait_event(dve, l, "sigc")
                v.tensor_tensor(c_seq[:, :, :], c_seq[:, :, :], sig_c[:, :, :], ALU.mult).then_inc(ev["c_out"], 1)
                dve.drain().then_inc(rows_used, 1)

                def gated(ch, dst):
                    wait_chunk(dve, l, ch)
                    c = slice((ch % 2) * HALF, (ch % 2 + 1) * HALF)
                    for s in range(S):
                        i = v.tensor_tensor(dst[:, s, c], bank(ch % 2, s), dst[:, s, c], ALU.mult)
                    i.then_inc(psum_read[ch % 2], 1)

                mid_lo(l, 26)
                gated(YH, sigB)
                mid_lo(l, 27)
                gated(YH + 1, sigB)
                wait_event(dve, l, "cThi")
                split_lo(xT_lo[:, 0:4, :], xT_hi[:, 0:4, :], 2).then_inc(psum_read[2], 1)
                mid_lo(l, 28)
                gated(YC, sigA)
                mid_lo(l, 29)
                gated(YC + 1, sigA)
                dve.drain()
                for s in range(S):
                    v.tensor_tensor(sigA[:, s, :], sigA[:, s, :], sigB[:, s, :], ALU.add).then_inc(ev["mix"], 1)
                mid_lo(l, 30)
                for s in range(S):
                    wait_event(dve, l, "mixThi", s + 1)
                    c = slice(s * P, (s + 1) * P)
                    split_lo(xT_lo[:, :, c], xT_hi[:, :, c], 2 + s).then_inc(psum_read[2 + s], 1)
                mid_lo(l, 31, 32, 33, 34)

                def ln_chunks(n, ch, between):
                    layer_norm(l, n, lambda s, i: bank((ch + i) % 2, s), lambda s: wait_rows(dve, l, ch + 1, s), None,
                               (2, 3), between, ch)

                ln_chunks(1, MO, lambda: mid_lo(l, 35))
                mid_lo(l, 36, 37, 38)

                def row_max(g):
                    wait_done(dve, l, 2 + g, "score")
                    v.tensor_reduce(mx[:, g, :], pair(2 + g).rearrange("p (i m) -> p i m", i=4), AX_X, ALU.max)
                    dve.drain()
                    v.tensor_scalar(mx[:, g, :], mx[:, g, :], -XSCALE, None, ALU.mult).then_inc(ev["mx"], 1)

                def normalise(g):
                    wait_read(dve, l, 2 + g, "score")
                    v.reciprocal(rden[:, g, :], den[:, g, :])
                    dve.drain()
                    for i in range(4):
                        k = v.tensor_scalar(Px[:, 4 * g + i, :], Px[:, 4 * g + i, :], rden[:, g, i:i + 1], None, ALU.mult)
                    k.then_inc(ev["Pn"], 1)

                row_max(0)
                mid_lo(l, 39)
                normalise(0)
                row_max(1)
                mid_lo(l, 40)
                normalise(1)
                mid_lo(l, 41)
                for g in range(2):
                    wait_event(dve, l, "oThi", g + 1)
                    split_lo(xT_lo[:, 4 * g:4 * g + 4, :], xT_hi[:, 4 * g:4 * g + 4, :], 2 + g).then_inc(psum_read[2 + g], 1)
                mid_lo(l, 42, 43)
                lo(l, 0, FFN2_BASE[0])
                ln_chunks(2, WO, lambda: lo(l, 1, FFN2_BASE[1]))
                wait_acc = ffn_dve(l, 1)
                layer_norm(l, 3, lambda s, i: bank(2 + s, i), wait_acc, (2, 3), None, None)

        @block.tensor
        def _(pe):
            t_ = nc.tensor

            def turn(dst, src):
                return t_.transpose(dst, src, ident[0:src.shape[0], 0:src.shape[0]])

            def three(dst, hi_, lo_, w, slot, start, stop):
                t_.matmul(dst, hi_, w_hi[slot][:, w], start=start, stop=False)
                t_.matmul(dst, hi_, w_lo[slot][:, w], start=False, stop=False)
                return t_.matmul(dst, lo_, w_hi[slot][:, w], start=False, stop=stop)

            def wait_weights(l, slot, use):
                pe.wait_ge(lo_ready[slot], l * USES[slot] + use + 2)

            def unit(l, slot, use, hi_, lo_, t0, r, first, last):
                wait_weights(l, slot, use)
                for i in range(4):
                    for s in range(S):
                        c = slice(s * P, (s + 1) * P)
                        k = three(bank(r, s), hi_[:, t0 + i, c], lo_[:, t0 + i, c], slice(i * HALF, (i + 1) * HALF),
                                  slot, first and i == 0, last and i == 3)
                k.then_inc(unit_done[slot], 1)

            def units_by_rows(l, units, hi_, lo_, r, ready, between, finished=None):
                for s in range(S):
                    ready(s)
                    c = slice(s * P, (s + 1) * P)
                    for part, (slot, use) in enumerate(units):
                        if s == 0:
                            wait_weights(l, slot, use)
                        for i in range(4):
                            k = three(bank(r, s), hi_[:, 4 * part + i, c], lo_[:, 4 * part + i, c],
                                      slice(i * HALF, (i + 1) * HALF), slot, part + i == 0, part + i == 4)
                        if s == 1:
                            k.then_inc(unit_done[slot], 1)
                        elif part == 0:
                            between()
                        elif finished is not None:
                            k.then_inc(finished, 1)

            def tiles_T(dst, src, n):
                for s in range(S):
                    for i in range(n):
                        k = turn(dst[:, i * SEQ + s * P:i * SEQ + (s + 1) * P], src(s, i))
                return k

            def rows_T(l, use, ready, regs, which):
                for s in which:
                    wait_room(pe, l, regs[s], use)
                    pe.wait_ge(x_ready, ready + s)
                    for i in range(KT):
                        k = turn(pair(regs[s])[:, i * P:(i + 1) * P], x_res[:, s, i * P:(i + 1) * P])
                    k.then_inc(done[regs[s]], 1)

            def ln_T(l, n, regs, which):
                rows_T(l, f"ln{n}", l * 8 + X0 + 2 * n + 1, regs, which)

            def x_T(l, which):
                rows_T(l, "x", l * 8 + 1, (0, 1), which)

            pe.wait_ge(const_landed, 16)
            pe.wait_ge(mem_landed, 16)
            for s in range(S):
                for j in range(KT):
                    k = turn(pair(2 + s)[:, j * P:(j + 1) * P], y[:, s, j * P:(j + 1) * P])
                k.then_inc(memT_done, 1)

            def ffn_pe(l, f):
                b = F_BASE[f]

                def gate_up(c, part, slot, use):
                    if part == 0:
                        wait_room_step(pe, l, 0, f, c)
                    unit(l, slot, use, xT_hi, xT_lo, 4 * part, 0, part == 0, part == 1)

                def h_T(c):
                    wait_read_step(pe, l, 0, f, c)
                    wait_room_step(pe, l, 1, f, c)
                    tiles_T(bank(1), lambda s, i: hx[:, s, i * P:(i + 1) * P], 2).then_inc(done[1], 1)

                def down_rows(s, slot, hi_, lo_, first, last, tiles=(0, 1)):
                    t = slice(s * P, (s + 1) * P)
                    for i in tiles:
                        for half in range(2):
                            w = slice(i * D + half * HALF, i * D + (half + 1) * HALF)
                            k = three(bank(2 + s, half), hi_[:, i, t], lo_[:, i, t], w, slot,
                                      first and i == 0, last and i == 1)
                    return k

                def down(c, slot, use, first):
                    wait_weights(l, slot, use)
                    wait_read_step(pe, l, 1, f, c)
                    for s in range(S):
                        k = down_rows(s, slot, hT_hi, hT_lo, first, False)
                    k.then_inc(unit_done[slot], 1)

                def ready(s):
                    if f:
                        wait_read(pe, l, 2 + s, "ln2")
                        if s == 0:
                            wait_room_step(pe, l, 0, 1, 0)
                    else:
                        wait_room_step(pe, l, 0, 0, 0) if s == 0 else wait_room_step(pe, l, 1, 0, 0)

                if f == 0:
                    x_T(l, (0,))
                units_by_rows(l, [(0, b[0]), (1, b[1])], xT_hi, xT_lo, 0, ready,
                              (lambda: ln_T(l, 2, (2, 3), (1,))) if f else (lambda: x_T(l, (1,))))

                def step(c, first):
                    gate_up(c, 0, 2, c + (b[2] - 1))
                    h_T(c - 1)
                    gate_up(c, 1, 0, c + b[0])
                    if first:
                        wait_room(pe, l, 2, f"acc{f}")
                        wait_room(pe, l, 3, f"acc{f}")
                    if not (isinstance(c, int) and c == NC - 1):
                        down(c - 1, 1, c + b[1], first)

                step(1, True)
                with pe.Fori(2, NC - 1) as c:
                    step(c, False)
                step(NC - 1, False)
                wait_weights(l, 1, b[1] + NC - 1)
                wait_read_step(pe, l, 1, f, NC - 2)
                down_rows(0, 1, hT_hi, hT_lo, False, False)
                h_T(NC - 1)
                down_rows(1, 1, hT_hi, hT_lo, False, False, (0,))
                wait_weights(l, 2, b[2] + NC - 1)
                wait_read_step(pe, l, 1, f, NC - 1)
                down_rows(0, 2, xT_hi, xT_lo, False, True).then_inc(acc0_done, 1)
                down_rows(1, 1, hT_hi, hT_lo, False, False, (1,)).then_inc(unit_done[1], 1)
                down_rows(1, 2, xT_hi, xT_lo, False, True).then_inc(unit_done[2], 1)

            with pe.Fori(0, L) as l:
                ffn_pe(l, 0)
                ln_T(l, 0, (0, 1), (0,))

                def chunk_part(ch, part, hi_=xT_hi, lo_=xT_lo):
                    if part == 0:
                        wait_room(pe, l, ch % 2, f"chunk{ch}")
                    unit(l, *mid_unit(chunk_units(ch)[part]), hi_, lo_, 4 * part, ch % 2, part == 0, part == 1)

                def chunk(ch, hi_=xT_hi, lo_=xT_lo):
                    chunk_part(ch, 0, hi_, lo_)
                    chunk_part(ch, 1, hi_, lo_)

                def small_T(r, name, src, n=4):
                    wait_room(pe, l, r, name)
                    tiles_T(pair(r), src, n).then_inc(done[r], 1)

                def chunk_by_rows(ch, ready, between, finished=None):
                    units_by_rows(l, [mid_unit(u) for u in chunk_units(ch)], xT_hi, xT_lo, ch % 2, ready, between,
                                  finished)

                chunk_by_rows(0, lambda s: wait_read(pe, l, s, "ln0"), lambda: ln_T(l, 0, (0, 1), (1,)))
                wait_room(pe, l, 2, "taps")
                pe.wait_ge(conv_landed, l * 32 + 32)
                chunk_part(1, 0)
                for g in range(HEADS):
                    k = turn(bank(2)[:, g * 32:(g + 1) * 32], conv_rows[0:32, g * P:(g + 1) * P])
                k.then_inc(done[2], 1)
                chunk_part(1, 1)
                chunk_part(2, 0)
                wait_read(pe, l, 1, "chunk1")
                small_T(2, "conv_h", lambda s, g: h_seq[:, s, g * P:(g + 1) * P])
                chunk_part(2, 1)
                chunk_part(3, 0)
                wait_event(pe, l, "kscaled")
                small_T(3, "k_T", lambda s, g: k_seq[:, s, g * P:(g + 1) * P])
                chunk_part(3, 1)
                chunk_part(4, 0)
                wait_read(pe, l, 1, "chunk3")
                small_T(2, "q_T", lambda s, g: q_seq[:, s, g * P:(g + 1) * P])
                chunk_part(4, 1)
                wait_room(pe, l, 3, "kd")
                wait_event(pe, l, "logf_lo")
                pe.wait_ge(sums_ready, 1)
                for s in range(S):
                    tail = sums[:, DECAYS * P:(DECAYS + 1) * P]
                    t_.matmul(bank(3, s), tail, logf_hi[:, s, :], start=True, stop=False)
                    k = t_.matmul(bank(3, s), tail, logf_lo[:, s, :], start=False, stop=True)
                k.then_inc(done[3], 1)
                chunk(5)
                for r in (2, 3):
                    wait_room(pe, l, r, "state")
                wait_event(pe, l, "kd")
                wait_read(pe, l, 0, "chunk4")
                for c in range(NCH - 1):
                    rows_c = slice(c % 2 * CHUNK, (c % 2 + 1) * CHUNK)
                    for h in range(HEADS):
                        cols = slice(h * P, (h + 1) * P)
                        k = t_.matmul(bank(2 + c // 2, c % 2)[:, cols], kd[rows_c, c // 2, cols],
                                      v_seq[rows_c, c // 2, cols], start=True, stop=True)
                    if c == 1:
                        k.then_inc(done[2], 1)
                for h in range(HEADS):
                    for s in range(S):
                        for f_ in (logf_hi, logf_lo):
                            k = t_.matmul(bank(3, 1)[:, h * NCH + 2 * s:h * NCH + 2 * s + 2],
                                          f_[:, s, h * P:(h + 1) * P], sums[:, (DECAYS + 1) * P:],
                                          start=f_ is logf_hi, stop=f_ is logf_lo)
                k.then_inc(done[3], 1)
                chunk_part(6, 0)

                def decays(h):
                    for s in range(S):
                        wait_room(pe, l, 2 + s, f"e{h}")
                        for part in (logf_hi, logf_lo):
                            f_, first = part[:, s, h * P:(h + 1) * P], part is logf_hi
                            t_.matmul(bank(2 + s, 0), f_, sums[:, 0:HALF], start=first, stop=not first)
                            k = t_.matmul(bank(2 + s, 1)[:, 0:DECAYS * P - HALF], f_, sums[:, HALF:DECAYS * P],
                                          start=first, stop=not first)
                        k.then_inc(done[2 + s], 1)

                def scores(h):
                    wait_event(pe, l, "X", h + 1)
                    for s in range(S):
                        wait_room(pe, l, 2 + s, f"s{h}")
                        pe.sem_inc(pe_steps, 1)
                        for c in (2 * s, 2 * s + 1):
                            at = slice(c % 2 * CHUNK, (c % 2 + 1) * CHUNK)
                            t = slice(c * CHUNK, (c + 1) * CHUNK)
                            for i in range(MASKS):
                                k_, q_ = (E[:, i, t], E[:, i, t]) if i < NL else (kT[:, h, t], qT[:, h, t])
                                k = t_.matmul(bank(2 + s)[at, i * CHUNK:(i + 1) * CHUNK], k_, q_, start=True, stop=True)
                        k.then_inc(done[2 + s], 1)

                def outputs(h):
                    cols = slice(h * P, (h + 1) * P)
                    for s in range(S):
                        wait_event(pe, l, "ST", 2 * h + s + 1)
                        if h == 0 and s == 0:
                            wait_read(pe, l, 3, "state")
                        pe.sem_inc(pe_steps, 1)
                        o = bank(2 + s, 1)[:, 0:P]
                        for c in (2 * s, 2 * s + 1):
                            at = slice(c % 2 * CHUNK, (c % 2 + 1) * CHUNK)
                            k = t_.matmul(o[at, :], ST[at, s, :], v_seq[at, s, cols], start=True, stop=c == 0)
                            if c:
                                k = t_.matmul(o[at, :], E[:, NL, c * CHUNK:(c + 1) * CHUNK], state[:, c - 1, h, :],
                                              start=False, stop=True)
                        k.then_inc(done[2 + s], 1)

                decays(0)
                chunk_part(6, 1)
                scores(0)
                chunk_part(7, 0)
                outputs(0)
                decays(1)
                chunk_part(7, 1)
                scores(1)
                chunk_part(8, 0)
                outputs(1)
                decays(2)
                chunk_part(8, 1)
                scores(2)
                chunk_part(9, 0)
                outputs(2)
                decays(3)
                chunk_part(9, 1)
                scores(3)
                chunk_part(K_, 0, memT_hi, memT_lo)
                outputs(3)
                chunk_part(K_, 1, memT_hi, memT_lo)
                chunk_part(K_ + 1, 0, memT_hi, memT_lo)
                wait_event(pe, l, "z")
                small_T(3, "z_T", lambda s, g: o_seq[:, s, g * P:(g + 1) * P])
                chunk_part(K_ + 1, 1, memT_hi, memT_lo)
                wait_event(pe, l, "conv")
                wait_room(pe, l, 2, "c_seq")
                for s in range(S):
                    for g in range(HEADS):
                        k = turn(bank(2, s)[:, g * P:(g + 1) * P], acc[:, g, s * P:(s + 1) * P])
                k.then_inc(done[2], 1)

                def branch(ch, t0):
                    wait_room(pe, l, ch % 2, f"chunk{ch}")
                    unit(l, *mid_unit(chunk_units(ch)[0]), xT_hi, xT_lo, t0, ch % 2, True, True)

                wait_read(pe, l, 3, "z_T")
                branch(YH, 4)
                branch(YH + 1, 4)
                wait_event(pe, l, "c_out")
                small_T(2, "c_T", lambda s, g: c_seq[:, s, g * P:(g + 1) * P])
                wait_read(pe, l, 2, "c_T")
                branch(YC, 0)
                branch(YC + 1, 0)
                chunk_part(V0, 0, memT_hi, memT_lo)
                for s in range(S):
                    wait_event(pe, l, "mix", s + 1)
                    wait_room(pe, l, 2 + s, "mix")
                    for i in range(KT):
                        k = turn(pair(2 + s)[:, i * P:(i + 1) * P], sigA[:, s, i * P:(i + 1) * P])
                    k.then_inc(done[2 + s], 1)
                chunk_part(V0, 1, memT_hi, memT_lo)
                wait_read(pe, l, 2, "mix")
                wait_read(pe, l, 3, "mix")
                chunk(MO)
                wait_read(pe, l, 0, f"chunk{K_}")
                small_T(2, "K0", lambda s, g: kseq_x[0][:, s, g * P:(g + 1) * P])
                wait_read(pe, l, 1, f"chunk{K_ + 1}")
                small_T(3, "K1", lambda s, g: kseq_x[1][:, s, g * P:(g + 1) * P])

                def room(ch):
                    return lambda s: wait_room(pe, l, ch % 2, f"chunk{ch}") if s == 0 else None

                chunk_by_rows(MO + 1, room(MO + 1), lambda: None, rows0_done)
                ln_T(l, 1, (2, 3), (0,))

                def q_ready(s):
                    wait_read(pe, l, 2 + s, "ln1")
                    room(Q_)(s)

                chunk_by_rows(Q_, q_ready, lambda: ln_T(l, 1, (2, 3), (1,)))
                chunk_part(Q_ + 1, 0)
                wait_read(pe, l, Q_ % 2, f"chunk{Q_}")
                small_T(2, "Q0", lambda s, g: qseq_x[0][:, s, g * P:(g + 1) * P])
                chunk_part(Q_ + 1, 1)
                def score(g):
                    wait_room(pe, l, 2 + g, "score")
                    for h in (2 * g, 2 * g + 1):
                        for s in range(S):
                            o = bank(2 + g, h % 2)[:, s * N_MEM:(s + 1) * N_MEM]
                            for d in range(2):
                                k = t_.matmul(o, QTx[:, 2 * h + d, s * P:(s + 1) * P], KTx[:, 2 * h + d, :],
                                              start=d == 0, stop=d == 1)
                    k.then_inc(done[2 + g], 1)

                score(0)
                wait_read(pe, l, (Q_ + 1) % 2, f"chunk{Q_ + 1}")
                small_T(3, "Q1", lambda s, g: qseq_x[1][:, s, g * P:(g + 1) * P])
                chunk_part(V1, 0, memT_hi, memT_lo)
                score(1)

                def P_T(g):
                    wait_room(pe, l, 2 + g, "P_T")
                    wait_event(pe, l, "Pn", g + 1)
                    for h in (2 * g, 2 * g + 1):
                        k = tiles_T(bank(2 + g, h % 2), lambda s, m: Px[:, 2 * h + s, m * P:(m + 1) * P], 2)
                    k.then_inc(done[2 + g], 1)

                P_T(0)
                chunk_part(V1, 1, memT_hi, memT_lo)
                P_T(1)
                for g in range(2):
                    wait_room(pe, l, 2 + g, "pv")
                    if g:
                        wait_read(pe, l, V1 % 2, f"chunk{V1}")
                    for h in (2 * g, 2 * g + 1):
                        for d in range(2):
                            for m in range(2):
                                k = t_.matmul(bank(2 + g, h % 2)[:, d * SEQ:(d + 1) * SEQ],
                                              Vx[:, m, h * XD + d * P:h * XD + (d + 1) * P], PTx[:, h, m, :],
                                              start=m == 0, stop=m == 1)
                    k.then_inc(done[2 + g], 1)
                for g in range(2):
                    wait_read(pe, l, 2 + g, "pv")
                    chunk_part(WO, g)
                chunk_by_rows(WO + 1, room(WO + 1), lambda: None, rows0_done)
                ln_T(l, 2, (2, 3), (0,))
                ffn_pe(l, 1)


INPUTS = ("x mem ln_g ln_b ffn1_w_gu ffn1_w_down w_in conv_w conv_b conv_ln_g conv_ln_b w_conv_proj hgrn_lb "
          "hgrn_norm_g w_hgrn_proj w_mix_out xa_wq xa_wkv xa_wo ffn2_w_gu ffn2_w_down").split()


def kernel(**inputs):
    import concourse.bacc as bacc
    from concourse.bass_utils import run_bass_kernel_spmd

    nc = bacc.Bacc("TRN2", target_bir_lowering=False, num_devices=1)
    arrays, args = {}, []
    for name in INPUTS + ["consts"]:
        a = np.ascontiguousarray(layout_constants() if name == "consts" else inputs[name])
        arrays["in_" + name] = a
        args.append(nc.dram_tensor("in_" + name, a.shape, mybir.dt.from_np(a.dtype), kind="ExternalInput").ap())
    shape = tuple(inputs["x"].shape)
    out = nc.dram_tensor("out_0", shape, F32, kind="ExternalOutput").ap()
    build(nc, *args, out)
    r = run_bass_kernel_spmd(nc, [arrays], core_ids=[0])
    return r.results[0]["out_0"]
```

```python
from contextlib import ExitStack
import math

import numpy as np

import concourse.bass as bass
from concourse import mybir
from concourse.alu_op_type import AluOpType as ALU

ACT = mybir.ActivationFunctionType
F32 = mybir.dt.float32
FR = mybir.dt.float32r
BF16 = mybir.dt.bfloat16
AX_X = mybir.AxisListType.X

P = 128
HALF = 512
RING = 3
CHUNK = 64
CONV_K = 31
LN_EPS = 1e-5
RMS_EPS = 1e-6
KEY_MAX = 1.0 - 1e-6
LEVELS = (32, 16, 8, 4, 2, 1)
NL = len(LEVELS)
DECAYS = NL + 1
MASKS = NL + 1


def layout_constants():
    t = np.arange(P)
    same_chunk = (t[:, None] // CHUNK) == (t[None, :] // CHUNK)
    sums = np.zeros((P, DECAYS, P), np.float32)
    masks = np.zeros((P, MASKS, P), np.float32)
    for i, m in enumerate(LEVELS):
        mid = t // (2 * m) * (2 * m) + m
        late = t >= mid
        src = t[:, None]
        sums[:, i, :] = np.where(late[None, :], (src >= mid[None, :]) & (src <= t[None, :]),
                                 (src > t[None, :]) & (src < mid[None, :]))
        same = (t[:, None] // (2 * m)) == (t[None, :] // (2 * m))
        masks[:, i, :] = same & ~late[:, None] & late[None, :]
    sums[:, NL, :] = same_chunk & (t[:, None] <= t[None, :])
    masks[:, NL, :] = np.eye(P)
    masks = np.concatenate([masks[c:c + CHUNK, :, c:c + CHUNK] for c in range(0, P, CHUNK)])
    tail = (same_chunk & (t[:, None] > t[None, :])).astype(np.float32)
    chunk_sum = ((t[:, None] // CHUNK) == np.arange(P // CHUNK)[None, :]).astype(np.float32)
    return np.concatenate([sums.reshape(P, -1), tail, chunk_sum, masks.reshape(P, -1),
                           np.eye(P, dtype=np.float32)], axis=1)




class Uses:

    def __init__(self, names):
        self.names = names
        self.n = len(names)

    def __call__(self, name):
        return self.names.index(name)


def build(nc, x, mem, ln_g, ln_b, ffn1_w_gu, ffn1_w_down, w_in, conv_w, conv_b, conv_ln_g, conv_ln_b,
          w_conv_proj, hgrn_lb, hgrn_norm_g, w_hgrn_proj, w_mix_out, xa_wq, xa_wkv, xa_wo,
          ffn2_w_gu, ffn2_w_down, consts, out):
    _, SEQ, D = x.shape
    N_MEM = mem.shape[1]
    L = ln_g.shape[0]
    D_FF = ffn1_w_down.shape[1]
    W = conv_w.shape[2]
    ALPHA = float((2 * L) ** 0.25)
    S = SEQ // P
    KT = D // P
    HEADS = W // P
    XH = 4
    XD = D // XH
    XSCALE = XD ** -0.5
    QSCALE = P ** -0.5
    CF = 256
    NC = D_FF // CF
    NCH = SEQ // CHUNK
    assert S == 2 and KT == 8 and NC * CF == D_FF and N_MEM == SEQ and XD == 2 * P and W == HALF and L == 2

    MID = 44
    FFN_USES = [NC, NC, NC]
    MID_BASE = list(FFN_USES)
    SKIP = 20
    mid_slots = [(u + (u >= SKIP)) % RING for u in range(MID)]
    FFN2_BASE = [MID_BASE[j] + mid_slots.count(j) for j in range(RING)]
    USES = [FFN2_BASE[j] + FFN_USES[j] for j in range(RING)]
    F_BASE = ([0] * RING, FFN2_BASE)

    def mid_unit(u):
        j = mid_slots[u]
        return j, MID_BASE[j] + mid_slots[:u].count(j)

    gu = [[f"gu{f}_{c}" for c in range(NC)] for f in (0, 1)]
    hT = [[f"hT{f}_{c}" for c in range(NC)] for f in (0, 1)]
    K_, YH, YC, V0, MO, Q_, V1, WO = 10, 12, 14, 16, 17, 19, 21, 22
    R0 = Uses(["x_0", "x_1"] + gu[0][1:] + [f"chunk{c}" for c in range(0, 24, 2)] + gu[1][1:])
    R1 = Uses(gu[0][:1] + hT[0] + ["ln0_0", "ln0_1"] + [f"chunk{c}" for c in range(1, 24, 2)] + gu[1][:1] + hT[1])

    def chunk_units(ch):
        first = 2 * ch if ch < YH else 2 * YH + ch - YH if ch < V0 else 2 * ch - 4
        return (first,) if YH <= ch < V0 else (first, first + 1)

    heads = [f"{k}{h}" for h in range(HEADS) for k in "es"]
    R2 = Uses(["acc0", "taps", "conv_h", "q_T", "state"] + heads
              + ["c_seq", "c_T", "mix", "K0", "ln1_0", "Q0", "score", "P_T", "pv", "ln2_0", "acc1"])
    R3 = Uses(["acc0", "k_T", "kd", "state"] + heads
              + ["z_T", "mix", "K1", "ln1_1", "Q1", "score", "P_T", "pv", "ln2_1", "acc1"])
    R = [R0, R1, R2, R3]
    def signals(names):
        for n in names:
            yield n
            if n.startswith(("x_", "ln")):
                yield n + "b"
            elif n[0] == "s" and n[1:].isdigit():
                yield "o" + n[1:]

    D0, D1, D2, D3 = (Uses([k for k in signals(r.names) if not k.startswith(("acc", "gu", "chunk"))]) for r in
                      (R0, R1, R2, R3))
    DONE = [D0, D1, D2, D3]

    with ExitStack() as ctx:
        def sb(name, shape, dt=F32):
            return ctx.enter_context(nc.sbuf_tensor(name, shape, dt))

        def sem(name):
            return ctx.enter_context(nc.semaphore(name))

        UNIT = 4 * HALF
        raw = [sb(f"raw{j}", [P, UNIT]) for j in range(RING)]
        w_hi = [sb(f"w_hi{j}", [P, UNIT], FR) for j in range(RING)]
        w_lo = [sb(f"w_lo{j}", [P, UNIT], FR) for j in range(RING)]
        xT_hi = sb("xT_hi", [P, KT, SEQ], FR)
        xT_lo = sb("xT_lo", [P, KT, SEQ], FR)
        memT_hi = sb("memT_hi", [P, KT, SEQ], FR)
        memT_lo = sb("memT_lo", [P, KT, SEQ], FR)
        hT_hi = sb("hT_hi", [P, 2, SEQ], FR)
        hT_lo = sb("hT_lo", [P, 2, SEQ], FR)
        x_res = sb("x_res", [P, S, D])
        y = sb("y", [P, S, D])
        sums = sb("sums", [P, (DECAYS + 1) * P + 2], FR)
        logf_hi = sb("logf_hi", [P, S, W], FR)
        logf_lo = sb("logf_lo", [P, S, W], FR)
        ident = sb("ident", [P, P])
        masks = sb("masks", [P, MASKS * CHUNK], BF16)
        rows = sb("rows", [P, 4, HALF])
        rows_ln = rows[:, :, :].rearrange("p (a b) n -> p a (b n)", a=2)
        taps = sb("taps", [P, HEADS, 32])
        stats = sb("stats", [P, S, 12])
        mv = sb("mv", [P, S, 2])
        var = sb("var", [P, S])
        rstd = sb("rstd", [P, S])
        mhalf = sb("mhalf", [P, 8])
        eb = sb("eb", [P, HEADS, NCH])
        sq = sb("sq", [P, S, HEADS])
        squares = sb("squares", [P, S, P])
        rrms = sb("rrms", [P, S, HEADS])
        mx = sb("mx", [P, 2, 4])
        den = sb("den", [P, 2, 4])
        rden = sb("rden", [P, 2, 4])

        ARENA = 15104
        arena = sb("arena", [P, ARENA])
        top = [0]

        def cut(n):
            top[0] += n
            assert top[0] <= ARENA
            return arena[:, top[0] - n:top[0]]

        def by(ap, a):
            return ap.rearrange("p (a n) -> p a n", a=a)

        sigA = by(cut(S * D), S)
        sigB = by(cut(S * D), S)
        E = by(cut(DECAYS * SEQ), DECAYS)
        kT = by(cut(HEADS * SEQ), HEADS)
        qT = by(cut(HEADS * SEQ), HEADS)
        v_seq = by(cut(S * W), S)
        kd = by(cut(S * W), S)
        logf = kd
        og = by(cut(S * W), S)
        PAD = CONV_K - 1
        hc = by(cut(HEADS * (SEQ + PAD)), HEADS)
        acc = by(cut(HEADS * SEQ), HEADS)
        conv_rows = arena[:, top[0]:top[0] + W]
        state = cut((NCH - 1) * W).rearrange("p (c h v) -> p c h v", c=NCH - 1, h=HEADS)
        ST = by(cut(S * CHUNK), S)
        k_seq = y[:, 0, :].rearrange("p (s n) -> p s n", s=S)
        q_seq = y[:, 1, :].rearrange("p (s n) -> p s n", s=S)
        sig_b, h_seq, sig_c = og, by(acc.rearrange("p h t -> p (h t)"), S), by(acc.rearrange("p h t -> p (h t)"), S)
        prod, c_seq, o_seq = y[:, 0, 0:MASKS * CHUNK], k_seq, q_seq
        top[0] = 0
        KTx = by(cut(KT * N_MEM), KT)
        QTx = by(cut(KT * SEQ), KT)
        kseq_x = [by(cut(S * HALF), S) for _ in range(2)]
        Vx = by(cut(S * D), S)
        qseq_x = [by(cut(S * HALF), S) for _ in range(2)]
        Px = by(cut(XH * S * N_MEM), XH * S)
        PTx = cut(XH * 2 * SEQ).rearrange("p (h m t) -> p h m t", h=XH, m=2)
        top[0] = 0
        sg = by(cut(S * CF), S)
        hx = by(cut(S * CF), S)

        lb_in = by(E[:, 0, 0:L * W // P], L)
        lb_sum = E[:, 1, 0:W // P]
        key = by(kT[:, 0, 0:L * W // P], L)

        ps = ctx.enter_context(nc.psum_tensor("ps", [P, 8, HALF], F32))

        def bank(r, i=0):
            return ps[:, 2 * r + i, :]

        def pair(r):
            return ps[:, 2 * r:2 * r + 2, :].rearrange("p b n -> p (b n)")

        scratch = nc.dram_tensor("key_scale", [L, W], F32, kind="Internal").ap()

        raw_landed = [sem(f"raw_landed{j}") for j in range(RING)]
        hi_ready = [sem(f"hi_ready{j}") for j in range(RING)]
        lo_ready = [sem(f"lo_ready{j}") for j in range(RING)]
        unit_done = [sem(f"unit_done{j}") for j in range(RING)]
        psum_read = [sem(f"psum_read{r}") for r in range(4)]
        done = [sem(f"psum_done{r}") for r in range(4)]
        acc_done = sem("acc_done")
        rows0_done = sem("rows0_done")
        x_landed = sem("x_landed")
        sp_steps = sem("sp_steps")
        pe_steps = sem("pe_steps")
        const_landed = sem("const_landed")
        memT_done = sem("memT_done")
        memThi_ready = sem("memThi_ready")
        consts_landed = sem("consts_landed")
        lb_landed = sem("lb_landed")
        sums_ready = sem("sums_ready")
        masks_ready = sem("masks_ready")
        conv_landed = sem("conv_landed")
        mem_landed = sem("mem_landed")
        mhalf_ready = sem("mhalf_ready")
        lb_centered = sem("lb_centered")
        lb_exp = sem("lb_exp")
        key_ready = sem("key_ready")
        scratch_stored = sem("scratch_stored")
        rows_landed = sem("rows_landed")
        rows_used = sem("rows_used")
        half_split = sem("half_split")
        sig_ready = sem("sig_ready")
        hThi_ready = sem("hThi_ready")
        var_ready = sem("var_ready")
        rstd_ready = sem("rstd_ready")
        x_ready = sem("x_ready")
        xThi_ready = sem("xThi_ready")
        names = ["kscaled", "logf_hi", "logf_lo", "sigq", "kd", "sigo", "eb", "X", "ST", "sq", "ms", "rrms", "z",
                 "zThi", "cvar", "crstd", "c_norm", "sigc", "c_out", "cThi", "padded", "tap0", "conv", "mix",
                 "mixThi", "mx", "Pn", "oThi"]
        ev = {n: sem(n + "_ready") for n in names}
        out_stored = sem("out_stored")

        X0 = S

        PER = dict.fromkeys(names, 1)
        PER.update(X=HEADS, ST=2 * HEADS, mix=S, mixThi=S, mx=2, Pn=2, oThi=2)

        def wait_event(eng, l, name, k=1):
            eng.wait_ge(ev[name], l * PER[name] + k)

        def wait_unit_done(eng, l, slot, use):
            eng.wait_ge(unit_done[slot], l * USES[slot] + use + 2)

        def wait_chunk(eng, l, ch):
            wait_unit_done(eng, l, *mid_unit(chunk_units(ch)[-1]))

        def wait_rows(eng, l, ch, s):
            if s == 0:
                eng.wait_ge(rows0_done, l * 2 + (1 if ch < WO else 2))
            else:
                wait_chunk(eng, l, ch)

        def wait_done(eng, l, r, name):
            eng.wait_ge(done[r], l * DONE[r].n + DONE[r](name) + 1)

        def wait_done_step(eng, l, f, c):
            eng.wait_ge(done[1], l * D1.n + D1(f"hT{f}_0") + c + 1)

        def wait_room(eng, l, r, name):
            eng.wait_ge(psum_read[r], l * R[r].n + R[r](name) + 1)

        def wait_read(eng, l, r, name):
            eng.wait_ge(psum_read[r], l * R[r].n + R[r](name) + 2)

        def wait_gu_read(eng, l, f, c):
            if isinstance(c, int) and c == 0:
                wait_read(eng, l, 1, f"gu{f}_0")
            else:
                eng.wait_ge(psum_read[0], c + (l * R0.n + R0(f"gu{f}_1") + 1))

        def wait_hT_read(eng, l, f, c):
            eng.wait_ge(psum_read[1], c + (l * R1.n + R1(f"hT{f}_0") + 2))

        block = ctx.enter_context(nc.Block())

        @block.sync
        def _(sp):
            sp.dma_start(ident[:, :], consts[:, consts.shape[1] - P:]).then_inc(const_landed, 16)
            sp.dma_start(y[:, :, :], mem[0].rearrange("(s p) d -> p s d", p=P)).then_inc(mem_landed, 16)
            for s in range(S):
                sp.dma_start(x_res[:, s, :], x[0, s * P:(s + 1) * P, :]).then_inc(x_landed, 16)

            def load(l, slot, use, *parts):
                sp.wait_ge(lo_ready[slot], l * USES[slot] + use + 1)
                sp.sem_inc(sp_steps, 1)
                for dst, src in parts:
                    sp.dma_start(dst, src).then_inc(raw_landed[slot], 16)

            def load_gu(l, f, w, c, part, slot, use):
                src = w.rearrange("l (t p) (g n) -> l g p t n", p=P, g=2)
                dst = raw[slot][:, :].rearrange("p (t g n) -> p g t n", t=4, g=2)
                load(l, slot, use, *[(dst[:, g], src[l, g, :, 4 * part:4 * part + 4, bass.ds(c * CF, CF)])
                                     for g in range(2)])

            def load_down(l, f, w, c, slot, use):
                src = w.rearrange("l (t p) n -> l p t n", p=P)
                load(l, slot, use, *[(raw[slot][:, i * D:(i + 1) * D], src[l, :, bass.ds(c * 2 + i, 1), :])
                                     for i in range(2)])

            def load_ffn(l, f, w_gu, w_down):
                b = F_BASE[f]
                load_gu(l, f, w_gu, 0, 0, 0, b[0])
                load_gu(l, f, w_gu, 0, 1, 1, b[1])
                with sp.Fori(1, NC) as c:
                    load_gu(l, f, w_gu, c, 0, 2, c + (b[2] - 1))
                    load_gu(l, f, w_gu, c, 1, 0, c + b[0])
                    load_down(l, f, w_down, c - 1, 1, c + b[1])
                load_down(l, f, w_down, NC - 1, 2, b[2] + NC - 1)

            def load_cols(l, u, w, rows0, cols0):
                src = w.rearrange("l (t p) n -> l p t n", p=P)
                t0 = rows0 // P
                slot, use = mid_unit(u)
                dst = raw[slot][:, :].rearrange("p (t n) -> p t n", t=4)
                load(l, slot, use, *[(dst[:, t:t + 2], src[l, :, t0 + t:t0 + t + 2, cols0:cols0 + HALF])
                                     for t in (0, 2)])

            with sp.Fori(0, L) as l:
                load_ffn(l, 0, ffn1_w_gu, ffn1_w_down)
                u = 0
                order = [1, 0, 3, 2, 4, 5, 6, 7, 8, 9]
                for col in order:
                    for part in range(2):
                        load_cols(l, u, w_in, part * HALF, col * HALF)
                        u += 1
                for w, first, n in ((xa_wkv, 0, 2), (w_hgrn_proj, 0, 2), (w_conv_proj, 0, 2), (xa_wkv, D, 1),
                                    (w_mix_out, 0, 2), (xa_wq, 0, 2), (xa_wkv, D + HALF, 1), (xa_wo, 0, 2)):
                    for i in range(n):
                        for part in range(w.shape[1] // HALF):
                            load_cols(l, u, w, part * HALF, first + i * HALF)
                            u += 1
                assert u == MID
                load_ffn(l, 1, ffn2_w_gu, ffn2_w_down)
            for s in range(S):
                sp.wait_ge(x_ready, X0 + 8 * (L - 1) + 6 + s + 1)
                sp.dma_start(out[0, s * P:(s + 1) * P, :], x_res[:, s, :]).then_inc(out_stored, 16)
            sp.wait_ge(out_stored, 16 * S)

        @block.gpsimd
        def _(pool):
            cn = (DECAYS + 1) * P + 2
            consts_in = arena[:, S * D:S * D + cn + MASKS * CHUNK]
            pool.wait_ge(x_landed, 16 * S)
            pool.dma_start(consts_in, consts[:, 0:cn + MASKS * CHUNK]).then_inc(consts_landed, 16)
            pool.memset(mhalf[:, :], -0.5).then_inc(mhalf_ready, 1)
            pool.wait_ge(key_ready, 1)
            pool.dma_start(scratch.rearrange("l (p n) -> p l n", p=P), key).then_inc(scratch_stored, 16)
            pool.wait_ge(scratch_stored, 16)
            pool.wait_ge(mhalf_ready, 1)
            pool.wait_ge(consts_landed, 16)
            pool.tensor_copy(masks[:, :], consts_in[:, cn:]).then_inc(masks_ready, 1)
            pool.tensor_copy(sums[:, :], consts_in[:, 0:cn]).then_inc(sums_ready, 1)

            def load_ln(l, n):
                pool.wait_ge(rows_used, l * 5 + n + 1)
                k = n if n == 0 else n - 1
                pool.dma_start(rows_ln[:, 0, :], ln_g[l, k:k + 1, :].broadcast_to([P, D])).then_inc(rows_landed, 16)
                pool.dma_start(rows_ln[:, 1, :], ln_b[l, k:k + 1, :].broadcast_to([P, D])).then_inc(rows_landed, 16)

            def power(l, k, per, src_sem, out_sem, dst, src):
                pool.wait_ge(src_sem, l * per + k)
                pool.tensor_tensor(dst, src, mhalf[:, 0:src.shape[1]], ALU.pow).then_inc(out_sem, 1)

            def ln_powers(l, n):
                for s in range(S):
                    power(l, 2 * n + s + 1, 8, var_ready, rstd_ready, rstd[:, s:s + 1], var[:, s:s + 1])

            with pool.Fori(0, L) as l:
                load_ln(l, 0)
                ln_powers(l, 0)
                pool.wait_ge(rows_used, l * 5 + 2)
                for i, a in enumerate((conv_ln_g, conv_ln_b, hgrn_norm_g, scratch)):
                    pool.dma_start(rows[:, i, :], a[bass.ds(l, 1), :].broadcast_to([P, W])).then_inc(rows_landed, 16)
                pool.dma_start(conv_rows[0:CONV_K, :], conv_w[l]).then_inc(conv_landed, 16)
                pool.dma_start(conv_rows[CONV_K:32, :], conv_b[bass.ds(l, 1), :]).then_inc(conv_landed, 16)
                pool.wait_ge(ev["ms"], l + 1)
                pool.tensor_tensor(rrms[:, :, :], sq[:, :, :], mhalf[:, 0:8].rearrange("p (a b) -> p a b", a=2),
                                   ALU.pow).then_inc(ev["rrms"], 1)
                pool.wait_ge(ev["cvar"], l + 1)
                pool.tensor_tensor(rstd[:, :], var[:, :], mhalf[:, 0:2], ALU.pow).then_inc(ev["crstd"], 1)
                for n in (1, 2, 3):
                    load_ln(l, n + 1)
                    ln_powers(l, n)

        @block.scalar
        def _(act):
            sc = nc.scalar

            def hi(l, slot, use):
                act.wait_ge(raw_landed[slot], (l * USES[slot] + use + 1) * 32)
                act.wait_ge(unit_done[slot], l * USES[slot] + use + 1)
                sc.copy(w_hi[slot][:, :], raw[slot][:, :]).then_inc(hi_ready[slot], 1)

            def mid_hi(l, *us):
                for u in us:
                    hi(l, *mid_unit(u))

            def split_hi(dst, r, width=2 * HALF):
                return sc.copy(dst, pair(r)[:, 0:width].rearrange("p (a n) -> p a n", a=dst.shape[1]))

            def rows_hi(l, use, r, s):
                for i in range(2):
                    wait_done(act, l, r, f"{use}_{s}" + "b" * i)
                    sc.copy(xT_hi[:, 4 * i:4 * i + 4, s * P:(s + 1) * P],
                            bank(r, i).rearrange("p (a n) -> p a n", a=4)).then_inc(xThi_ready, 1)

            def ln_T(l, n, regs):
                for s in range(S):
                    rows_hi(l, f"ln{n}", regs[s], s)

            act.dma_start(lb_in, hgrn_lb.rearrange("l (p n) -> p l n", p=P)).then_inc(lb_landed, 16)
            act.wait_ge(lb_centered, 1)
            sc.activation(lb_in, lb_in, ACT.Exp).then_inc(lb_exp, 1)
            for s in range(S):
                act.wait_ge(memT_done, s + 1)
                split_hi(memT_hi[:, :, s * P:(s + 1) * P], 2 + s).then_inc(memThi_ready, 1)

            def ffn_act(l, f):
                b = F_BASE[f]

                def gate(c):
                    wait_unit_done(act, l, *((1, b[1]) if isinstance(c, int) and c == 0 else (0, c + b[0])))
                    r = 1 if isinstance(c, int) and c == 0 else 0
                    for s in range(S):
                        sc.activation(sg[:, s, :], bank(r, s)[:, 0:CF], ACT.Sigmoid).then_inc(sig_ready, 1)

                def hT(c, dst=hT_hi, last=False):
                    wait_done_step(act, l, f, c)
                    if not last and not (isinstance(c, int) and c == 0):
                        wait_unit_done(act, l, 1, c + b[1])
                    sc.copy(dst[:, 0:2, :], bank(1)[:, :].rearrange("p (a n) -> p a n", a=2)).then_inc(hThi_ready, 1)

                if f == 0:
                    hi(l, 0, b[0])
                    rows_hi(l, "x", 0, 0)
                    hi(l, 1, b[1])
                    rows_hi(l, "x", 0, 1)
                hi(l, 2, b[2])
                gate(0)
                hi(l, 0, b[0] + 1)

                def step(c, last):
                    hi(l, 1, c + b[1])
                    hT(c - 1)
                    hi(l, 2, c + b[2])
                    wait_gu_read(act, l, f, c - 1)
                    gate(c)
                    if not (last and f):
                        hi(l, 0, c + (b[0] + 1))

                step(1, False)
                with act.Fori(2, NC - 1) as c:
                    step(c, False)
                step(NC - 1, True)
                hT(NC - 1, xT_hi, True)

            with act.Fori(0, L) as l:
                ffn_act(l, 0)
                mid_hi(l, 1)
                ln_T(l, 0, (1, 1))
                mid_hi(l, 2, 3)
                wait_chunk(act, l, 0)
                for s in range(S):
                    i = sc.activation(sig_b[:, s, :], bank(0, s), ACT.Sigmoid)
                i.then_inc(psum_read[0], 1)
                mid_hi(l, 4, 5, 6)
                wait_done(act, l, 2, "taps")
                sc.copy(taps[:, :, :], bank(2)[:, 0:HEADS * 32].rearrange("p (h t) -> p h t", h=HEADS))\
                    .then_inc(psum_read[2], 1)
                wait_done(act, l, 2, "conv_h")
                sc.copy(hc[:, :, PAD:], pair(2).rearrange("p (a n) -> p a n", a=HEADS)).then_inc(psum_read[2], 1)
                act.drain()
                wait_event(act, l, "padded")
                for g in range(HEADS):
                    i = sc.activation(acc[:, g, :], hc[:, g, 0:SEQ], ACT.Identity, bias=taps[:, g, CONV_K:CONV_K + 1],
                                      scale=taps[:, g, 0:1])
                i.then_inc(ev["tap0"], 1)
                mid_hi(l, 7)
                wait_chunk(act, l, 2)
                for s in range(S):
                    i = sc.activation(k_seq[:, s, :], bank(0, s), ACT.Sigmoid, scale=-1.0)
                i.then_inc(psum_read[0], 1)
                mid_hi(l, 8, 9)
                wait_chunk(act, l, 3)
                for s in range(S):
                    i = sc.activation(q_seq[:, s, :], bank(1, s), ACT.Sigmoid)
                i.then_inc(ev["sigq"], 1)
                wait_event(act, l, "kscaled")
                sc.activation(logf[:, :, :], logf[:, :, :], ACT.Ln, scale=-1.0, bias=1.0)
                act.drain()
                sc.copy(logf_hi[:, :, :], logf[:, :, :]).then_inc(ev["logf_hi"], 1)
                mid_hi(l, 10)
                wait_done(act, l, 3, "k_T")
                sc.copy(kT[:, :, :], pair(3).rearrange("p (a n) -> p a n", a=HEADS)).then_inc(psum_read[3], 1)
                mid_hi(l, 11)
                wait_chunk(act, l, 4)
                for s in range(S):
                    i = sc.copy(v_seq[:, s, :], bank(0, s))
                i.then_inc(psum_read[0], 1)
                wait_done(act, l, 2, "q_T")
                sc.copy(qT[:, :, :], pair(2).rearrange("p (a n) -> p a n", a=HEADS)).then_inc(psum_read[2], 1)
                wait_done(act, l, 3, "kd")
                sc.activation(kd[:, :, :], pair(3).rearrange("p (a n) -> p a n", a=S), ACT.Exp).then_inc(psum_read[3], 1)
                mid_hi(l, 12, 13)
                wait_done(act, l, 2, "state")
                sc.copy(state[:, 0, :, :], bank(2, 0).rearrange("p (h v) -> p h v", h=HEADS))
                act.drain()
                wait_done(act, l, 3, "state")
                sc.activation(eb[:, :, :], bank(3, 1)[:, 0:HEADS * NCH].rearrange("p (h c) -> p h c", h=HEADS),
                              ACT.Exp).then_inc(ev["eb"], 1)

                def decays(h):
                    if h:
                        wait_done(act, l, 3, f"s{h - 1}")
                    for s in range(S):
                        wait_done(act, l, 2 + s, f"e{h}")
                        sc.activation(E[:, :, s * P:(s + 1) * P],
                                      pair(2 + s)[:, 0:DECAYS * P].rearrange("p (a n) -> p a n", a=DECAYS),
                                      ACT.Exp).then_inc(psum_read[2 + s], 1)

                def gate_chunk(ch, dst):
                    wait_chunk(act, l, ch)
                    for s in range(S):
                        i = sc.activation(dst[:, s, :], bank(ch % 2, s), ACT.Sigmoid)
                    return i

                def copy_chunk(ch, dst):
                    wait_chunk(act, l, ch)
                    for s in range(S):
                        i = sc.copy(dst[:, s, :], bank(ch % 2, s))
                    i.then_inc(psum_read[ch % 2], 1)

                def out_rows(h):
                    for s in range(S):
                        wait_done(act, l, 2 + s, f"o{h}")
                        o = bank(2 + s, 1)[:, 0:P]
                        sc.activation(squares[:, s, :], o, ACT.Square, accum_out=sq[:, s, h:h + 1])
                        sc.copy(o_seq[:, s, h * P:(h + 1) * P], o).then_inc(psum_read[2 + s], 1)
                    return act.drain()

                gate_chunk(5, og).then_inc(ev["sigo"], 1)
                mid_hi(l, 14)
                decays(0)
                mid_hi(l, 15)
                gate_chunk(6, sigA[:, :, 0:HALF]).then_inc(psum_read[0], 1)
                out_rows(0)
                decays(1)
                mid_hi(l, 16)
                gate_chunk(7, sigA[:, :, HALF:D]).then_inc(psum_read[1], 1)
                mid_hi(l, 17)
                out_rows(1)
                decays(2)
                mid_hi(l, 18)
                gate_chunk(8, sigB[:, :, 0:HALF]).then_inc(psum_read[0], 1)
                mid_hi(l, 19)
                out_rows(2)
                decays(3)
                mid_hi(l, 20)
                gate_chunk(9, sigB[:, :, HALF:D]).then_inc(psum_read[1], 1)
                mid_hi(l, 21)
                out_rows(3).then_inc(ev["sq"], 1)
                mid_hi(l, 22)
                copy_chunk(K_, kseq_x[0])
                mid_hi(l, 23, 24)
                wait_done(act, l, 3, "z_T")
                split_hi(xT_hi[:, 4:8, :], 3).then_inc(ev["zThi"], 1)
                mid_hi(l, 25)
                copy_chunk(K_ + 1, kseq_x[1])
                mid_hi(l, 26, 27)
                wait_event(act, l, "c_norm")
                sc.activation(sig_c[:, :, :], c_seq[:, :, :], ACT.Sigmoid).then_inc(ev["sigc"], 1)
                wait_done(act, l, 2, "c_T")
                split_hi(xT_hi[:, 0:4, :], 2).then_inc(ev["cThi"], 1)
                mid_hi(l, 28)
                mid_hi(l, 29, 30)
                wait_chunk(act, l, YC + 1)
                for s in range(S):
                    wait_done(act, l, 2 + s, "mix")
                    split_hi(xT_hi[:, :, s * P:(s + 1) * P], 2 + s).then_inc(ev["mixThi"], 1)
                mid_hi(l, 31)
                copy_chunk(V0, Vx[:, :, 0:HALF])
                mid_hi(l, 32, 33)

                def copy_T(r, use, dst):
                    wait_done(act, l, r, use)
                    sc.copy(dst, pair(r).rearrange("p (a n) -> p a n", a=4)).then_inc(psum_read[r], 1)

                copy_T(2, "K0", KTx[:, 0:4, :])
                copy_T(3, "K1", KTx[:, 4:8, :])
                mid_hi(l, 34, 35)
                ln_T(l, 1, (2, 3))
                mid_hi(l, 36)
                copy_chunk(Q_, qseq_x[0])
                mid_hi(l, 37, 38)
                copy_T(2, "Q0", QTx[:, 0:4, :])
                mid_hi(l, 39)
                copy_chunk(Q_ + 1, qseq_x[1])
                mid_hi(l, 40)
                copy_T(3, "Q1", QTx[:, 4:8, :])

                def softmax(g):
                    wait_event(act, l, "mx", g + 1)
                    for i in range(4):
                        k = sc.activation(Px[:, 4 * g + i, :], pair(2 + g)[:, i * N_MEM:(i + 1) * N_MEM], ACT.Exp,
                                          bias=mx[:, g, i:i + 1], scale=XSCALE, accum_out=den[:, g, i:i + 1])
                    k.then_inc(psum_read[2 + g], 1)

                def copy_P_T(g):
                    wait_done(act, l, 2 + g, "P_T")
                    sc.copy(PTx[:, 2 * g:2 * g + 2, :, :].rearrange("p h m t -> p (h m t)"), pair(2 + g))\
                        .then_inc(psum_read[2 + g], 1)

                softmax(0)
                mid_hi(l, 41)
                copy_P_T(0)
                softmax(1)
                copy_chunk(V1, Vx[:, :, HALF:D])
                copy_P_T(1)
                mid_hi(l, 42)
                for g in range(2):
                    wait_done(act, l, 2 + g, "pv")
                    split_hi(xT_hi[:, 4 * g:4 * g + 4, :], 2 + g).then_inc(ev["oThi"], 1)
                mid_hi(l, 43)
                hi(l, 0, FFN2_BASE[0])
                hi(l, 1, FFN2_BASE[1])
                ln_T(l, 2, (2, 3))
                ffn_act(l, 1)

        @block.vector
        def _(dve):
            v = nc.vector

            def lo(l, slot, use):
                dve.wait_ge(hi_ready[slot], l * USES[slot] + use + 1)
                v.tensor_tensor(w_lo[slot][:, :], raw[slot][:, :], w_hi[slot][:, :], ALU.subtract).then_inc(lo_ready[slot], 1)

            def mid_lo(l, *us):
                for u in us:
                    lo(l, *mid_unit(u))

            def split_lo(dst, hi, r):
                n = dst.shape[1]
                return v.tensor_tensor(dst, pair(r).rearrange("p (a n) -> p a n", a=n), hi, ALU.subtract)

            for s_ in lo_ready + unit_done + psum_read[0:2] + [rows_used]:
                dve.sem_inc(s_, 1)
            dve.wait_ge(lb_landed, 16)
            v.tensor_tensor(lb_sum, lb_in[:, 0, :], lb_in[:, 1, :], ALU.max)
            dve.drain()
            for l in range(L):
                v.tensor_tensor(lb_in[:, l, :], lb_in[:, l, :], lb_sum, ALU.subtract)
            dve.drain()
            v.memset(key[:, 0, :], 1.0).then_inc(lb_centered, 1)
            dve.wait_ge(lb_exp, 1)
            v.tensor_tensor(lb_sum, lb_in[:, 0, :], lb_in[:, 1, :], ALU.add)
            dve.drain()
            v.reciprocal(lb_sum, lb_sum)
            dve.drain()
            v.tensor_tensor(key[:, 1, :], lb_in[:, 1, :], lb_sum, ALU.mult)
            dve.drain()
            v.tensor_scalar(key[:, 1, :], key[:, 1, :], -1.0, 1.0, ALU.mult, ALU.add).then_inc(key_ready, 1)
            dve.wait_ge(x_landed, 16 * S)
            dve.sem_inc(x_ready, S)
            for s in range(S):
                dve.wait_ge(memThi_ready, s + 1)
                c = slice(s * P, (s + 1) * P)
                split_lo(memT_lo[:, :, c], memT_hi[:, :, c], 2 + s).then_inc(psum_read[2 + s], 1)

            def rows_lo(l, n, r, s):
                for i in range(2):
                    dve.wait_ge(xThi_ready, l * 16 + 4 * n + 2 * s + i + 1)
                    t = (slice(None), slice(4 * i, 4 * i + 4), slice(s * P, (s + 1) * P))
                    v.tensor_tensor(xT_lo[t], bank(r, i).rearrange("p (a n) -> p a n", a=4), xT_hi[t], ALU.subtract)\
                        .then_inc(psum_read[r] if i else half_split, 1)

            def ln_sum(l, s, i, src):
                c = slice(i * HALF, (i + 1) * HALF)
                return v.scalar_tensor_tensor(y[:, s, c], x_res[:, s, c], ALPHA, src, ALU.mult, ALU.add)

            def ln_stats(s, i):
                v.bn_stats(stats[:, s, 6 * i:6 * i + 6], y[:, s, i * HALF:(i + 1) * HALF])

            def layer_norm(l, n, half_sum, regs, between, split_after=0):

                def moments(s):
                    for i in range(2):
                        half_sum(s, i)
                        if s == 1 and i == split_after and regs is not None:
                            split(0)
                    dve.drain()
                    v.bn_aggr(mv[:, s, :], stats[:, s, :])
                    dve.drain()
                    v.tensor_scalar(var[:, s:s + 1], mv[:, s, 1:2], LN_EPS, None, ALU.add).then_inc(var_ready, 1)

                def scale(s):
                    if s == 0:
                        dve.wait_ge(rows_landed, l * 16 * 12 + 16 * (2, 8, 10, 12)[n])
                    v.scalar_tensor_tensor(y[:, s, :], y[:, s, :], mv[:, s, 0:1], rows_ln[:, 0, :],
                                           ALU.subtract, ALU.mult)
                    dve.drain()
                    dve.wait_ge(rstd_ready, l * 8 + 2 * n + s + 1)
                    v.scalar_tensor_tensor(x_res[:, s, :], y[:, s, :], rstd[:, s:s + 1], rows_ln[:, 1, :],
                                           ALU.mult, ALU.add).then_inc(x_ready, 1)

                def split(s):
                    rows_lo(l, n + 1, regs[s], s)

                moments(0)
                scale(0)
                moments(1)
                if regs is not None:
                    between()
                scale(1)
                dve.drain().then_inc(rows_used, 1)
                if regs is not None:
                    split(1)

            def ffn_dve(l, f):
                b = F_BASE[f]

                def gate(c):
                    if not (isinstance(c, int) and c == 0):
                        wait_done_step(dve, l, f, c - 1)
                    r = 1 if isinstance(c, int) and c == 0 else 0
                    for s in range(S):
                        dve.wait_ge(sig_ready, (l * 2 + f) * 2 * NC + c * 2 + (s + 1))
                        v.scalar_tensor_tensor(hx[:, s, :], bank(r, s)[:, 0:CF], 0.5, sg[:, s, :], ALU.mult, ALU.mult)
                    dve.drain()
                    for s in range(S):
                        i = v.tensor_tensor(hx[:, s, :], bank(r, s)[:, CF:2 * CF], hx[:, s, :], ALU.mult)
                    i.then_inc(psum_read[r], 1)

                def hT(c, lo_=hT_lo, hi_=hT_hi):
                    dve.wait_ge(hThi_ready, (l * 2 + f) * NC + c + 1)
                    v.tensor_tensor(lo_[:, 0:2, :], bank(1)[:, :].rearrange("p (a n) -> p a n", a=2), hi_[:, 0:2, :],
                                    ALU.subtract).then_inc(psum_read[1], 1)

                if f == 0:
                    lo(l, 0, b[0])
                    rows_lo(l, 0, 0, 0)
                    lo(l, 1, b[1])
                    rows_lo(l, 0, 0, 1)
                lo(l, 2, b[2])
                gate(0)
                lo(l, 0, b[0] + 1)

                def step(c, last):
                    lo(l, 1, c + b[1])
                    hT(c - 1)
                    lo(l, 2, c + b[2])
                    gate(c)
                    if not (last and f):
                        lo(l, 0, c + (b[0] + 1))

                with dve.Fori(1, NC - 1) as c:
                    step(c, False)
                step(NC - 1, True)
                hT(NC - 1, xT_lo, xT_hi)

                def half_sum(s, i):
                    if s == 1 and i == 1:
                        wait_unit_done(dve, l, 2, b[2] + NC - 1)
                    else:
                        dve.wait_ge(acc_done, (l * 2 + f) * 3 + 2 * s + i + 1)
                    k = ln_sum(l, s, i, bank(2 + s, i))
                    if i == 1:
                        k.then_inc(psum_read[2 + s], 1)
                    dve.drain()
                    ln_stats(s, i)

                return half_sum

            with dve.Fori(0, L) as l:
                half_sum = ffn_dve(l, 0)
                layer_norm(l, 0, half_sum, (1, 1), lambda: mid_lo(l, 1))
                mid_lo(l, 2, 3, 4, 5)
                v.memset(hc[:, :, 0:PAD], 0.0).then_inc(ev["padded"], 1)
                def conv(first, last):
                    for j in range(first, last):
                        if j > 1:
                            dve.drain()
                        for g in range(HEADS):
                            i = v.scalar_tensor_tensor(acc[:, g, :], hc[:, g, j:j + SEQ], taps[:, g, j:j + 1],
                                                       acc[:, g, :], ALU.mult, ALU.add)
                    return i

                wait_chunk(dve, l, 1)
                wait_read(dve, l, 0, "chunk0")
                for s in range(S):
                    i = v.tensor_tensor(h_seq[:, s, :], bank(1, s), sig_b[:, s, :], ALU.mult)
                i.then_inc(psum_read[1], 1)
                mid_lo(l, 6)
                wait_event(dve, l, "tap0")
                conv(1, 2)
                mid_lo(l, 7)
                wait_read(dve, l, 0, "chunk2")
                dve.wait_ge(rows_landed, l * 16 * 12 + 16 * 6)
                for s in range(S):
                    v.tensor_tensor(k_seq[:, s, :], k_seq[:, s, :], rows[:, 3, :], ALU.mult)
                dve.drain()
                v.tensor_scalar(logf[:, :, :], k_seq[:, :, :], KEY_MAX, None, ALU.min).then_inc(ev["kscaled"], 1)

                conv(2, 4)
                mid_lo(l, 8)
                conv(4, 6)
                wait_event(dve, l, "sigq")
                for s in range(S):
                    i = v.scalar_tensor_tensor(q_seq[:, s, :], bank(1, s), QSCALE, q_seq[:, s, :], ALU.mult, ALU.mult)
                i.then_inc(psum_read[1], 1)
                mid_lo(l, 9)
                wait_event(dve, l, "logf_hi")
                v.tensor_tensor(logf_lo[:, :, :], logf[:, :, :], logf_hi[:, :, :], ALU.subtract).then_inc(ev["logf_lo"], 1)
                conv(6, 8)
                mid_lo(l, 10)
                conv(8, 10)
                mid_lo(l, 11)
                wait_read(dve, l, 3, "kd")
                v.tensor_tensor(kd[:, :, :], kd[:, :, :], k_seq[:, :, :], ALU.mult).then_inc(ev["kd"], 1)
                conv(10, 13)
                mid_lo(l, 12)
                conv(13, 14)
                wait_event(dve, l, "eb")
                for c in range(1, NCH - 1):
                    u_c = bank(2, 1) if c == 1 else bank(3, 0)
                    for h in range(HEADS):
                        i = v.scalar_tensor_tensor(state[:, c, h, :], state[:, c - 1, h, :], eb[:, h, c:c + 1],
                                                   u_c[:, h * P:(h + 1) * P], ALU.mult, ALU.add)
                        if h == HEADS - 1:
                            i.then_inc(psum_read[2] if c == 1 else psum_read[3], 1)
                    dve.drain()

                mid_lo(l, 13)

                def scale_keys(h):
                    wait_read(dve, l, 2, f"e{h}")
                    wait_read(dve, l, 3, f"e{h}")
                    for i, m in enumerate(LEVELS):
                        half = lambda ap, k: ap.rearrange("p (b k m) -> p b k m", k=2, m=m)[:, :, k, :]
                        for k, src in ((0, kT), (1, qT)):
                            v.tensor_tensor(half(E[:, i, :], k), half(E[:, i, :], k), half(src[:, h, :], k), ALU.mult)
                    v.tensor_tensor(E[:, NL, :], E[:, NL, :], qT[:, h, :], ALU.mult).then_inc(ev["X"], 1)

                def scores(h):
                    for s in range(S):
                        wait_done(dve, l, 2 + s, f"s{h}")
                        v.tensor_tensor(prod, bank(2 + s)[:, 0:MASKS * CHUNK], masks[:, :], ALU.mult)
                        dve.drain()
                        v.tensor_reduce(ST[:, s, :], prod.rearrange("p (i t) -> p t i", i=MASKS), AX_X, ALU.add)\
                            .then_inc(ev["ST"], 1)
                        dve.drain()

                wait_event(dve, l, "sigo")
                for s in range(S):
                    i = v.tensor_tensor(og[:, s, :], bank(1, s), og[:, s, :], ALU.mult)
                i.then_inc(psum_read[1], 1)
                conv(14, 16)
                scale_keys(0)
                mid_lo(l, 14)
                dve.wait_ge(masks_ready, 1)
                scores(0)
                for s in range(S):
                    v.tensor_tensor(og[:, s, :], og[:, s, :], rows[:, 2, :], ALU.mult)
                mid_lo(l, 15)
                conv(16, 19)
                scale_keys(1)
                mid_lo(l, 16)
                conv(19, 20)
                scores(1)
                mid_lo(l, 17)
                conv(20, 22)
                scale_keys(2)
                mid_lo(l, 18)
                conv(22, 23)
                scores(2)
                mid_lo(l, 19)
                conv(23, 25)
                scale_keys(3)
                mid_lo(l, 20)
                conv(25, 26)
                scores(3)
                mid_lo(l, 21)
                conv(26, 27)
                wait_event(dve, l, "sq")
                v.tensor_scalar(sq[:, :, :], sq[:, :, :], 1.0 / P, RMS_EPS, ALU.mult, ALU.add).then_inc(ev["ms"], 1)
                mid_lo(l, 22)
                conv(27, 28)
                wait_event(dve, l, "rrms")
                for h in range(HEADS):
                    for s in range(S):
                        c = slice(h * P, (h + 1) * P)
                        i = v.scalar_tensor_tensor(o_seq[:, s, c], o_seq[:, s, c], rrms[:, s, h:h + 1], og[:, s, c],
                                                   ALU.mult, ALU.mult)
                i.then_inc(ev["z"], 1)
                mid_lo(l, 23)
                conv(28, 29)
                wait_event(dve, l, "zThi")
                split_lo(xT_lo[:, 4:8, :], xT_hi[:, 4:8, :], 3).then_inc(psum_read[3], 1)
                mid_lo(l, 24)
                conv(29, CONV_K).then_inc(ev["conv"], 1)
                mid_lo(l, 25)
                def gated(ch, dst):
                    wait_chunk(dve, l, ch)
                    c = slice((ch % 2) * HALF, (ch % 2 + 1) * HALF)
                    for s in range(S):
                        i = v.tensor_tensor(dst[:, s, c], bank(ch % 2, s), dst[:, s, c], ALU.mult)
                    i.then_inc(psum_read[ch % 2], 1)

                wait_done(dve, l, 2, "c_seq")
                for s in range(S):
                    v.bn_stats(stats[:, s, 0:6], bank(2, s))
                dve.drain()
                for s in range(S):
                    v.bn_aggr(mv[:, s, :], stats[:, s, 0:6])
                dve.drain()
                v.tensor_scalar(var[:, :], mv[:, :, 1], LN_EPS, None, ALU.add).then_inc(ev["cvar"], 1)
                for s in range(S):
                    i = v.scalar_tensor_tensor(c_seq[:, s, :], bank(2, s), mv[:, s, 0:1], rows[:, 0, :],
                                               ALU.subtract, ALU.mult)
                i.then_inc(psum_read[2], 1)
                dve.drain()
                wait_event(dve, l, "crstd")
                for s in range(S):
                    i = v.scalar_tensor_tensor(c_seq[:, s, :], c_seq[:, s, :], rstd[:, s:s + 1], rows[:, 1, :],
                                               ALU.mult, ALU.add)
                i.then_inc(ev["c_norm"], 1)
                gated(YH, sigB)
                wait_event(dve, l, "sigc")
                v.tensor_tensor(c_seq[:, :, :], c_seq[:, :, :], sig_c[:, :, :], ALU.mult).then_inc(ev["c_out"], 1)
                dve.drain().then_inc(rows_used, 1)

                def ln_first(ch):
                    wait_chunk(dve, l, ch)
                    for s in range(S):
                        k = ln_sum(l, s, 0, bank(ch % 2, s))
                    k.then_inc(psum_read[ch % 2], 1)
                    dve.drain()
                    for s in range(S):
                        ln_stats(s, 0)

                def ln_second(ch):
                    def half_sum(s, i):
                        if i == 1:
                            wait_rows(dve, l, ch + 1, s)
                            k = ln_sum(l, s, 1, bank((ch + 1) % 2, s))
                            if s == 1:
                                k.then_inc(psum_read[(ch + 1) % 2], 1)
                            dve.drain()
                            ln_stats(s, 1)
                    return half_sum

                mid_lo(l, 26)
                wait_event(dve, l, "cThi")
                split_lo(xT_lo[:, 0:4, :], xT_hi[:, 0:4, :], 2).then_inc(psum_read[2], 1)
                gated(YH + 1, sigB)
                mid_lo(l, 27)
                mid_lo(l, 28)
                gated(YC, sigA)
                mid_lo(l, 29)
                gated(YC + 1, sigA)
                dve.drain()
                for s in range(S):
                    v.tensor_tensor(sigA[:, s, :], sigA[:, s, :], sigB[:, s, :], ALU.add).then_inc(ev["mix"], 1)
                mid_lo(l, 30)
                for s in range(S):
                    wait_event(dve, l, "mixThi", s + 1)
                    c = slice(s * P, (s + 1) * P)
                    split_lo(xT_lo[:, :, c], xT_hi[:, :, c], 2 + s).then_inc(psum_read[2 + s], 1)
                mid_lo(l, 31, 32, 33)
                ln_first(MO)
                mid_lo(l, 34)

                layer_norm(l, 1, ln_second(MO), (2, 3), lambda: mid_lo(l, 35), 1)
                mid_lo(l, 36, 37, 38)

                def row_max(g):
                    wait_done(dve, l, 2 + g, "score")
                    v.tensor_reduce(mx[:, g, :], pair(2 + g).rearrange("p (i m) -> p i m", i=4), AX_X, ALU.max)
                    dve.drain()
                    v.tensor_scalar(mx[:, g, :], mx[:, g, :], -XSCALE, None, ALU.mult).then_inc(ev["mx"], 1)

                def normalise(g):
                    wait_read(dve, l, 2 + g, "score")
                    v.reciprocal(rden[:, g, :], den[:, g, :])
                    dve.drain()
                    for i in range(4):
                        k = v.tensor_scalar(Px[:, 4 * g + i, :], Px[:, 4 * g + i, :], rden[:, g, i:i + 1], None, ALU.mult)
                    k.then_inc(ev["Pn"], 1)

                row_max(0)
                mid_lo(l, 39)
                normalise(0)
                row_max(1)
                mid_lo(l, 40)
                normalise(1)
                mid_lo(l, 41)
                for g in range(2):
                    wait_event(dve, l, "oThi", g + 1)
                    split_lo(xT_lo[:, 4 * g:4 * g + 4, :], xT_hi[:, 4 * g:4 * g + 4, :], 2 + g).then_inc(psum_read[2 + g], 1)
                mid_lo(l, 42, 43)
                ln_first(WO)
                lo(l, 0, FFN2_BASE[0])
                layer_norm(l, 2, ln_second(WO), (2, 3),
                           lambda: lo(l, 1, FFN2_BASE[1]), 1)
                half_sum = ffn_dve(l, 1)
                layer_norm(l, 3, half_sum, None, None)

        @block.tensor
        def _(pe):
            t_ = nc.tensor

            def turn(dst, src):
                return t_.transpose(dst, src, ident[0:src.shape[0], 0:src.shape[0]])

            def three(dst, hi_, lo_, w, slot, start, stop):
                t_.matmul(dst, hi_, w_hi[slot][:, w], start=start, stop=False)
                t_.matmul(dst, hi_, w_lo[slot][:, w], start=False, stop=False)
                return t_.matmul(dst, lo_, w_hi[slot][:, w], start=False, stop=stop)

            def wait_weights(l, slot, use):
                pe.wait_ge(lo_ready[slot], l * USES[slot] + use + 2)

            def unit(l, slot, use, hi_, lo_, t0, r, first, last):
                wait_weights(l, slot, use)
                for i in range(4):
                    for s in range(S):
                        c = slice(s * P, (s + 1) * P)
                        k = three(bank(r, s), hi_[:, t0 + i, c], lo_[:, t0 + i, c], slice(i * HALF, (i + 1) * HALF),
                                  slot, first and i == 0, last and i == 3)
                k.then_inc(unit_done[slot], 1)

            def units_by_rows(l, units, hi_, lo_, r, ready, between, finished=None):
                for s in range(S):
                    c = slice(s * P, (s + 1) * P)
                    for part, (slot, use) in enumerate(units):
                        ready(s, part)
                        if s == 0:
                            wait_weights(l, slot, use)
                        for i in range(4):
                            k = three(bank(r, s), hi_[:, 4 * part + i, c], lo_[:, 4 * part + i, c],
                                      slice(i * HALF, (i + 1) * HALF), slot, part + i == 0, part + i == 4)
                        if s == 1:
                            k.then_inc(unit_done[slot], 1)
                        elif part == 1:
                            if finished is not None:
                                k.then_inc(finished, 1)
                            between()

            def tiles_T(dst, src, n):
                for s in range(S):
                    for i in range(n):
                        k = turn(dst[:, i * SEQ + s * P:i * SEQ + (s + 1) * P], src(s, i))
                return k

            def rows_T(l, use, ready, r, s):
                wait_room(pe, l, r, f"{use}_{s}")
                pe.wait_ge(x_ready, ready + s)
                for i in range(KT):
                    k = turn(pair(r)[:, i * P:(i + 1) * P], x_res[:, s, i * P:(i + 1) * P])
                    if i % 4 == 3:
                        k.then_inc(done[r], 1)

            def ln_T(l, n, r, s):
                rows_T(l, f"ln{n}", l * 8 + X0 + 2 * n + 1, r, s)

            def x_T(l, s):
                rows_T(l, "x", l * 8 + 1, 0, s)

            def wait_split(l, n, use, r, s, part):
                if part == 0:
                    pe.wait_ge(half_split, l * 8 + 2 * n + s + 1)
                else:
                    wait_read(pe, l, r, f"{use}_{s}")

            pe.wait_ge(const_landed, 16)
            pe.wait_ge(mem_landed, 16)
            for s in range(S):
                for j in range(KT):
                    k = turn(pair(2 + s)[:, j * P:(j + 1) * P], y[:, s, j * P:(j + 1) * P])
                k.then_inc(memT_done, 1)

            def ffn_pe(l, f):
                b = F_BASE[f]

                def gate_up(c, part, slot, use):
                    if part == 0:
                        if isinstance(c, int) and c == 1:
                            wait_room(pe, l, 0, f"gu{f}_1")
                        else:
                            wait_gu_read(pe, l, f, c - 1)
                    unit(l, slot, use, xT_hi, xT_lo, 4 * part, 0, part == 0, part == 1)

                def h_T(c):
                    wait_gu_read(pe, l, f, c)
                    if not (isinstance(c, int) and c == 0):
                        wait_hT_read(pe, l, f, c - 1)
                    tiles_T(bank(1), lambda s, i: hx[:, s, i * P:(i + 1) * P], 2).then_inc(done[1], 1)

                def down_part(s, i, half, slot, hi_, lo_, first, last):
                    t = slice(s * P, (s + 1) * P)
                    w = slice(i * D + half * HALF, i * D + (half + 1) * HALF)
                    return three(bank(2 + s, half), hi_[:, i, t], lo_[:, i, t], w, slot, first and i == 0,
                                 last and i == 1)

                def down_rows(s, slot, hi_, lo_, first):
                    for i in range(2):
                        for half in range(2):
                            k = down_part(s, i, half, slot, hi_, lo_, first, False)
                    return k

                def down_last(s, slot):
                    for half in range(2):
                        for i in range(2):
                            k = down_part(s, i, half, slot, xT_hi, xT_lo, False, True)
                        if s == 0 or half == 0:
                            k.then_inc(acc_done, 1)
                    return k

                def down(c, slot, use, first):
                    wait_weights(l, slot, use)
                    wait_hT_read(pe, l, f, c)
                    for s in range(S):
                        k = down_rows(s, slot, hT_hi, hT_lo, first)
                    k.then_inc(unit_done[slot], 1)

                def ready(s, part):
                    if s + part == 0:
                        wait_room(pe, l, 1, f"gu{f}_0")
                    if f:
                        wait_split(l, 3, "ln2", 2 + s, s, part)
                    else:
                        wait_split(l, 0, "x", 0, s, part)

                if f == 0:
                    x_T(l, 0)
                units_by_rows(l, [(0, b[0]), (1, b[1])], xT_hi, xT_lo, 1, ready,
                              (lambda: ln_T(l, 2, 3, 1)) if f else (lambda: x_T(l, 1)))

                def step(c, first):
                    gate_up(c, 0, 2, c + (b[2] - 1))
                    h_T(c - 1)
                    gate_up(c, 1, 0, c + b[0])
                    if first:
                        wait_room(pe, l, 2, f"acc{f}")
                        wait_room(pe, l, 3, f"acc{f}")
                    if not (isinstance(c, int) and c == NC - 1):
                        down(c - 1, 1, c + b[1], first)

                step(1, True)
                with pe.Fori(2, NC - 1) as c:
                    step(c, False)
                step(NC - 1, False)
                wait_weights(l, 1, b[1] + NC - 1)
                wait_hT_read(pe, l, f, NC - 2)
                down_rows(0, 1, hT_hi, hT_lo, False)
                h_T(NC - 1)
                down_rows(1, 1, hT_hi, hT_lo, False).then_inc(unit_done[1], 1)
                wait_weights(l, 2, b[2] + NC - 1)
                wait_hT_read(pe, l, f, NC - 1)
                down_last(0, 2)
                down_last(1, 2).then_inc(unit_done[2], 1)

            with pe.Fori(0, L) as l:
                ffn_pe(l, 0)
                ln_T(l, 0, 1, 0)

                def chunk_part(ch, part, hi_=xT_hi, lo_=xT_lo):
                    if part == 0:
                        wait_room(pe, l, ch % 2, f"chunk{ch}")
                    unit(l, *mid_unit(chunk_units(ch)[part]), hi_, lo_, 4 * part, ch % 2, part == 0, part == 1)

                def chunk(ch, hi_=xT_hi, lo_=xT_lo):
                    chunk_part(ch, 0, hi_, lo_)
                    chunk_part(ch, 1, hi_, lo_)

                def small_T(r, name, src, n=4):
                    wait_room(pe, l, r, name)
                    tiles_T(pair(r), src, n).then_inc(done[r], 1)

                def chunk_by_rows(ch, ready, between, finished=None):
                    units_by_rows(l, [mid_unit(u) for u in chunk_units(ch)], xT_hi, xT_lo, ch % 2, ready, between,
                                  finished)

                def chunk0_ready(s, part):
                    if s + part == 0:
                        wait_room(pe, l, 0, "chunk0")
                    wait_split(l, 1, "ln0", 1, s, part)

                chunk_by_rows(0, chunk0_ready, lambda: ln_T(l, 0, 1, 1))
                wait_room(pe, l, 2, "taps")
                pe.wait_ge(conv_landed, l * 32 + 32)
                chunk_part(1, 0)
                for g in range(HEADS):
                    k = turn(bank(2)[:, g * 32:(g + 1) * 32], conv_rows[0:32, g * P:(g + 1) * P])
                k.then_inc(done[2], 1)
                chunk_part(1, 1)
                chunk_part(2, 0)
                wait_read(pe, l, 1, "chunk1")
                small_T(2, "conv_h", lambda s, g: h_seq[:, s, g * P:(g + 1) * P])
                chunk_part(2, 1)
                chunk_part(3, 0)
                wait_event(pe, l, "kscaled")
                small_T(3, "k_T", lambda s, g: k_seq[:, s, g * P:(g + 1) * P])
                chunk_part(3, 1)
                chunk_part(4, 0)
                wait_read(pe, l, 1, "chunk3")
                small_T(2, "q_T", lambda s, g: q_seq[:, s, g * P:(g + 1) * P])
                chunk_part(4, 1)
                wait_room(pe, l, 3, "kd")
                wait_event(pe, l, "logf_lo")
                pe.wait_ge(sums_ready, 1)
                for s in range(S):
                    tail = sums[:, DECAYS * P:(DECAYS + 1) * P]
                    t_.matmul(bank(3, s), tail, logf_hi[:, s, :], start=True, stop=False)
                    k = t_.matmul(bank(3, s), tail, logf_lo[:, s, :], start=False, stop=True)
                k.then_inc(done[3], 1)
                chunk(5)
                for r in (2, 3):
                    wait_room(pe, l, r, "state")
                wait_event(pe, l, "kd")
                wait_read(pe, l, 0, "chunk4")
                for c in range(NCH - 1):
                    rows_c = slice(c % 2 * CHUNK, (c % 2 + 1) * CHUNK)
                    for h in range(HEADS):
                        cols = slice(h * P, (h + 1) * P)
                        k = t_.matmul(bank(2 + c // 2, c % 2)[:, cols], kd[rows_c, c // 2, cols],
                                      v_seq[rows_c, c // 2, cols], start=True, stop=True)
                    if c == 1:
                        k.then_inc(done[2], 1)
                for h in range(HEADS):
                    for s in range(S):
                        for f_ in (logf_hi, logf_lo):
                            k = t_.matmul(bank(3, 1)[:, h * NCH + 2 * s:h * NCH + 2 * s + 2],
                                          f_[:, s, h * P:(h + 1) * P], sums[:, (DECAYS + 1) * P:],
                                          start=f_ is logf_hi, stop=f_ is logf_lo)
                k.then_inc(done[3], 1)
                chunk_part(6, 0)

                def decays(h):
                    for s in range(S):
                        wait_room(pe, l, 2 + s, f"e{h}")
                        for part in (logf_hi, logf_lo):
                            f_, first = part[:, s, h * P:(h + 1) * P], part is logf_hi
                            t_.matmul(bank(2 + s, 0), f_, sums[:, 0:HALF], start=first, stop=not first)
                            k = t_.matmul(bank(2 + s, 1)[:, 0:DECAYS * P - HALF], f_, sums[:, HALF:DECAYS * P],
                                          start=first, stop=not first)
                        k.then_inc(done[2 + s], 1)

                def scores(h):
                    wait_event(pe, l, "X", h + 1)
                    for s in range(S):
                        wait_room(pe, l, 2 + s, f"s{h}")
                        pe.sem_inc(pe_steps, 1)
                        for c in (2 * s, 2 * s + 1):
                            at = slice(c % 2 * CHUNK, (c % 2 + 1) * CHUNK)
                            t = slice(c * CHUNK, (c + 1) * CHUNK)
                            for i in range(MASKS):
                                k_, q_ = (E[:, i, t], E[:, i, t]) if i < NL else (kT[:, h, t], qT[:, h, t])
                                k = t_.matmul(bank(2 + s)[at, i * CHUNK:(i + 1) * CHUNK], k_, q_, start=True, stop=True)
                        k.then_inc(done[2 + s], 1)

                def outputs(h):
                    cols = slice(h * P, (h + 1) * P)
                    for s in range(S):
                        wait_event(pe, l, "ST", 2 * h + s + 1)
                        if h == 0 and s == 0:
                            wait_read(pe, l, 3, "state")
                        pe.sem_inc(pe_steps, 1)
                        o = bank(2 + s, 1)[:, 0:P]
                        for c in (2 * s, 2 * s + 1):
                            at = slice(c % 2 * CHUNK, (c % 2 + 1) * CHUNK)
                            k = t_.matmul(o[at, :], ST[at, s, :], v_seq[at, s, cols], start=True, stop=c == 0)
                            if c:
                                k = t_.matmul(o[at, :], E[:, NL, c * CHUNK:(c + 1) * CHUNK], state[:, c - 1, h, :],
                                              start=False, stop=True)
                        k.then_inc(done[2 + s], 1)

                decays(0)
                chunk_part(6, 1)
                scores(0)
                chunk_part(7, 0)
                outputs(0)
                decays(1)
                chunk_part(7, 1)
                scores(1)
                chunk_part(8, 0)
                outputs(1)
                decays(2)
                chunk_part(8, 1)
                scores(2)
                chunk_part(9, 0)
                outputs(2)
                decays(3)
                chunk_part(9, 1)
                scores(3)
                chunk_part(K_, 0, memT_hi, memT_lo)
                outputs(3)
                chunk_part(K_, 1, memT_hi, memT_lo)
                chunk_part(K_ + 1, 0, memT_hi, memT_lo)
                wait_event(pe, l, "z")
                small_T(3, "z_T", lambda s, g: o_seq[:, s, g * P:(g + 1) * P])
                chunk_part(K_ + 1, 1, memT_hi, memT_lo)
                def branch(ch, t0):
                    wait_room(pe, l, ch % 2, f"chunk{ch}")
                    unit(l, *mid_unit(chunk_units(ch)[0]), xT_hi, xT_lo, t0, ch % 2, True, True)

                wait_read(pe, l, 3, "z_T")
                branch(YH, 4)
                wait_event(pe, l, "conv")
                wait_room(pe, l, 2, "c_seq")
                for s in range(S):
                    for g in range(HEADS):
                        k = turn(bank(2, s)[:, g * P:(g + 1) * P], acc[:, g, s * P:(s + 1) * P])
                k.then_inc(done[2], 1)
                branch(YH + 1, 4)
                wait_event(pe, l, "c_out")
                small_T(2, "c_T", lambda s, g: c_seq[:, s, g * P:(g + 1) * P])
                wait_read(pe, l, 2, "c_T")
                branch(YC, 0)
                branch(YC + 1, 0)
                chunk_part(V0, 0, memT_hi, memT_lo)
                for s in range(S):
                    wait_event(pe, l, "mix", s + 1)
                    wait_room(pe, l, 2 + s, "mix")
                    for i in range(KT):
                        k = turn(pair(2 + s)[:, i * P:(i + 1) * P], sigA[:, s, i * P:(i + 1) * P])
                    k.then_inc(done[2 + s], 1)
                chunk_part(V0, 1, memT_hi, memT_lo)
                wait_read(pe, l, 2, "mix")
                wait_read(pe, l, 3, "mix")
                chunk(MO)
                wait_read(pe, l, 0, f"chunk{K_}")
                small_T(2, "K0", lambda s, g: kseq_x[0][:, s, g * P:(g + 1) * P])
                wait_read(pe, l, 1, f"chunk{K_ + 1}")
                small_T(3, "K1", lambda s, g: kseq_x[1][:, s, g * P:(g + 1) * P])

                def room(ch):
                    return lambda s, part: wait_room(pe, l, ch % 2, f"chunk{ch}") if s + part == 0 else None

                chunk_by_rows(MO + 1, room(MO + 1), lambda: None, rows0_done)
                ln_T(l, 1, 2, 0)

                def q_ready(s, part):
                    room(Q_)(s, part)
                    wait_split(l, 2, "ln1", 2 + s, s, part)

                chunk_by_rows(Q_, q_ready, lambda: ln_T(l, 1, 3, 1))
                chunk_part(Q_ + 1, 0)
                wait_read(pe, l, Q_ % 2, f"chunk{Q_}")
                small_T(2, "Q0", lambda s, g: qseq_x[0][:, s, g * P:(g + 1) * P])
                chunk_part(Q_ + 1, 1)
                def score(g):
                    wait_room(pe, l, 2 + g, "score")
                    for h in (2 * g, 2 * g + 1):
                        for s in range(S):
                            o = bank(2 + g, h % 2)[:, s * N_MEM:(s + 1) * N_MEM]
                            for d in range(2):
                                k = t_.matmul(o, QTx[:, 2 * h + d, s * P:(s + 1) * P], KTx[:, 2 * h + d, :],
                                              start=d == 0, stop=d == 1)
                    k.then_inc(done[2 + g], 1)

                score(0)
                wait_read(pe, l, (Q_ + 1) % 2, f"chunk{Q_ + 1}")
                small_T(3, "Q1", lambda s, g: qseq_x[1][:, s, g * P:(g + 1) * P])
                chunk_part(V1, 0, memT_hi, memT_lo)
                score(1)

                def P_T(g):
                    wait_room(pe, l, 2 + g, "P_T")
                    wait_event(pe, l, "Pn", g + 1)
                    for h in (2 * g, 2 * g + 1):
                        k = tiles_T(bank(2 + g, h % 2), lambda s, m: Px[:, 2 * h + s, m * P:(m + 1) * P], 2)
                    k.then_inc(done[2 + g], 1)

                P_T(0)
                chunk_part(V1, 1, memT_hi, memT_lo)
                P_T(1)
                for g in range(2):
                    wait_room(pe, l, 2 + g, "pv")
                    if g:
                        wait_read(pe, l, V1 % 2, f"chunk{V1}")
                    for h in (2 * g, 2 * g + 1):
                        for d in range(2):
                            for m in range(2):
                                k = t_.matmul(bank(2 + g, h % 2)[:, d * SEQ:(d + 1) * SEQ],
                                              Vx[:, m, h * XD + d * P:h * XD + (d + 1) * P], PTx[:, h, m, :],
                                              start=m == 0, stop=m == 1)
                    k.then_inc(done[2 + g], 1)
                for g in range(2):
                    wait_read(pe, l, 2 + g, "pv")
                    chunk_part(WO, g)
                chunk_by_rows(WO + 1, room(WO + 1), lambda: None, rows0_done)
                ln_T(l, 2, 2, 0)
                ffn_pe(l, 1)


INPUTS = ("x mem ln_g ln_b ffn1_w_gu ffn1_w_down w_in conv_w conv_b conv_ln_g conv_ln_b w_conv_proj hgrn_lb "
          "hgrn_norm_g w_hgrn_proj w_mix_out xa_wq xa_wkv xa_wo ffn2_w_gu ffn2_w_down").split()


def kernel(**inputs):
    import concourse.bacc as bacc
    from concourse.bass_utils import run_bass_kernel_spmd

    nc = bacc.Bacc("TRN2", target_bir_lowering=False, num_devices=1)
    arrays, args = {}, []
    for name in INPUTS + ["consts"]:
        a = np.ascontiguousarray(layout_constants() if name == "consts" else inputs[name])
        arrays["in_" + name] = a
        args.append(nc.dram_tensor("in_" + name, a.shape, mybir.dt.from_np(a.dtype), kind="ExternalInput").ap())
    shape = tuple(inputs["x"].shape)
    out = nc.dram_tensor("out_0", shape, F32, kind="ExternalOutput").ap()
    build(nc, *args, out)
    r = run_bass_kernel_spmd(nc, [arrays], core_ids=[0])
    return r.results[0]["out_0"]
```
